# Optimizing a Trainium2 kernel written in Bass

```python
import math
import jax, jax.numpy as jnp
from jax import lax
import numpy as np

D_MODEL = 1024
BATCH = 1
SEQ = 256
DEPTH = 1

A_HEADS = 4
A_DK = 128
A_DV = 128
A_W = A_HEADS * A_DK
A_CONV = 4
A_CHUNK = 64
B_CH = 512
B_KERNEL = 31
C_QHEADS = 8
C_KVHEADS = 2
C_HD = 64
C_QW = C_QHEADS * C_HD
C_KW = C_KVHEADS * C_HD
C_WINDOW = 128
REL_BUCKETS = 32
REL_MAX_DIST = 128
N_BRANCH = 3
N_EXPERTS = 32
TOP_K = 4
D_EXPERT = 1024
SWIGLU_LIMIT = 7.0
SWIGLU_ALPHA = 1.702
LN_EPS = 1e-5
RMS_EPS = 1e-6
DEEPNORM_ALPHA = (2 * DEPTH) ** 0.25
DEEPNORM_BETA = (8 * DEPTH) ** -0.25
IN_SPLITS = (A_W, A_W, A_W, A_W, A_HEADS, A_HEADS, 2 * B_CH, C_QW, C_KW, C_KW, N_BRANCH * D_MODEL)
N_IN = sum(IN_SPLITS)

kernel_name = "hybrid_deltanet_conformer_swa_moe"

F32 = jnp.float32

def layer_norm(x, g, b):
    xf = x.astype(F32)
    mu = jnp.mean(xf, -1, keepdims=True)
    var = jnp.mean(jnp.square(xf - mu), -1, keepdims=True)
    y = (xf - mu) * lax.rsqrt(var + LN_EPS)
    return (y * g.astype(F32) + b.astype(F32)).astype(x.dtype)

def rms_norm(x):
    xf = x.astype(F32)
    return xf * lax.rsqrt(jnp.mean(xf * xf, -1, keepdims=True) + RMS_EPS)

def l2norm(x):
    xf = x.astype(F32)
    return xf * lax.rsqrt(jnp.sum(xf * xf, -1, keepdims=True) + RMS_EPS)

def causal_depthwise_conv(x, w):
    width, ch = w.shape
    return lax.conv_general_dilated(
        x, w[:, None, :].astype(x.dtype), window_strides=(1,), padding=[(width - 1, 0)],
        dimension_numbers=("NWC", "WIO", "NWC"), feature_group_count=ch)

def gated_delta_rule(q, k, v, g, beta):
    b, s, h, dk = q.shape
    dv = v.shape[-1]
    c = A_CHUNK
    n = s // c

    def chunks(t):
        t = t.astype(F32).reshape((b, n, c, h) + t.shape[3:])
        return jnp.moveaxis(t, 3, 1)

    q = chunks(q) * (dk ** -0.5)
    k, v, beta, g = chunks(k), chunks(v), chunks(beta), chunks(g)
    gcum = jnp.cumsum(g, axis=-1)
    diff = gcum[..., :, None] - gcum[..., None, :]
    incl = jnp.tril(jnp.ones((c, c), bool))
    strict = jnp.tril(jnp.ones((c, c), bool), -1)
    decay = jnp.where(incl, jnp.exp(jnp.minimum(diff, 0.0)), 0.0)
    kk = jnp.einsum("bhncd,bhnjd->bhncj", k * beta[..., None], k)
    a_mat = jnp.eye(c, dtype=F32) + jnp.where(strict, kk * decay, 0.0)
    rhs = jnp.concatenate([v * beta[..., None], k * (beta * jnp.exp(gcum))[..., None]], -1)
    sol = lax.linalg.triangular_solve(a_mat, rhs, left_side=True, lower=True, unit_diagonal=True)
    u, w = sol[..., :dv], sol[..., dv:]
    qk = jnp.einsum("bhncd,bhnjd->bhncj", q, k) * decay
    q_dec = q * jnp.exp(gcum)[..., None]
    k_dec = k * jnp.exp(gcum[..., -1:] - gcum)[..., None]
    g_last = jnp.exp(gcum[..., -1])

    def step(state, inp):
        u_i, w_i, qk_i, qd_i, kd_i, gl_i = inp
        v_new = u_i - jnp.einsum("bhcd,bhde->bhce", w_i, state)
        o = jnp.einsum("bhcd,bhde->bhce", qd_i, state) + jnp.einsum("bhcj,bhje->bhce", qk_i, v_new)
        state = state * gl_i[..., None, None] + jnp.einsum("bhcd,bhce->bhde", kd_i, v_new)
        return state, o

    xs = tuple(jnp.moveaxis(t, 2, 0) for t in (u, w, qk, q_dec, k_dec, g_last))
    _, o = lax.scan(step, jnp.zeros((b, h, dk, dv), F32), xs)
    o = jnp.moveaxis(jnp.moveaxis(o, 0, 2), 1, 3)
    return o.reshape(b, s, h, dv)

def rel_bucket(dist):
    exact = REL_BUCKETS // 2
    large = exact + (jnp.log(jnp.maximum(dist, 1).astype(F32) / exact)
                     / math.log(REL_MAX_DIST / exact) * (REL_BUCKETS - exact)).astype(jnp.int32)
    large = jnp.minimum(large, REL_BUCKETS - 1)
    return jnp.where(dist < exact, dist, large)

def sliding_window_attention(q, k, v, sinks, rel_bias):
    b, s, hq, hd = q.shape
    hkv = k.shape[2]
    grp = hq // hkv
    w = C_WINDOW
    nb = s // w
    qb = q.astype(F32).reshape(b, nb, w, hkv, grp, hd)

    def windows(t):
        tb = t.astype(F32).reshape(b, nb, w, hkv, hd)
        prev = jnp.pad(tb, ((0, 0), (1, 0), (0, 0), (0, 0), (0, 0)))[:, :-1]
        return jnp.concatenate([prev, tb], axis=2)

    kw, vw = windows(k), windows(v)
    scores = jnp.einsum("bnqhgd,bnkhd->bhgnqk", qb, kw) * (hd ** -0.5)
    qi = jnp.arange(w)[:, None]
    kj = jnp.arange(2 * w)[None, :]
    dist = qi + w - kj
    band = (dist >= 0) & (dist < w)
    bias = rel_bias.astype(F32)[rel_bucket(jnp.maximum(dist, 0))]
    bias = jnp.transpose(bias, (2, 0, 1)).reshape(hkv, grp, 1, w, 2 * w)
    key_pos = jnp.arange(nb)[:, None] * w + kj - w
    mask = band[None] & (key_pos >= 0)[:, None, :]
    scores = jnp.where(mask, scores + bias, -jnp.inf)
    sink = jnp.broadcast_to(sinks.astype(F32).reshape(hkv, grp, 1, 1, 1), scores.shape[:-1] + (1,))
    probs = jax.nn.softmax(jnp.concatenate([scores, sink], -1), axis=-1)[..., :-1]
    out = jnp.einsum("bhgnqk,bnkhd->bnqhgd", probs, vw)
    return out.reshape(b, s, hq * hd)

def hybrid_mixer(x, rel_bias, w_in, a_conv_w, a_log, a_dt_bias, a_norm_g, w_a_out,
                 b_dw_w, b_dw_b, b_ln_g, b_ln_b, w_b_out, c_sinks, w_c_out, w_out):
    b, s, d = x.shape
    proj = x @ w_in
    split_points = np.cumsum(IN_SPLITS)[:-1].tolist()
    aq, ak, av, az, ab, aa, b_glu, cq, ck, cv, gate_logits = jnp.split(proj, split_points, axis=-1)

    qkv = jax.nn.silu(causal_depthwise_conv(jnp.concatenate([aq, ak, av], -1), a_conv_w))
    aq, ak, av = jnp.split(qkv, 3, axis=-1)
    heads = lambda t: t.reshape(b, s, A_HEADS, -1)
    beta = jax.nn.sigmoid(ab.astype(F32))
    g = -jnp.exp(a_log.astype(F32)) * jax.nn.softplus(aa.astype(F32) + a_dt_bias.astype(F32))
    o_a = gated_delta_rule(l2norm(heads(aq)), l2norm(heads(ak)), heads(av), g, beta)
    o_a = rms_norm(o_a) * a_norm_g.astype(F32) * jax.nn.silu(heads(az).astype(F32))
    y_a = o_a.reshape(b, s, A_W).astype(x.dtype) @ w_a_out

    glu_val, glu_gate = jnp.split(b_glu, 2, axis=-1)
    hb = glu_val * jax.nn.sigmoid(glu_gate)
    hb = causal_depthwise_conv(hb, b_dw_w) + b_dw_b
    hb = jax.nn.silu(layer_norm(hb, b_ln_g, b_ln_b))
    y_b = hb @ w_b_out

    o_c = sliding_window_attention(cq.reshape(b, s, C_QHEADS, C_HD), ck.reshape(b, s, C_KVHEADS, C_HD),
                                   cv.reshape(b, s, C_KVHEADS, C_HD), c_sinks, rel_bias)
    y_c = o_c.astype(x.dtype) @ w_c_out

    gates = jax.nn.sigmoid(gate_logits.astype(F32)).reshape(b, s, N_BRANCH, d).astype(x.dtype)
    mixed = gates[..., 0, :] * y_a + gates[..., 1, :] * y_b + gates[..., 2, :] * y_c
    return mixed @ w_out

def moe_ffn(x, w_router, b_router, w1, b1, w2, b2):
    b, s, d = x.shape
    xt = x.reshape(-1, d)
    logits = (xt @ w_router + b_router).astype(F32)
    top_val, top_idx = lax.top_k(logits, TOP_K)
    top_w = jax.nn.softmax(top_val, axis=-1)
    comb = jnp.einsum("nk,nke->ne", top_w, jax.nn.one_hot(top_idx, N_EXPERTS, dtype=F32))
    out = jnp.zeros((xt.shape[0], d), F32)
    for e in range(N_EXPERTS):
        hidden = xt @ w1[e] + b1[e]
        gate = jnp.minimum(hidden[:, :D_EXPERT], SWIGLU_LIMIT)
        lin = jnp.clip(hidden[:, D_EXPERT:], -SWIGLU_LIMIT, SWIGLU_LIMIT)
        act = gate * jax.nn.sigmoid(SWIGLU_ALPHA * gate) * (lin + 1.0)
        out = out + comb[:, e:e + 1] * (act @ w2[e] + b2[e])
    return out.astype(x.dtype).reshape(b, s, d)

def setup_inputs(seed: int = 0) -> dict:
    key = jax.random.key(seed)
    ks = jax.random.split(key, 32)
    L, D, E, F = DEPTH, D_MODEL, N_EXPERTS, D_EXPERT
    nrm = lambda i, shape, scale: jax.random.normal(ks[i], shape, F32) * scale
    a_log = jnp.log(jax.random.uniform(ks[5], (L, A_HEADS), F32, 1.0, 16.0))
    dt = jnp.exp(jax.random.uniform(ks[6], (L, A_HEADS), F32, math.log(1e-3), math.log(1e-1)))
    a_dt_bias = dt + jnp.log(-jnp.expm1(-dt))
    return {
        "x": nrm(0, (BATCH, SEQ, D), 1.0),
        "ln_in_g": 1.0 + nrm(1, (D,), 0.02),
        "ln_in_b": nrm(2, (D,), 0.02),
        "rel_bias": nrm(3, (REL_BUCKETS, C_QHEADS), 0.5),
        "w_in": nrm(4, (L, D, N_IN), D ** -0.5),
        "a_conv_w": nrm(7, (L, A_CONV, 3 * A_W), A_CONV ** -0.5),
        "a_log": a_log,
        "a_dt_bias": a_dt_bias,
        "a_norm_g": 1.0 + nrm(8, (L, A_DV), 0.02),
        "w_a_out": nrm(9, (L, A_W, D), A_W ** -0.5 * DEEPNORM_BETA),
        "b_dw_w": nrm(10, (L, B_KERNEL, B_CH), B_KERNEL ** -0.5),
        "b_dw_b": nrm(11, (L, B_CH), 0.02),
        "b_ln_g": 1.0 + nrm(12, (L, B_CH), 0.02),
        "b_ln_b": nrm(13, (L, B_CH), 0.02),
        "w_b_out": nrm(14, (L, B_CH, D), B_CH ** -0.5 * DEEPNORM_BETA),
        "c_sinks": nrm(15, (L, C_QHEADS), 1.0),
        "w_c_out": nrm(16, (L, C_QW, D), C_QW ** -0.5 * DEEPNORM_BETA),
        "w_out": nrm(17, (L, D, D), D ** -0.5 * DEEPNORM_BETA),
        "ln1_g": 1.0 + nrm(18, (L, D), 0.02),
        "ln1_b": nrm(19, (L, D), 0.02),
        "w_router": nrm(20, (L, D, E), D ** -0.5),
        "b_router": nrm(21, (L, E), 0.01),
        "w1": nrm(22, (L, E, D, 2 * F), D ** -0.5),
        "b1": nrm(23, (L, E, 2 * F), 0.02),
        "w2": nrm(24, (L, E, F, D), F ** -0.5 * DEEPNORM_BETA),
        "b2": nrm(25, (L, E, D), 0.02),
        "ln2_g": 1.0 + nrm(26, (L, D), 0.02),
        "ln2_b": nrm(27, (L, D), 0.02),
    }

def reference(x, ln_in_g, ln_in_b, rel_bias, w_in, a_conv_w, a_log, a_dt_bias, a_norm_g, w_a_out,
              b_dw_w, b_dw_b, b_ln_g, b_ln_b, w_b_out, c_sinks, w_c_out, w_out, ln1_g, ln1_b,
              w_router, b_router, w1, b1, w2, b2, ln2_g, ln2_b):
    h = layer_norm(x, ln_in_g, ln_in_b)
    for l in range(DEPTH):
        mix = hybrid_mixer(h, rel_bias, w_in[l], a_conv_w[l], a_log[l], a_dt_bias[l], a_norm_g[l], w_a_out[l],
                           b_dw_w[l], b_dw_b[l], b_ln_g[l], b_ln_b[l], w_b_out[l], c_sinks[l], w_c_out[l], w_out[l])
        h = layer_norm(DEEPNORM_ALPHA * h + mix, ln1_g[l], ln1_b[l])
        ffn = moe_ffn(h, w_router[l], b_router[l], w1[l], b1[l], w2[l], b2[l])
        h = layer_norm(DEEPNORM_ALPHA * h + ffn, ln2_g[l], ln2_b[l])
    return h


_drawn_inputs = setup_inputs


def setup_inputs(seed=0):
    import zlib

    import numpy as np

    out = dict(_drawn_inputs(seed))
    spreads = {}
    factors = {'rel_bias': 2.75,
     'a_log': 5.309,
     'a_norm_g': 21.361,
     'b_dw_b': 3.35,
     'b_ln_g': 18.666,
     'b_ln_b': 20.588,
     'c_sinks': 8.0,
     'b_router': 6.251,
     'b1': 8.0,
     'b2': 6.452,
     'ln2_g': 7.861,
     'ln2_b': 8.728}
    for name, (base, spread) in spreads.items():
        noise = np.random.default_rng([zlib.crc32(name.encode()), seed]).standard_normal(out[name].shape)
        drawn = base * np.exp(spread * noise) if base else spread * noise
        out[name] = __import__('jax').numpy.asarray(drawn.astype(out[name].dtype))
    for name, factor in factors.items():
        out[name] = (out[name] * factor).astype(out[name].dtype)
    return out
```

```python
import math
import numpy as np
import concourse.bass as bass
from concourse import mybir
from contextlib import ExitStack

P = 128
D = 1024
S = 256
DC = D // P
ST = S // P
AH = 4
CH = 64
NB = 4
KB = 31
KA = 4
NE = 32
F = 1024
W1C = 4
NARROW, WIDE = 64, 128
ALPHA = 2.0 ** 0.25
LEVELS = 6
QH, HD = 8, 64

O_AQ, O_AK, O_AV, O_AZ, O_AB, O_BV, O_BG, O_CQ, O_CK, O_G = 0, 512, 1024, 1536, 2048, 2056, 2568, 3080, 3592, 3848
N_IN = 6920

C_ID, C_TRI, C_SUF, C_STR, C_LVL = 0, 128, 256, 384, 512
C_TRI128 = C_LVL + LEVELS * P
C_ONES = C_TRI128 + P
C_IOTA1 = C_ONES + P
C_IOTA0 = C_IOTA1 + P
C_OH = C_IOTA0 + NE
C_I512 = C_OH + 384
C_I128 = C_I512 + P
N_C = C_I128 + P

H_ACW = 0
H_BW = H_ACW + 12 * KA
H_BB = H_BW + NB * KB
H_BG = H_BB + NB
H_BN = H_BG + NB
H_AN = H_BN + NB
N_H = H_AN + 1

R_ALOG, R_DT, R_SINK, R_BR = 0, 4, 8, 16
N_R = R_BR + NE


def constants():
    i = np.arange(P)
    j, c = i[:, None], i[None, :]
    same = j // CH == c // CH
    out = np.zeros((P, N_C), np.float32)
    out[:, C_ID:C_ID + P] = j == c
    out[:, C_TRI:C_TRI + P] = same & (j <= c)
    out[:, C_SUF:C_SUF + P] = same & (j > c)
    out[:, C_STR:C_STR + P] = same & (j < c)
    for l in range(LEVELS):
        s = 1 << l
        out[:, C_LVL + l * P:C_LVL + (l + 1) * P] = (j // (2 * s) == c // (2 * s)) & (c // s % 2 == 1) & (j // s % 2 == 0)
    out[:, C_TRI128:C_TRI128 + P] = j < c
    out[:, C_ONES:C_ONES + P] = 1.0
    out[:, C_IOTA1:C_IOTA1 + P] = c + 1
    out[:, C_IOTA0:C_IOTA0 + NE] = np.arange(NE)
    out[:, C_I512:C_I512 + P] = 1.0 / 512
    out[:, C_I128:C_I128 + P] = 1.0 / 128
    m = np.arange(384)
    dist = P - (m - 127)
    exact = 16
    large = exact + (np.log(np.maximum(dist, 1).astype(np.float32) / np.float32(exact))
                     / np.float32(math.log(128 / exact)) * np.float32(exact)).astype(np.int32)
    bucket = np.where(dist < exact, dist, np.minimum(large, 31))
    seen = (dist >= 0) & (dist < P)
    out[32, C_OH:C_OH + 384] = ~seen
    for b in range(32):
        out[b, C_OH:C_OH + 384] = seen & (bucket == b)
    return out


def mixer_jobs():
    jobs = [f"hT{t}{h}" for t in range(ST) for h in range(2)]
    jobs += ["relvec"]
    jobs += ["projBV0", "projBV1", "projBG0", "projBG1", "ab", "CK", "CV"]
    jobs += ["gcol", "grow0", "grow1", "brow0", "brow1"]
    jobs += ["projK0", "projK1", "projQ0", "projQ1", "ssK0", "ssK1", "projV0", "projV1", "ssQ0", "ssQ1"]
    jobs += ["kk0", "kk1", "ktok0", "ktok1", "qk0", "qk1"]
    jobs += ["projZ0", "projZ1", "vtok0", "vtok1"]
    jobs += ["projC0", "projC1"]
    fill = [f"projG{g}{h}" for g in range(6) for h in range(2)]
    attn = []
    for n in range(6):
        attn += [[f"sc{n}"], [f"pt{n}"], [f"pv{n}"]]
    attn = [attn[0], attn[3]] + [x for n in range(6) for x in ([attn[3 * n + 1]] + ([attn[3 * n + 6]] if n < 4 else []) + [attn[3 * n + 2]])]
    jobs += ["trT0", "trT1"]
    for l in range(1, LEVELS):
        jobs += [f"lp{l}0", f"lp{l}1"] + fill[:1]
        fill = fill[1:]
        if l < LEVELS - 1:
            jobs += [f"lt{l}0", f"lt{l}1"]
        jobs += [f"lu{l}0", f"lu{l}1"] + fill[:1]
        fill = fill[1:]
    jobs += ["bmean"] + fill[:1]
    fill = fill[1:]
    jobs += ["wT0", "wT1"]
    k = 0
    for n in range(4):
        jobs += [f"vn{n}"]
        for x in attn[k:k + 2]:
            jobs += x
        k += 2
        if n == 0:
            jobs += fill[:1]
        if n == 1:
            jobs += ["bvar"]
        jobs += [f"oT{n}"]
        if n < 3:
            jobs += [f"dS{n}"]
        for x in attn[k:k + 2]:
            jobs += x
        k += 2
    for x in attn[k:]:
        jobs += x
    jobs += ["yB0", "yB1", "yB2", "yB3"]
    jobs += ["rms0", "rms1"]
    jobs += ["yC0", "yC1", "yC2", "yC3", "yA0", "yA1", "yA2", "yA3"]
    jobs += ["mix00", "mix10", "mix01", "mix11"]
    jobs += [f"h1T{t}{h}" for t in range(ST) for h in range(2)]
    jobs += ["router", "rank", "count", "combT"]
    return jobs


JOBS = mixer_jobs()
BANK = {name: n % 8 for n, name in enumerate(JOBS)}
FILL = {name: n // 8 + 1 for n, name in enumerate(JOBS)}
TILES = ["BV", "BG", "M", "K", "Q", "V", "Z", "C", "G0", "G1", "G2", "G3", "G4", "G5", "WB", "WC", "WA", "WO0", "WO1"]
TILE = {name: n for n, name in enumerate(TILES)}
LAST_JOB = {"BV": "projBV1", "BG": "projBG1", "M": "CV", "K": "projK1", "Q": "projQ1", "V": "projV1", "Z": "projZ1",
            "C": "projC1", "WB": "yB3", "WC": "yC3", "WA": "yA3", "WO0": "mix10", "WO1": "mix11"}
LAST_JOB.update({f"G{g}": f"projG{g}1" for g in range(6)})
NT = len(TILES)


def build(nc, x, lnp, rel, w_in, wa, wb, wc, wo, chan, rows, w_router, w1, b1, w2, b2, cst, out):
    f32, i32, u32 = mybir.dt.float32, mybir.dt.int32, mybir.dt.uint32
    ALU, ACT, AX = mybir.AluOpType, mybir.ActivationFunctionType, mybir.AxisListType
    ctx = ExitStack()
    with ctx:
        def sb(name, shape, dt=f32):
            return ctx.enter_context(nc.sbuf_tensor(name, shape, dt))

        def sem(name):
            return ctx.enter_context(nc.semaphore(name))

        w1s = sb("w1s", [P, W1C, 4096])
        w2s = sb("w2s", [P, 2, 4096])
        consts = sb("consts", [P, N_C])
        chp = sb("chp", [P, N_H])
        rowp = sb("rowp", [P, N_R])
        lngb = sb("lngb", [P, 2, D])
        h = sb("h", [P, ST, D])
        hT = sb("hT", [P, DC, S])
        gates = sb("gates", [P, 24, S])
        arena = sb("arena", [P, 13, 1024])
        small = sb("small", [P, 272])
        relw = sb("relw", [33, 8])
        tab_i = sb("tab_i", [1, 3 * NE + 1], i32)
        idx = sb("idx", [P, ST, 8], u32)

        def a4(k, n=4):
            return arena[:, k, :].rearrange("p (n c) -> p n c", n=n)

        def w2v(k, n=4):
            return w2s[:, k // 4, (k % 4) * 1024:(k % 4 + 1) * 1024].rearrange("p (n c) -> p n c", n=n)

        kT, qT, vT = a4(0), a4(1), a4(2)
        az = a4(3)
        cq = a4(4)
        ckv = arena[:, 5, :]
        ck, cv = ckv[:, 0:256], ckv[:, 256:512].rearrange("p (b c) -> p b c", b=2)
        sq = a4(6)
        mst = a4(2, 8)
        convin = gates[:, 0:13, :].rearrange("p a b -> p (a b)")[:, 0:12 * 259].rearrange("p (n c) -> p n c", n=12)
        lnf = lngb[:, :, :].rearrange("p a b -> p (a b)")
        bv = lnf[:, 0:NB * (KB - 1 + S)].rearrange("p (n c) -> p n c", n=NB)
        relv, tmpb = lnf[0:8, 1152:1536], lnf[:, 1536:1792]
        bacc = w2v(0)
        kbt, kdt, vbt = a4(7, 8), a4(8, 8), a4(9, 8)
        at = a4(10, 8)
        tm, um = a4(11, 8), a4(12, 8)
        dt_ = w2v(1, 8)
        eg = w2v(2, 8)
        brow = w2v(3, 8)
        p1 = brow
        bias = w2s[:, 1, 0:2048].rearrange("p (h k) -> p h k", h=8)
        ssc = w2s[:, 1, 2048:3072].rearrange("p (n k) -> p n k", n=2)
        pts = w2s[:, 1, 3072:4096].rearrange("p (n k) -> p n k", n=2)
        wT = at
        oaT = tm
        ocT = kT
        vn = arena[:, 2, 0:512].rearrange("p (n c) -> p n c", n=AH)
        st = arena[:, 2, 512:1024].rearrange("p (n c) -> p n c", n=AH)
        mxT = hT
        xT = arena[:, 0, :].rearrange("p (n c) -> p n c", n=8)
        actT = arena[:, 1, :].rearrange("p (n c) -> p n c", n=8)
        hb = arena[:, 2, 0:512].rearrange("p (n c) -> p n c", n=4)
        gm = arena[:, 3, 0:256].rearrange("p (n c) -> p n c", n=2)
        sg = arena[:, 3, 256:512].rearrange("p (n c) -> p n c", n=2)
        ln_ = arena[:, 3, 512:768].rearrange("p (n c) -> p n c", n=2)
        gs = arena[:, 3, 768:1024].rearrange("p (n c) -> p n c", n=2)
        ys = arena[:, 4, :]
        b2s = arena[0:NE, 7, :]
        b1s = arena[:, 8, 0:512].rearrange("p (e c) -> p e c", e=NE)
        wr = arena[:, 8, 512:768].rearrange("p (k e) -> p k e", k=DC)
        pg = arena[:, 5, 0:256].rearrange("p (n c) -> p n c", n=2)
        pw = arena[:, 5, 256:512].rearrange("p (n c) -> p n c", n=2)
        ptw = arena[:, 5, 512:768].rearrange("p (n c) -> p n c", n=2)
        comb = arena[:, 6, 0:64].rearrange("p (t e) -> p t e", t=2)
        mask = arena[:, 6, 64:128].rearrange("p (t e) -> p t e", t=2)
        rk = arena[:, 6, 128:256].rearrange("p (k t e) -> p k t e", k=2, t=2)
        lg = arena[:, 6, 256:320].rearrange("p (t e) -> p t e", t=2)
        oneh = arena[:, 6, 320:384].rearrange("p (t e) -> p t e", t=2)
        combTs = arena[0:NE, 6, 384:640].rearrange("p (t c) -> p t c", t=2)
        tabf = arena[0:1, 6, 640:768].rearrange("p (t e) -> p t e", t=4)

        def col(a, b):
            return small[:, a:b]

        stats = col(0, 24).rearrange("p (t k s) -> p t k s", t=2, k=2)
        mv = col(24, 28).rearrange("p (t k) -> p t k", t=2)
        rstd = col(28, 30)
        beta = col(32, 40).rearrange("p (t h) -> p t h", t=2)
        gg = col(40, 48).rearrange("p (t h) -> p t h", t=2)
        uu, au, yy, ss, s2, po = (col(48 + 8 * k, 56 + 8 * k) for k in range(6))
        ealog = col(96, 100)
        gcs = col(104, 120).rearrange("p (k t h) -> p k t h", k=2, t=2)
        egc = col(120, 136).rearrange("p (k t h) -> p k t h", k=2, t=2)
        bek = col(136, 144).rearrange("p (t h) -> p t h", t=2)
        mxx = col(144, 168).rearrange("p (n k) -> p n k", n=6)
        smx = col(168, 192).rearrange("p (n k) -> p n k", n=6)
        esk = col(192, 216).rearrange("p (n k) -> p n k", n=6)
        eps5, eps6 = col(216, 217), col(217, 218)
        top = col(224, 240).rearrange("p (t k) -> p t k", t=2)
        ntop = col(240, 242)
        tsum = col(242, 244)
        tw = col(244, 252).rearrange("p (t k) -> p t k", t=2)
        idf = col(252, 268).rearrange("p (t k) -> p t k", t=2)

        ident = consts[:, C_ID:C_ID + P]
        ones = consts[:, C_ONES:C_ONES + P]
        inv512 = consts[:, C_I512:C_I512 + P]
        inv128 = consts[:, C_I128:C_I128 + P]

        rel_d = nc.dram_tensor("relative_vector", (8, P, 384), f32)
        rel_toep = bass.AP(rel_d.ap().tensor, 127, [[383, P], [P * 384, 8], [1, 256]])

        bk = [ctx.enter_context(nc.psum_tensor(f"bank{b}", [P, 512], f32))[:, :] for b in range(8)]
        acc = [[bk[0], bk[1]], [bk[2], bk[3]]]
        wka, wkb = bk[4], bk[5]
        yb = [bk[6], bk[7]]

        filled = [sem(f"bank_filled{b}") for b in range(8)]
        drained = [sem(f"bank_drained{b}") for b in range(8)]
        x_in, params_in, wr_in = sem("x_in"), sem("params_in"), sem("wr_in")
        ln_in = [sem(f"ln_in{k}") for k in range(3)]
        tile_in = [sem(f"tile_in{k}") for k in range(W1C)]
        w2_in = [sem("w2_in0"), sem("w2_in1")]
        rel_out, rel_in, store = sem("rel_out"), sem("rel_in"), sem("stored")
        dve_step, act_step, pool_step = sem("dve_step"), sem("act_step"), sem("pool_step")
        names = ("pad_zero relvec_sb ln_used var_ready sd_ready h_ready hT_ready bvin bgate bglu conv_in conv_out silu_done "
                 "sq_ready l2_sd l2_ready beta_ready aa_ready expu g_ready ealog_rd gcs_ready egc_ready eg_ready "
                 "brow_ready dmin dexp dt_ready at_ready qk_ready kb_ready vb_ready mst_ready t_ready u_ready p1_ready "
                 "qd_ready z_ready cq_ready ck_ready cv_ready gates_ready bconv bcent bsq bsd bnorm bsilu wT_ready vn_ready oT_ready st_ready "
                 "osq rms_sd oa_ready ssc_ready pexp pnorm pt_ready oc_ready mx_ready h1T_ready logits top_ready texp "
                 "comb_ready mask_ready combT_ready table_ready mixer_done "
                 "p_ready gathered xt_ready pt_filled ptw_ready h_filled h_read g_clamped sig_ready act_ready y_filled ys_ready "
                 "swish_ready all_scattered").split()
        sm = {n: sem(n) for n in names}

        def wait_fill(eng, job):
            eng.wait_ge(filled[BANK[job]], FILL[job])

        block = ctx.enter_context(nc.Block())

        @block.sync
        def _(sp):
            sp.dma_start(h[:, :, :], x.rearrange("(t p) d -> p t d", p=P)).then_inc(x_in, 16)

            def load_ln(k):
                sp.dma_start(lngb[:, :, :], bass.AP(lnp.tensor, 2 * D * k, [[0, P], [D, 2], [1, D]])).then_inc(ln_in[k], 16)

            load_ln(0)
            sp.dma_start(consts[:, :], cst).then_inc(params_in, 16)
            sp.dma_start(chp[:, :], chan).then_inc(params_in, 16)
            sp.dma_start(rowp[:, :], bass.AP(rows.tensor, 0, [[0, P], [1, N_R]])).then_inc(params_in, 16)
            sp.dma_start(relw[0:32, :], rel).then_inc(params_in, 16)

            def load_tile(name):
                n = TILE[name]
                if n >= W1C:
                    wait_fill(sp, LAST_JOB[TILES[n - W1C]])
                s = n % W1C
                v8 = w1s[:, s, :].rearrange("p (k c) -> p k c", k=DC)
                v4 = w1s[:, s, :].rearrange("p (k c) -> p k c", k=4)

                def cols(a, b):
                    return w_in[:, a:b].rearrange("(k p) c -> p k c", p=P)

                if name == "M":
                    sp.dma_start(v8[:, :, 0:8], cols(O_AB, O_AB + 8)).then_inc(tile_in[s], 16)
                    sp.dma_start(v8[:, :, 128:384], cols(O_CK, O_CK + 256)).then_inc(tile_in[s], 16)
                elif name in ("WA", "WB"):
                    src = wa if name == "WA" else wb
                    sp.dma_start(v4, src.rearrange("(k p) c -> p k c", p=P)).then_inc(tile_in[s], 16)
                elif name == "WC":
                    for g in range(2):
                        sp.dma_start(v4[64 * g:64 * g + 64, :, :],
                                     wc[256 * g:256 * g + 256, :].rearrange("(j c) n -> c j n", c=64)).then_inc(tile_in[s], 16)
                elif name in ("WO0", "WO1"):
                    c = 512 * int(name[2])
                    sp.dma_start(v8, wo[:, c:c + 512].rearrange("(k p) c -> p k c", p=P)).then_inc(tile_in[s], 16)
                elif name == "C":
                    dst = w1s[:, s, :].rearrange("p (k j g c) -> p k g j c", k=DC, j=4, g=2)
                    for k in range(DC):
                        for g in range(2):
                            sp.dma_start(dst[:, k, g], w_in[k * P:(k + 1) * P, O_CQ + 256 * g:O_CQ + 256 * g + 256]
                                         .rearrange("p (j c) -> p j c", j=4)).then_inc(tile_in[s], 16)
                else:
                    base = {"BV": O_BV, "BG": O_BG, "K": O_AK, "Q": O_AQ, "V": O_AV, "Z": O_AZ}.get(name)
                    if base is None:
                        base = O_G + 512 * int(name[1])
                    sp.dma_start(v8, cols(base, base + 512)).then_inc(tile_in[s], 16)

            for n, name in enumerate(TILES):
                load_tile(name)
                if n == 4:
                    sp.wait_ge(sm["relvec_sb"], 1)
                    sp.dma_start(rel_d[:, :, :], relv.rearrange("h (o c) -> h o c", o=1).broadcast_to([8, P, 384])).then_inc(rel_out, 16)
                    sp.wait_ge(rel_out, 16)
                    sp.dma_start(bias, rel_toep).then_inc(rel_in, 16)

            def load_w1(e, j):
                s = (NT + j) % W1C
                for g in range(2):
                    dst = w1s[:, s, :].rearrange("p (k g c) -> p k g c", k=DC, g=2)[:, :, g, :]
                    src = w1[e, :, g * F + 256 * j:g * F + 256 * j + 256] if isinstance(e, int) else \
                        w1[bass.ds(e, 1), :, g * F + 256 * j:g * F + 256 * j + 256].rearrange("o d c -> (o d) c")
                    sp.dma_start(dst, src.rearrange("(k p) c -> p k c", p=P)).then_inc(tile_in[s], 16)

            def load_w2(e, q):
                dst = w2s[:, q, :].rearrange("p (k c) -> p k c", k=4)
                src = w2[e, 512 * q:512 * q + 512, :] if isinstance(e, int) else \
                    w2[bass.ds(e, 1), 512 * q:512 * q + 512, :].rearrange("o d c -> (o d) c")
                sp.dma_start(dst, src.rearrange("(k p) c -> p k c", p=P)).then_inc(w2_in[q], 16)

            sp.wait_ge(sm["mixer_done"], 2)
            load_ln(1)
            sp.dma_start(wr, w_router.rearrange("(k p) e -> p k e", p=P)).then_inc(wr_in, 16)
            sp.dma_start(b1s, b1).then_inc(wr_in, 16)
            sp.dma_start(b2s, b2).then_inc(wr_in, 16)
            for j in range(W1C):
                wait_fill(sp, LAST_JOB[TILES[NT - W1C + j]])
                load_w1(0, j)
            load_w2(0, 0)
            load_w2(0, 1)
            sp.wait_ge(sm["ln_used"], 2)
            load_ln(2)
            sp.wait_ge(sm["table_ready"], 1)
            with sp.Fori(1, NE) as e:
                last = sp.value_load(tab_i[0:1, bass.ds(e + 2 * NE, 1)], min_val=0, max_val=2 * NE)
                for j in range(W1C):
                    sp.wait_ge(sm["h_filled"], last * 4 + (j + 1))
                    load_w1(e, j)
                sp.wait_ge(sm["y_filled"], last + 1)
                load_w2(e, 0)
                load_w2(e, 1)
            sp.wait_ge(sm["h_ready"], 6)
            sp.dma_start(out.rearrange("(t p) d -> p t d", p=P), h[:, :, :]).then_inc(store, 16)
            sp.wait_ge(store, 16)

        @block.gpsimd
        def _(pool):
            pool.wait_ge(params_in, 64)
            pool.wait_ge(sm["at_ready"], 2)
            wait_fill(pool, "vtok1")
            for l in range(1, LEVELS):
                if l > 1:
                    wait_fill(pool, f"lp{l - 1}1")
                m = consts[:, C_LVL + l * P:C_LVL + (l + 1) * P].rearrange("p (o c) -> p o c", o=1).broadcast_to([P, 8, P])
                pool.tensor_tensor(mst, at, m, ALU.mult).then_inc(sm["mst_ready"], 1)

        @block.scalar
        def _(act):
            def drain(job, ins):
                ins.then_inc(drained[BANK[job]], 1)

            def bank(job):
                wait_fill(act, job)
                return bk[BANK[job]]

            n_act = [0]

            def link(ins):
                n_act[0] += 1
                ins.then_inc(act_step, 1)
                act.wait_ge(act_step, n_act[0])

            A = nc.scalar.activation
            act.wait_ge(sm["pad_zero"], 1)
            for t in range(ST):
                act.wait_ge(sm["var_ready"], t + 1)
                A(rstd[:, t:t + 1], mv[:, t, 1:2], ACT.Sqrt, bias=eps5).then_inc(sm["sd_ready"], 1)
            for t in range(ST):
                for hh in range(2):
                    j = f"hT{t}{hh}"
                    link(A(hT[:, 4 * hh:4 * hh + 4, t * P:(t + 1) * P], bank(j).rearrange("p (k c) -> p k c", k=4), ACT.Copy))
                    act.sem_inc(drained[BANK[j]], 1)
                    act.sem_inc(sm["hT_ready"], 1)
            j = "relvec"
            link(A(relv, bank(j)[0:8, 0:384], ACT.Copy))
            act.sem_inc(drained[BANK[j]], 1)
            act.sem_inc(sm["relvec_sb"], 1)

            def proj(job, dst, func=ACT.Copy):
                drain(job, A(dst, bank(job).rearrange("p (n c) -> p n c", n=2), func))

            proj("projBV0", bv[:, 0:2, KB - 1:])
            proj("projBV1", bv[:, 2:4, KB - 1:])
            proj("projBG0", bacc[:, 0:2, :], ACT.Sigmoid)
            j = "projBG1"
            link(A(bacc[:, 2:4, :], bank(j).rearrange("p (n c) -> p n c", n=2), ACT.Sigmoid))
            act.sem_inc(drained[BANK[j]], 1)
            act.sem_inc(sm["bgate"], 1)
            j = "ab"
            abv = bank(j)[:, 0:16].rearrange("p (t k h) -> p t k h", t=2, k=2)
            link(A(beta, abv[:, :, 0, :], ACT.Sigmoid))
            link(A(uu.rearrange("p (t h) -> p t h", t=2), abv[:, :, 1, :], ACT.Copy))
            act.sem_inc(drained[BANK[j]], 1)
            act.sem_inc(sm["beta_ready"], 1)
            A(ealog, rowp[:, R_ALOG:R_ALOG + 4], ACT.Exp)
            act.wait_ge(sm["aa_ready"], 1)
            A(yy, au, ACT.Exp, scale=-1.0).then_inc(sm["expu"], 1)
            drain("CK", A(ck, bank("CK")[:, 0:256], ACT.Copy))
            j = "CV"
            link(A(cv, bank(j)[:, 0:256].rearrange("p (b c) -> p b c", b=2), ACT.Copy))
            act.sem_inc(drained[BANK[j]], 1)
            act.sem_inc(sm["cv_ready"], 1)
            act.wait_ge(sm["gcs_ready"], 1)
            A(egc, gcs, ACT.Exp).then_inc(sm["egc_ready"], 1)
            act.wait_ge(sm["dmin"], 2)
            for t in range(ST):
                j = f"grow{t}"
                drain(j, A(eg[:, 4 * t:4 * t + 4, :], bank(j).rearrange("p (n c) -> p n c", n=4), ACT.Exp))
            for t in range(ST):
                j = f"brow{t}"
                drain(j, A(brow[:, 4 * t:4 * t + 4, :], bank(j).rearrange("p (n c) -> p n c", n=4), ACT.Copy))
            link(A(dt_, dt_, ACT.Exp))
            act.sem_inc(sm["dexp"], 1)
            base = {"Q": 0, "K": 4, "V": 8}
            dstT = {"K": kT, "Q": qT, "V": vT}

            def conv_in(x_):
                for hh in range(2):
                    j = f"proj{x_}{hh}"
                    link(A(convin[:, base[x_] + 2 * hh:base[x_] + 2 * hh + 2, KA - 1:], bank(j).rearrange("p (n c) -> p n c", n=2), ACT.Copy))
                    act.sem_inc(drained[BANK[j]], 1)
                act.sem_inc(sm["conv_in"], 1)

            def silu(x_, n):
                act.wait_ge(sm["conv_out"], n)
                link(A(dstT[x_], dstT[x_], ACT.Silu))
                act.sem_inc(sm["silu_done"], 1)

            def l2(x_, n):
                if n > 1:
                    wait_fill(act, "ssK1")
                link(A(sq, dstT[x_], ACT.Square))
                act.sem_inc(sm["sq_ready"], 1)

            def l2_root(x_):
                for hh in range(2):
                    j = f"ss{x_}{hh}"
                    link(A(sq[:, 2 * hh:2 * hh + 2, :], bank(j).rearrange("p (n c) -> p n c", n=2), ACT.Sqrt, bias=eps6))
                    act.sem_inc(drained[BANK[j]], 1)
                act.sem_inc(sm["l2_sd"], 1)

            conv_in("K")
            silu("K", 1)
            l2("K", 1)
            conv_in("Q")
            l2_root("K")
            conv_in("V")
            act.wait_ge(sm["l2_ready"], 1)
            silu("Q", 2)
            l2("Q", 2)
            l2_root("Q")
            silu("V", 3)
            for hh in range(2):
                j = f"projZ{hh}"
                link(A(az[:, 2 * hh:2 * hh + 2, :], bank(j).rearrange("p (n c) -> p n c", n=2), ACT.Silu))
                act.sem_inc(drained[BANK[j]], 1)
            for hh in range(2):
                j = f"projC{hh}"
                link(A(cq[:, 2 * hh:2 * hh + 2, :], bank(j).rearrange("p (n c) -> p n c", n=2), ACT.Copy))
                act.sem_inc(drained[BANK[j]], 1)
            act.sem_inc(sm["cq_ready"], 1)

            def gate(job):
                k = 4 * int(job[5]) + 2 * int(job[6])
                drain(job, A(gates[:, k:k + 2, :], bank(job).rearrange("p (n c) -> p n c", n=2), ACT.Sigmoid))

            def level_p(job):
                t = int(job[3])
                link(A(p1[:, 4 * t:4 * t + 4, :], bank(job).rearrange("p (n c) -> p n c", n=4), ACT.Copy))
                act.sem_inc(drained[BANK[job]], 1)
                act.sem_inc(sm["p1_ready"], 1)

            def w_t(job):
                t = int(job[2])
                link(A(wT[:, 4 * t:4 * t + 4, :], bank(job).rearrange("p (n c) -> p n c", n=4), ACT.Copy, scale=-1.0))
                act.sem_inc(drained[BANK[job]], 1)
                act.sem_inc(sm["wT_ready"], 1)

            def v_new(job):
                r = 64 * (int(job[2]) % 2)
                link(A(vn[r:r + 64, :, :], bank(job)[r:r + 64, :].rearrange("p (n c) -> p n c", n=4), ACT.Copy))
                act.sem_inc(drained[BANK[job]], 1)
                act.sem_inc(sm["vn_ready"], 1)

            def o_t(job):
                n = int(job[2])
                link(A(oaT.rearrange("p a b -> p (a b)").rearrange("p (n c) -> p n c", n=4)[:, :, n * CH:(n + 1) * CH],
                       bank(job)[:, 0:256].rearrange("p (n c) -> p n c", n=4), ACT.Copy))
                act.sem_inc(drained[BANK[job]], 1)
                act.sem_inc(sm["oT_ready"], 1)

            def softmax(n):
                heads, keys = (4, 128) if n < 2 else (2, 256)
                act.wait_ge(sm["ssc_ready"], n + 1)
                for k in range(heads):
                    hd = 4 * n + k if n < 2 else 2 * (n - 2) + k
                    A(ssc[:, n % 2, k * keys:(k + 1) * keys], ssc[:, n % 2, k * keys:(k + 1) * keys], ACT.Exp,
                      bias=mxx[:, n, k:k + 1], accum_out=smx[:, n, k:k + 1])
                    ins = A(esk[:, n, k:k + 1], rowp[:, R_SINK + hd:R_SINK + hd + 1], ACT.Exp, bias=mxx[:, n, k:k + 1])
                ins.then_inc(sm["pexp"], 1)

            def p_t(job):
                n = int(job[2])
                link(A(pts[:, n % 2, :], bank(job), ACT.Copy))
                act.sem_inc(drained[BANK[job]], 1)
                act.sem_inc(sm["pt_ready"], 1)

            def p_v(job):
                n = int(job[2])
                g, j0, nh, q0 = (n, 0, 4, 0) if n < 2 else ((n - 2) // 2, 2 * (n % 2), 2, P)
                r = 64 * g
                link(A(ocT[r:r + 64, j0:j0 + nh, q0:q0 + P], bank(job)[r:r + 64, 0:nh * P].rearrange("p (n c) -> p n c", n=nh), ACT.Copy))
                act.sem_inc(drained[BANK[job]], 1)
                act.sem_inc(sm["oc_ready"], 1)

            def b_var(job):
                drain(job, A(tmpb, bank(job)[:, 0:256], ACT.Sqrt, bias=eps5))
                act.wait_ge(drained[BANK[job]], FILL[job])
                act.sem_inc(sm["bsd"], 1)
                act.wait_ge(sm["bnorm"], 1)
                for c in range(NB):
                    ins = A(bacc[:, c, :], bacc[:, c, :], ACT.Silu, bias=chp[:, H_BN + c:H_BN + c + 1], scale=chp[:, H_BG + c:H_BG + c + 1])
                ins.then_inc(sm["bsilu"], 1)

            def b_square(job):
                act.wait_ge(sm["bcent"], 1)
                A(bv[:, :, 0:S], bacc, ACT.Square).then_inc(sm["bsq"], 1)

            steps = {"projG": gate, "lp": level_p, "wT": w_t, "vn": v_new, "oT": o_t, "pt": p_t, "pv": p_v, "bvar": b_var, "bmean": b_square}
            start = JOBS.index("trT0")
            for job in JOBS[start:JOBS.index("yB0")]:
                for key, step in steps.items():
                    if job.startswith(key):
                        step(job)
                if job.startswith("sc"):
                    softmax(int(job[2]))
            act.wait_ge(sm["oT_ready"], 4)
            link(A(sq, oaT.rearrange("p a b -> p (a b)").rearrange("p (n c) -> p n c", n=4), ACT.Square))
            act.sem_inc(sm["osq"], 1)
            for hh in range(2):
                j = f"rms{hh}"
                link(A(sq[:, 2 * hh:2 * hh + 2, :], bank(j).rearrange("p (n c) -> p n c", n=2), ACT.Sqrt, bias=eps6))
                act.sem_inc(drained[BANK[j]], 1)
            act.sem_inc(sm["rms_sd"], 1)
            act.sem_inc(sm["mixer_done"], 1)
            for t in range(ST):
                act.wait_ge(sm["var_ready"], ST + t + 1)
                A(rstd[:, t:t + 1], mv[:, t, 1:2], ACT.Sqrt, bias=eps5).then_inc(sm["sd_ready"], 1)
            for t in range(ST):
                for hh in range(2):
                    j = f"h1T{t}{hh}"
                    link(A(hT[:, 4 * hh:4 * hh + 4, t * P:(t + 1) * P], bank(j).rearrange("p (k c) -> p k c", k=4), ACT.Copy))
                    act.sem_inc(drained[BANK[j]], 1)
                    act.sem_inc(sm["h1T_ready"], 1)
            for t in range(ST):
                act.wait_ge(sm["top_ready"], t + 1)
                A(tw[:, t, :], top[:, t, 0:4], ACT.Exp, bias=ntop[:, t:t + 1], accum_out=tsum[:, t:t + 1]).then_inc(sm["texp"], 1)
            act.wait_ge(sm["table_ready"], 1)

            def window(g, width):
                for k, wk in enumerate((wka, wkb)):
                    act.wait_ge(sm["gathered"], g * 2 + (k + 1))
                    A(xT[:, 4 * k:4 * k + 4, 0:width], wk[:, 0:4 * width].rearrange("p (n c) -> p n c", n=4), ACT.Copy).then_inc(sm["xt_ready"], 1)
                for j in range(W1C):
                    act.wait_ge(sm["g_clamped"], g * 4 + (j + 1))
                    A(sg[:, :, 0:width], gm[:, :, 0:width], ACT.Sigmoid, scale=1.702).then_inc(sm["sig_ready"], 1)
                act.wait_ge(sm["y_filled"], g + 1)
                for k in range(2):
                    A(ys[0:width, 512 * k:512 * k + 512], yb[k][0:width, :], ACT.Copy).then_inc(sm["ys_ready"], 1)

            with act.Fori(0, NE) as e:
                g0 = act.value_load(tab_i[0:1, bass.ds(e, 1)], min_val=0, max_val=2 * NE)
                cnt = act.value_load(tab_i[0:1, bass.ds(e + NE, 1)], min_val=0, max_val=S)
                with act.If(cnt > WIDE):
                    window(g0, WIDE)
                    window(g0 + 1, WIDE)
                with act.Else():
                    with act.If(cnt > NARROW):
                        window(g0, WIDE)
                    with act.Else():
                        window(g0, NARROW)
            for t in range(ST):
                act.wait_ge(sm["var_ready"], 2 * ST + t + 1)
                A(rstd[:, t:t + 1], mv[:, t, 1:2], ACT.Sqrt, bias=eps5).then_inc(sm["sd_ready"], 1)

        @block.vector
        def _(dve):
            V = nc.vector
            n_dve = [0]

            def link(ins):
                n_dve[0] += 1
                ins.then_inc(dve_step, 1)
                dve.wait_ge(dve_step, n_dve[0])

            def signal(ins, *sems):
                link(ins)
                for s in sems:
                    dve.sem_inc(s, 1)

            def bank(job):
                wait_fill(dve, job)
                return bk[BANK[job]]

            def layer_norm(k):
                for t in range(ST):
                    for q in range(2):
                        V.bn_stats(stats[:, t, q, :], h[:, t, 512 * q:512 * q + 512]).then_inc(dve_step, 1)
                        n_dve[0] += 1
                    dve.wait_ge(dve_step, n_dve[0])
                    V.bn_aggr(mv[:, t, :], stats[:, t, :, :].rearrange("p a b -> p (a b)")).then_inc(sm["var_ready"], 1)
                dve.wait_ge(ln_in[k], 16)
                for t in range(ST):
                    dve.wait_ge(sm["sd_ready"], ST * k + t + 1)
                    link(V.reciprocal(rstd[:, t:t + 1], rstd[:, t:t + 1]))
                    link(V.tensor_scalar(h[:, t, :], h[:, t, :], mv[:, t, 0:1], rstd[:, t:t + 1], ALU.subtract, ALU.mult))
                    link(V.tensor_tensor(h[:, t, :], h[:, t, :], lngb[:, 0, :], ALU.mult))
                    signal(V.tensor_tensor(h[:, t, :], h[:, t, :], lngb[:, 1, :], ALU.add), sm["h_ready"])
                dve.sem_inc(sm["ln_used"], 1)

            link(V.memset(small[:, :], 0.0))
            V.memset(eps5, 1e-5)
            V.memset(eps6, 1e-6)
            V.memset(relw[32:33, :], -1e30)
            signal(V.memset(convin[:, :, 0:KA - 1], 0.0), sm["pad_zero"])
            dve.wait_ge(x_in, 16)
            layer_norm(0)
            signal(V.memset(bv[:, :, 0:KB - 1], 0.0))
            dve.wait_ge(params_in, 64)
            dve.wait_ge(sm["bgate"], 1)
            link(V.tensor_tensor(bv[:, :, KB - 1:], bv[:, :, KB - 1:], bacc, ALU.mult))
            dve.wait_ge(sm["beta_ready"], 1)
            v42 = "p (t h) -> p t h"
            dtb = rowp[:, R_DT:R_DT + 4].rearrange("p (o h) -> p o h", o=1).broadcast_to([P, 2, 4])
            link(V.tensor_tensor(uu.rearrange(v42, t=2), uu.rearrange(v42, t=2), dtb, ALU.add))
            link(V.tensor_scalar(au, uu, -1.0, None, ALU.mult))
            signal(V.tensor_tensor(au, au, uu, ALU.max), sm["aa_ready"])
            dve.wait_ge(sm["expu"], 1)
            link(V.tensor_scalar(ss, yy, 2.0, None, ALU.add))
            link(V.reciprocal(ss, ss))
            link(V.tensor_tensor(ss, ss, yy, ALU.mult))
            link(V.tensor_tensor(s2, ss, ss, ALU.mult))
            link(V.tensor_scalar(po, s2, 1.0 / 17, 1.0 / 15, ALU.mult, ALU.add))
            for k in (13, 11, 9, 7, 5, 3, 1):
                link(V.tensor_tensor(po, po, s2, ALU.mult))
                link(V.tensor_scalar(po, po, 1.0 / k, None, ALU.add))
            link(V.scalar_tensor_tensor(po, po, 2.0, ss, ALU.mult, ALU.mult))
            link(V.scalar_tensor_tensor(po, uu, 0.0, po, ALU.max, ALU.add))
            eal = ealog.rearrange("p (o h) -> p o h", o=1).broadcast_to([P, 2, 4])
            signal(V.scalar_tensor_tensor(gg, po.rearrange(v42, t=2), -1.0, eal, ALU.mult, ALU.mult), sm["g_ready"])
            j = "gcol"
            signal(V.tensor_copy(gcs, bank(j)[:, 0:16].rearrange("p (k t h) -> p k t h", k=2, t=2)),
                   sm["gcs_ready"], drained[BANK[j]])
            strict = consts[:, C_STR:C_STR + P]
            for t in range(ST):
                b_ = bank(f"grow{t}")
                for hh in range(AH):
                    link(V.scalar_tensor_tensor(dt_[:, 4 * t + hh, :], b_[:, hh * P:(hh + 1) * P], gcs[:, 0, t, hh:hh + 1],
                                                strict, ALU.subtract, ALU.mult))
                signal(V.tensor_scalar(dt_[:, 4 * t:4 * t + 4, :], dt_[:, 4 * t:4 * t + 4, :], 0.0, None, ALU.min), sm["dmin"])
            dve.wait_ge(sm["egc_ready"], 1)
            link(V.tensor_tensor(bek, beta, egc[:, 0], ALU.mult))

            n_conv = [0]

            def conv_a(x_, k0, dstT):
                dve.wait_ge(sm["conv_in"], n_conv[0] + 1)
                for c in range(4):
                    w = chp[:, H_ACW + (k0 + c) * KA:H_ACW + (k0 + c + 1) * KA]
                    V.tensor_scalar(dstT[:, c, :], convin[:, k0 + c, 0:S], w[:, 0:1], None, ALU.mult).then_inc(dve_step, 1)
                n_dve[0] += 4
                for k in range(1, KA):
                    for c in range(4):
                        w = chp[:, H_ACW + (k0 + c) * KA:H_ACW + (k0 + c + 1) * KA]
                        dve.wait_ge(dve_step, n_dve[0] - 3)
                        V.scalar_tensor_tensor(dstT[:, c, :], convin[:, k0 + c, k:k + S], w[:, k:k + 1], dstT[:, c, :],
                                               ALU.mult, ALU.add).then_inc(dve_step, 1)
                        n_dve[0] += 1
                dve.wait_ge(dve_step, n_dve[0])
                n_conv[0] += 1
                dve.sem_inc(sm["conv_out"], 1)

            def l2(dstT, n, scale):
                dve.wait_ge(sm["l2_sd"], n)
                link(V.reciprocal(sq, sq))
                signal(V.scalar_tensor_tensor(dstT, dstT, scale, sq, ALU.mult, ALU.mult), sm["l2_ready"])

            conv_a("K", 4, kT)
            conv_a("Q", 0, qT)
            l2(kT, 1, 1.0)
            dve.wait_ge(sm["dexp"], 1)
            incl = consts[:, C_TRI:C_TRI + P].rearrange("p (o c) -> p o c", o=1).broadcast_to([P, 8, P])
            link(V.tensor_tensor(dt_, dt_, incl, ALU.mult))
            conv_a("V", 8, vT)
            l2(qT, 2, 128 ** -0.5)
            for t in range(ST):
                j = f"kk{t}"
                link(V.tensor_tensor(at[:, 4 * t:4 * t + 4, :], bank(j).rearrange("p (n c) -> p n c", n=4), brow[:, 4 * t:4 * t + 4, :], ALU.mult))
                dve.sem_inc(drained[BANK[j]], 1)
                signal(V.tensor_tensor(at[:, 4 * t:4 * t + 4, :], at[:, 4 * t:4 * t + 4, :], dt_[:, 4 * t:4 * t + 4, :], ALU.mult), sm["at_ready"])
            m0 = consts[:, C_LVL:C_LVL + P].rearrange("p (o c) -> p o c", o=1).broadcast_to([P, 8, P])
            idb = ident.rearrange("p (o c) -> p o c", o=1).broadcast_to([P, 8, P])
            link(V.tensor_tensor(um, at, m0, ALU.mult))
            signal(V.tensor_tensor(um, idb, um, ALU.subtract), sm["u_ready"])
            for t in range(ST):
                j = f"ktok{t}"
                b_ = bank(j).rearrange("p (n c) -> p n c", n=4)
                V.tensor_tensor(kbt[:, 4 * t:4 * t + 4, :], b_, bek[:, t, :].rearrange("p (h o) -> p h o", o=1).broadcast_to([P, 4, P]), ALU.mult)
                signal(V.tensor_tensor(kdt[:, 4 * t:4 * t + 4, :], b_, egc[:, 1, t, :].rearrange("p (h o) -> p h o", o=1).broadcast_to([P, 4, P]), ALU.mult),
                       drained[BANK[j]], sm["kb_ready"])
            for t in range(ST):
                j = f"qk{t}"
                signal(V.tensor_tensor(dt_[:, 4 * t:4 * t + 4, :], bank(j).rearrange("p (n c) -> p n c", n=4), dt_[:, 4 * t:4 * t + 4, :], ALU.mult),
                       drained[BANK[j]], sm["qk_ready"])
            for t in range(ST):
                signal(V.tensor_tensor(qT[:, :, t * P:(t + 1) * P], qT[:, :, t * P:(t + 1) * P], eg[:, 4 * t:4 * t + 4, :], ALU.mult), sm["qd_ready"])
            for t in range(ST):
                j = f"vtok{t}"
                signal(V.tensor_tensor(vbt[:, 4 * t:4 * t + 4, :], bank(j).rearrange("p (n c) -> p n c", n=4),
                                       beta[:, t, :].rearrange("p (h o) -> p h o", o=1).broadcast_to([P, 4, P]), ALU.mult),
                       drained[BANK[j]], sm["vb_ready"])
            for t in range(ST):
                j = f"trT{t}"
                signal(V.tensor_copy(tm[:, 4 * t:4 * t + 4, :], bank(j).rearrange("p (n c) -> p n c", n=4)), drained[BANK[j]], sm["t_ready"])

            taps = [(k, c) for k in range(KB) for c in range(NB)]
            sem_conv = sm["bconv"]
            done = [0]

            def conv_b(count):
                for k, c in taps[done[0]:done[0] + count]:
                    w = chp[:, H_BW + c * KB + k:H_BW + c * KB + k + 1]
                    if k == 0:
                        V.tensor_scalar(bacc[:, c, :], bv[:, c, 0:S], w, chp[:, H_BB + c:H_BB + c + 1], ALU.mult, ALU.add).then_inc(sem_conv, 1)
                    else:
                        dve.wait_ge(sem_conv, done[0] - 3)
                        V.scalar_tensor_tensor(bacc[:, c, :], bv[:, c, k:k + S], w, bacc[:, c, :], ALU.mult, ALU.add).then_inc(sem_conv, 1)
                    done[0] += 1

            def level(job, buf, ready):
                t = int(job[3])
                v = buf[:, 4 * t:4 * t + 4, :]
                signal(V.tensor_tensor(v, v, bank(job).rearrange("p (n c) -> p n c", n=4), ALU.subtract), drained[BANK[job]], sm[ready])

            def scores(n):
                heads, keys = (4, 128) if n < 2 else (2, 256)
                job = f"sc{n}"
                if n >= 2:
                    wait_fill(dve, f"pt{n - 2}")
                b_ = bank(job)[:, 0:heads * keys].rearrange("p (n c) -> p n c", n=heads)
                s_ = ssc[:, n % 2, :].rearrange("p (n c) -> p n c", n=heads)
                h0 = 4 * n if n < 2 else 2 * (n - 2)
                if n == 0:
                    dve.wait_ge(rel_in, 16)
                signal(V.scalar_tensor_tensor(s_, b_, HD ** -0.5, bias[:, h0:h0 + heads, 256 - keys:256], ALU.mult, ALU.add), drained[BANK[job]])
                link(V.tensor_reduce(mxx[:, n, 0:heads], s_, AX.X, ALU.max))
                link(V.tensor_tensor(mxx[:, n, 0:heads], mxx[:, n, 0:heads], rowp[:, R_SINK + h0:R_SINK + h0 + heads], ALU.max))
                signal(V.tensor_scalar(mxx[:, n, 0:heads], mxx[:, n, 0:heads], -1.0, None, ALU.mult), sm["ssc_ready"])
                conv_b(8)
                dve.wait_ge(sm["pexp"], n + 1)
                link(V.tensor_tensor(smx[:, n, 0:heads], smx[:, n, 0:heads], esk[:, n, 0:heads], ALU.add))
                link(V.reciprocal(smx[:, n, 0:heads], smx[:, n, 0:heads]))
                signal(V.tensor_tensor(s_, s_, smx[:, n, 0:heads].rearrange("p (h o) -> p h o", o=1).broadcast_to([P, heads, keys]), ALU.mult), sm["pnorm"])

            def state(n):
                job = f"dS{n}"
                t, r = n // 2, n % 2
                if n == 0:
                    signal(V.tensor_copy(st, bank(job).rearrange("p (n c) -> p n c", n=4)), drained[BANK[job]], sm["st_ready"])
                    return
                for hh in range(AH):
                    ins = V.scalar_tensor_tensor(st[:, hh, :], st[:, hh, :], eg[:, 4 * t + hh, 64 * r + 63:64 * r + 64],
                                                 bank(job)[:, hh * P:(hh + 1) * P], ALU.mult, ALU.add)
                signal(ins, drained[BANK[job]], sm["st_ready"])

            for job in JOBS[JOBS.index("lp10"):JOBS.index("yB0")]:
                if job[:2] == "lt":
                    level(job, tm, "t_ready")
                elif job[:2] == "lu":
                    level(job, um, "u_ready")
                elif job[:5] == "projG":
                    conv_b(12)
                elif job[:2] == "sc":
                    scores(int(job[2]))
                elif job[:2] == "dS":
                    state(int(job[2]))
                elif job == "bmean":
                    conv_b(len(taps))
                    dve.wait_ge(sem_conv, len(taps))
                    dve.sem_inc(sm["conv_out"], 1)
                    b_ = bank(job)[:, 0:256].rearrange("p (o c) -> p o c", o=1).broadcast_to([P, 4, 256])
                    signal(V.tensor_tensor(bacc, bacc, b_, ALU.subtract), drained[BANK[job]], sm["bcent"])
                elif job == "bvar":
                    dve.wait_ge(sm["bsd"], 1)
                    link(V.reciprocal(tmpb, tmpb))
                    signal(V.tensor_tensor(bacc, bacc, tmpb.rearrange("p (o c) -> p o c", o=1).broadcast_to([P, 4, 256]), ALU.mult), sm["bnorm"])

            def merge(br, b, q):
                job = f"y{br}{q}"
                g_ = gates[:, 8 * b + 2 * q:8 * b + 2 * q + 2, :]
                b_ = bank(job).rearrange("p (n c) -> p n c", n=2)
                dst = mxT[:, 2 * q:2 * q + 2, :]
                if br == "B":
                    signal(V.tensor_tensor(dst, b_, g_, ALU.mult), drained[BANK[job]])
                else:
                    signal(V.tensor_tensor(g_, b_, g_, ALU.mult), drained[BANK[job]])
                    signal(V.tensor_tensor(dst, dst, g_, ALU.add), *([sm["mx_ready"]] if br == "A" else []))

            for q in range(4):
                merge("B", 1, q)
            dve.wait_ge(sm["rms_sd"], 1)
            oa4 = oaT.rearrange("p a b -> p (a b)").rearrange("p (n c) -> p n c", n=4)
            link(V.reciprocal(sq, sq))
            link(V.tensor_tensor(oa4, oa4, sq, ALU.mult))
            signal(V.scalar_tensor_tensor(oa4, oa4, chp[:, H_AN:H_AN + 1], az, ALU.mult, ALU.mult), sm["oa_ready"], sm["mixer_done"])
            for q in range(4):
                merge("C", 2, q)
            for q in range(4):
                merge("A", 0, q)
            for hf in range(2):
                for t in range(ST):
                    job = f"mix{t}{hf}"
                    v = h[:, t, 512 * hf:512 * hf + 512]
                    signal(V.scalar_tensor_tensor(v, v, ALPHA, bank(job), ALU.mult, ALU.add), drained[BANK[job]])
            layer_norm(1)
            dve.wait_ge(wr_in, 48)
            V.memset(ys, 0.0)
            signal(V.memset(ptw, 0.0))
            dve.sem_inc(sm["ys_ready"], 2)
            dve.sem_inc(sm["ptw_ready"], 1)
            brt = rowp[:, R_BR:R_BR + NE].rearrange("p (o e) -> p o e", o=1).broadcast_to([P, 2, NE])
            j = "router"
            signal(V.tensor_tensor(lg, bank(j)[:, 0:2 * NE].rearrange("p (t e) -> p t e", t=2), brt, ALU.add), drained[BANK[j]])
            for t in range(ST):
                link(V.max(top[:, t, :], lg[:, t, :]))
                link(V.max_index(idx[:, t, :], top[:, t, :], lg[:, t, :]))
                link(V.tensor_copy(idf[:, t, :], idx[:, t, :]))
                signal(V.tensor_scalar(ntop[:, t:t + 1], top[:, t, 0:1], -1.0, None, ALU.mult), sm["top_ready"])
            io = consts[:, C_IOTA0:C_IOTA0 + NE]
            for t in range(ST):
                link(V.tensor_scalar(mask[:, t, :], io, idf[:, t, 0:1], None, ALU.is_equal))
                for k in range(1, 4):
                    link(V.scalar_tensor_tensor(mask[:, t, :], io, idf[:, t, k:k + 1], mask[:, t, :], ALU.is_equal, ALU.add))
            dve.sem_inc(sm["mask_ready"], 1)
            for t in range(ST):
                dve.wait_ge(sm["texp"], t + 1)
                link(V.reciprocal(tsum[:, t:t + 1], tsum[:, t:t + 1]))
                link(V.tensor_scalar(tw[:, t, :], tw[:, t, :], tsum[:, t:t + 1], None, ALU.mult))
                link(V.tensor_scalar(comb[:, t, :], io, idf[:, t, 0:1], tw[:, t, 0:1], ALU.is_equal, ALU.mult))
                for k in range(1, 4):
                    link(V.tensor_scalar(oneh[:, t, :], io, idf[:, t, k:k + 1], tw[:, t, k:k + 1], ALU.is_equal, ALU.mult))
                    link(V.tensor_tensor(comb[:, t, :], comb[:, t, :], oneh[:, t, :], ALU.add))
            dve.sem_inc(sm["comb_ready"], 1)
            j = "rank"
            link(V.scalar_tensor_tensor(rk[:, 0], bank(j)[:, 0:2 * NE].rearrange("p (t e) -> p t e", t=2), 1.0, mask, ALU.add, ALU.mult))
            dve.sem_inc(drained[BANK[j]], 1)
            link(V.tensor_scalar(rk[:, 1], rk[:, 0], float(WIDE), None, ALU.subtract))
            j = "count"
            link(V.tensor_copy(tabf[:, 1, :], bank(j)[0:1, 0:NE]))
            dve.sem_inc(drained[BANK[j]], 1)
            link(V.tensor_copy(tab_i[0:1, NE:2 * NE], tabf[:, 1, :]))
            link(V.tensor_scalar(tabf[:, 2, :], tabf[:, 1, :], float(WIDE), 1.0, ALU.is_gt, ALU.add))
            link(V.memset(tabf[:, 3, :], 1.0))
            link(V.tensor_tensor_scan(tabf[:, 0, :], tabf[:, 3, :], tabf[:, 2, :], 0.0, ALU.mult, ALU.add))
            link(V.tensor_copy(tab_i[0:1, 3 * NE:3 * NE + 1], tabf[:, 0, NE - 1:NE]))
            link(V.tensor_tensor(tabf[:, 0, :], tabf[:, 0, :], tabf[:, 2, :], ALU.subtract))
            link(V.tensor_copy(tab_i[0:1, 0:NE], tabf[:, 0, :]))
            link(V.tensor_scalar(tabf[:, 0, :], tabf[:, 0, :], -1.0, 0.0, ALU.add, ALU.max))
            link(V.tensor_copy(tab_i[0:1, 2 * NE:3 * NE], tabf[:, 0, :]))
            dve.sem_inc(sm["table_ready"], 1)
            j = "combT"
            signal(V.tensor_copy(combTs, bank(j)[0:NE, 0:256].rearrange("p (t c) -> p t c", t=2)), drained[BANK[j]], sm["combT_ready"])
            io1 = consts[:, C_IOTA1:C_IOTA1 + P]

            def window(e, g, width, part):
                dve.wait_ge(sm["pt_filled"], g + 1)
                for t in range(ST):
                    V.tensor_scalar(pg[:, t, :], io1, rk[:, part, t, bass.ds(e, 1)], None, ALU.is_equal)
                    ins = V.tensor_scalar(pw[:, t, :], io1, rk[:, part, t, bass.ds(e, 1)], comb[:, t, bass.ds(e, 1)], ALU.is_equal, ALU.mult)
                ins.then_inc(sm["p_ready"], 1)
                dve.wait_ge(sm["pt_filled"], g + 2)
                V.tensor_copy(ptw, wka[:, 0:256].rearrange("p (t c) -> p t c", t=2)).then_inc(sm["ptw_ready"], 1)
                for j in range(W1C):
                    wk = (wkb, wka)[j % 2]
                    dve.wait_ge(sm["h_filled"], g * 4 + (j + 1))
                    bb = b1s[:, bass.ds(e, 1), 4 * j:4 * j + 4].rearrange("p o (k z) -> p (o k) z", z=1).broadcast_to([P, 4, width])
                    V.tensor_tensor(hb[:, :, 0:width], wk[:, 0:4 * width].rearrange("p (n c) -> p n c", n=4), bb, ALU.add).then_inc(sm["h_read"], 1)
                    dve.wait_ge(sm["h_read"], g * 4 + (j + 1))
                    V.tensor_scalar(gm[:, :, 0:width], hb[:, 0:2, 0:width], 7.0, None, ALU.min).then_inc(sm["g_clamped"], 1)
                    V.tensor_scalar(ln_[:, :, 0:width], hb[:, 2:4, 0:width], 7.0, -7.0, ALU.min, ALU.max)
                    dve.wait_ge(sm["sig_ready"], g * 4 + (j + 1))
                    V.tensor_tensor(gs[:, :, 0:width], gm[:, :, 0:width], sg[:, :, 0:width], ALU.mult).then_inc(sm["swish_ready"], 1)
                    dve.wait_ge(sm["swish_ready"], g * 4 + (j + 1))
                    V.scalar_tensor_tensor(actT[:, 2 * j:2 * j + 2, 0:width], ln_[:, :, 0:width], 1.0, gs[:, :, 0:width], ALU.add, ALU.mult).then_inc(sm["act_ready"], 1)

            with dve.Fori(0, NE) as e:
                g0 = dve.value_load(tab_i[0:1, bass.ds(e, 1)], min_val=0, max_val=2 * NE)
                cnt = dve.value_load(tab_i[0:1, bass.ds(e + NE, 1)], min_val=0, max_val=S)
                with dve.If(cnt > WIDE):
                    window(e, g0, WIDE, 0)
                    window(e, g0 + 1, WIDE, 1)
                with dve.Else():
                    with dve.If(cnt > NARROW):
                        window(e, g0, WIDE, 0)
                    with dve.Else():
                        window(e, g0, NARROW, 0)
            dve.wait_ge(sm["all_scattered"], 1)
            for t in range(ST):
                for k in range(2):
                    v = h[:, t, 512 * k:512 * k + 512]
                    link(V.scalar_tensor_tensor(v, v, ALPHA, acc[t][k][:, :], ALU.mult, ALU.add))
            layer_norm(2)

        @block.tensor
        def _(pe):
            mm = nc.tensor.matmul

            def tr(o, i):
                return nc.tensor.transpose(o, i, ident)

            def open_bank(job):
                if FILL[job] > 1:
                    pe.wait_ge(drained[BANK[job]], FILL[job] - 1)
                return bk[BANK[job]]

            def close(job, ins):
                ins.then_inc(filled[BANK[job]], 1)

            seen = {}

            def tile(name):
                n = TILE[name]
                s = n % W1C
                if name not in seen:
                    parts = {"M": 2, "WC": 2, "C": 16}
                    total = sum(parts.get(TILES[m], 1) for m in range(s, n + 1, W1C))
                    pe.wait_ge(tile_in[s], 16 * total)
                    seen[name] = True
                return w1s[:, s, :]

            tile_total = [sum({"M": 2, "WC": 2, "C": 16}.get(TILES[m], 1) for m in range(s, NT, W1C)) for s in range(W1C)]

            def proj(job, name, cols):
                w = tile(name).rearrange("p (k c) -> p k c", k=DC)
                b = open_bank(job)
                for n, c in enumerate(cols):
                    for k in range(DC):
                        ins = mm(b[:, n * S:(n + 1) * S], lhsT=w[:, k, c:c + P], rhs=hT[:, k, :], start=k == 0, stop=k == DC - 1)
                close(job, ins)

            srcT = {"K": kT, "Q": qT}
            level_n = {}
            for job in JOBS:
                if job[:2] == "hT" or job[:3] == "h1T":
                    t, hh = int(job[-2]), int(job[-1])
                    pe.wait_ge(params_in, 64)
                    pe.wait_ge(sm["h_ready"], t + 1 + (ST if job[1] == "1" else 0))
                    b = open_bank(job)
                    for k in range(4):
                        ins = tr(b[:, k * P:(k + 1) * P], h[:, t, (4 * hh + k) * P:(4 * hh + k + 1) * P])
                    close(job, ins)
                elif job == "relvec":
                    pe.wait_ge(sm["pad_zero"], 1)
                    close(job, mm(open_bank(job)[0:8, 0:384], lhsT=relw[:, :], rhs=consts[0:33, C_OH:C_OH + 384], start=True, stop=True))
                    pe.wait_ge(sm["hT_ready"], 4)
                elif job[:4] == "proj":
                    x_ = job[4:-1]
                    name = {"BV": "BV", "BG": "BG", "K": "K", "Q": "Q", "V": "V", "Z": "Z", "C": "C"}.get(x_, x_)
                    c0 = 256 * int(job[-1])
                    proj(job, name, (c0, c0 + P))
                elif job == "ab":
                    w = tile("M").rearrange("p (k c) -> p k c", k=DC)
                    b = open_bank(job)
                    for t in range(ST):
                        for k in range(DC):
                            ins = mm(b[:, 8 * t:8 * t + 8], lhsT=hT[:, k, t * P:(t + 1) * P], rhs=w[:, k, 0:8], start=k == 0, stop=k == DC - 1)
                    close(job, ins)
                elif job == "CK":
                    proj(job, "M", (P,))
                elif job == "CV":
                    w = tile("M").rearrange("p (k c) -> p k c", k=DC)
                    b = open_bank(job)
                    for t in range(ST):
                        for k in range(DC):
                            ins = mm(b[:, P * t:P * t + P], lhsT=hT[:, k, t * P:(t + 1) * P], rhs=w[:, k, 2 * P:3 * P], start=k == 0, stop=k == DC - 1)
                    close(job, ins)
                elif job == "gcol":
                    pe.wait_ge(sm["g_ready"], 1)
                    b = open_bank(job)
                    for k, m in enumerate((C_TRI, C_SUF)):
                        for t in range(ST):
                            ins = mm(b[:, 8 * k + 4 * t:8 * k + 4 * t + 4], lhsT=consts[:, m:m + P], rhs=gg[:, t, :], start=True, stop=True)
                    close(job, ins)
                elif job[:4] in ("grow", "brow"):
                    t = int(job[4])
                    b = open_bank(job)
                    src, m = (gg, C_TRI) if job[0] == "g" else (beta, C_ID)
                    for hh in range(AH):
                        ins = mm(b[:, hh * P:(hh + 1) * P], lhsT=src[:, t, hh:hh + 1].broadcast_to([P, P]), rhs=consts[:, m:m + P], start=True, stop=True)
                    close(job, ins)
                elif job[:2] == "ss":
                    hh = int(job[3])
                    pe.wait_ge(sm["sq_ready"], 1 if job[2] == "K" else 2)
                    b = open_bank(job)
                    close(job, mm(b[:, :], lhsT=ones, rhs=sq[:, 2 * hh:2 * hh + 2, :], start=True, stop=True))
                elif job[:2] in ("kk", "qk"):
                    t = int(job[2])
                    pe.wait_ge(sm["l2_ready"], 1 if job[0] == "k" else 2)
                    b = open_bank(job)
                    for hh in range(AH):
                        tt = slice(t * P, (t + 1) * P)
                        ins = mm(b[:, hh * P:(hh + 1) * P], lhsT=kT[:, hh, tt], rhs=(kT if job[0] == "k" else qT)[:, hh, tt], start=True, stop=True)
                    close(job, ins)
                elif job[1:4] == "tok":
                    t = int(job[4])
                    if job[0] == "v":
                        pe.wait_ge(sm["silu_done"], 3)
                    b = open_bank(job)
                    for hh in range(AH):
                        ins = tr(b[:, hh * P:(hh + 1) * P], (kT if job[0] == "k" else vT)[:, hh, t * P:(t + 1) * P])
                    close(job, ins)
                elif job[:3] == "trT":
                    t = int(job[3])
                    pe.wait_ge(sm["u_ready"], 1)
                    b = open_bank(job)
                    for hh in range(AH):
                        ins = tr(b[:, hh * P:(hh + 1) * P], um[:, 4 * t + hh, :])
                    close(job, ins)
                elif job[:2] in ("lp", "lt", "lu"):
                    l, t = int(job[2]), int(job[3])
                    if job[1] == "p":
                        pe.wait_ge(sm["mst_ready"], l)
                        pe.wait_ge(sm["t_ready"], 2 * (l - 1) + t + 1)
                        lhs, rhs = mst, tm
                    else:
                        pe.wait_ge(sm["p1_ready"], 2 * (l - 1) + t + 1)
                        pe.wait_ge(sm["u_ready"], 1 + 2 * (l - 1))
                        lhs, rhs = (um, p1) if job[1] == "t" else (p1, um)
                    b = open_bank(job)
                    for hh in range(AH):
                        ins = mm(b[:, hh * P:(hh + 1) * P], lhsT=lhs[:, 4 * t + hh, :], rhs=rhs[:, 4 * t + hh, :], start=True, stop=True)
                    close(job, ins)
                elif job == "bmean":
                    pe.wait_ge(sm["conv_out"], 4)
                    b = open_bank(job)
                    for c in range(NB):
                        ins = mm(b[:, 0:S], lhsT=inv512[:, :], rhs=bacc[:, c, :], start=c == 0, stop=c == NB - 1)
                    close(job, ins)
                elif job == "bvar":
                    pe.wait_ge(sm["bsq"], 1)
                    b = open_bank(job)
                    for c in range(NB):
                        ins = mm(b[:, 0:S], lhsT=inv512[:, :], rhs=bv[:, c, 0:S], start=c == 0, stop=c == NB - 1)
                    close(job, ins)
                elif job[:2] == "wT":
                    t = int(job[2])
                    pe.wait_ge(sm["u_ready"], 1 + 2 * (LEVELS - 1))
                    pe.wait_ge(sm["kb_ready"], 2)
                    b = open_bank(job)
                    for hh in range(AH):
                        ins = mm(b[:, hh * P:(hh + 1) * P], lhsT=kbt[:, 4 * t + hh, :], rhs=um[:, 4 * t + hh, :], start=True, stop=True)
                    close(job, ins)
                elif job[:2] == "vn":
                    n = int(job[2])
                    t, r = n // 2, 64 * (n % 2)
                    pe.wait_ge(sm["wT_ready"], t + 1)
                    pe.wait_ge(sm["vb_ready"], 2)
                    if n:
                        pe.wait_ge(sm["st_ready"], n)
                    b = open_bank(job)
                    for hh in range(AH):
                        o = b[r:r + 64, hh * P:(hh + 1) * P]
                        ins = mm(o, lhsT=um[r:r + 64, 4 * t + hh, r:r + 64], rhs=vbt[r:r + 64, 4 * t + hh, :], start=True, stop=n == 0)
                        if n:
                            ins = mm(o, lhsT=wT[:, 4 * t + hh, r:r + 64], rhs=st[:, hh, :], start=False, stop=True)
                    close(job, ins)
                elif job[:2] == "oT":
                    n = int(job[2])
                    t, r = n // 2, 64 * (n % 2)
                    pe.wait_ge(sm["vn_ready"], n + 1)
                    pe.wait_ge(sm["qk_ready"], 2)
                    pe.wait_ge(sm["qd_ready"], 2)
                    b = open_bank(job)
                    for hh in range(AH):
                        o = b[:, hh * CH:(hh + 1) * CH]
                        ins = mm(o, lhsT=vn[r:r + 64, hh, :], rhs=dt_[r:r + 64, 4 * t + hh, r:r + 64], start=True, stop=n == 0)
                        if n:
                            ins = mm(o, lhsT=st[:, hh, :], rhs=qT[:, hh, n * CH:(n + 1) * CH], start=False, stop=True)
                    close(job, ins)
                elif job[:2] == "dS":
                    n = int(job[2])
                    t, r = n // 2, 64 * (n % 2)
                    b = open_bank(job)
                    for hh in range(AH):
                        ins = mm(b[:, hh * P:(hh + 1) * P], lhsT=kdt[r:r + 64, 4 * t + hh, :], rhs=vn[r:r + 64, hh, :], start=True, stop=True)
                    close(job, ins)
                elif job[:2] == "sc":
                    n = int(job[2])
                    pe.wait_ge(sm["cq_ready"], 1)
                    pe.wait_ge(sm["cv_ready"], 1)
                    g, j0, nh, q0 = (n, 0, 4, 0) if n < 2 else ((n - 2) // 2, 2 * (n % 2), 2, P)
                    keys = P if n < 2 else 2 * P
                    b = open_bank(job)
                    for k in range(nh):
                        ins = mm(b[:, k * keys:(k + 1) * keys], lhsT=cq[64 * g:64 * g + 64, j0 + k, q0:q0 + P],
                                 rhs=ck[64 * g:64 * g + 64, 0:keys], start=True, stop=True)
                    close(job, ins)
                elif job[:2] == "pt":
                    n = int(job[2])
                    pe.wait_ge(sm["pnorm"], n + 1)
                    b = open_bank(job)
                    for k in range(4):
                        ins = tr(b[:, k * P:(k + 1) * P], ssc[:, n % 2, k * P:(k + 1) * P])
                    close(job, ins)
                elif job[:2] == "pv":
                    n = int(job[2])
                    g, j0, nh, q0 = (n, 0, 4, 0) if n < 2 else ((n - 2) // 2, 2 * (n % 2), 2, P)
                    pe.wait_ge(sm["pt_ready"], n + 1)
                    b = open_bank(job)
                    nk = 1 if n < 2 else 2
                    for k in range(nh):
                        for kb in range(nk):
                            ins = mm(b[64 * g:64 * g + 64, k * P:(k + 1) * P], lhsT=cv[:, kb, 64 * g:64 * g + 64],
                                     rhs=pts[:, n % 2, (k * nk + kb) * P:(k * nk + kb + 1) * P], start=kb == 0, stop=kb == nk - 1)
                    close(job, ins)
                elif job[:3] == "rms":
                    hh = int(job[3])
                    pe.wait_ge(sm["osq"], 1)
                    b = open_bank(job)
                    close(job, mm(b[:, :], lhsT=inv128[:, :], rhs=sq[:, 2 * hh:2 * hh + 2, :], start=True, stop=True))
                elif job[0] == "y":
                    q = int(job[2])
                    src, ready, cnt_ = {"B": (bacc, "bsilu", 1), "C": (ocT, "oc_ready", 6), "A": (oaT.rearrange("p a b -> p (a b)").rearrange("p (n c) -> p n c", n=4), "oa_ready", 1)}[job[1]]
                    pe.wait_ge(sm[ready], cnt_)
                    w = tile("W" + job[1]).rearrange("p (k c) -> p k c", k=4)
                    b = open_bank(job)
                    for n in range(2):
                        c = (2 * q + n) * P
                        for k in range(4):
                            ins = mm(b[:, n * S:(n + 1) * S], lhsT=w[:, k, c:c + P], rhs=src[:, k, :], start=k == 0, stop=k == 3)
                    close(job, ins)
                elif job[:3] == "mix":
                    t, hf = int(job[3]), int(job[4])
                    pe.wait_ge(sm["mx_ready"], 4)
                    w = tile(f"WO{hf}").rearrange("p (k c) -> p k c", k=DC)
                    b = open_bank(job)
                    for k in range(DC):
                        ins = mm(b[:, :], lhsT=mxT[:, k, t * P:(t + 1) * P], rhs=w[:, k, :], start=k == 0, stop=k == DC - 1)
                    close(job, ins)
                elif job == "router":
                    pe.wait_ge(sm["h1T_ready"], 4)
                    pe.wait_ge(wr_in, 48)
                    b = open_bank(job)
                    for t in range(ST):
                        for k in range(DC):
                            ins = mm(b[:, NE * t:NE * (t + 1)], lhsT=hT[:, k, t * P:(t + 1) * P], rhs=wr[:, k, :], start=k == 0, stop=k == DC - 1)
                    close(job, ins)
                elif job == "rank":
                    pe.wait_ge(sm["mask_ready"], 1)
                    b = open_bank(job)
                    tri = consts[:, C_TRI128:C_TRI128 + P]
                    mm(b[:, 0:NE], lhsT=tri, rhs=mask[:, 0, :], start=True, stop=True)
                    mm(b[:, NE:2 * NE], lhsT=ones, rhs=mask[:, 0, :], start=True, stop=False)
                    close(job, mm(b[:, NE:2 * NE], lhsT=tri, rhs=mask[:, 1, :], start=False, stop=True))
                elif job == "count":
                    b = open_bank(job)
                    mm(b[:, 0:NE], lhsT=ones, rhs=mask[:, 0, :], start=True, stop=False)
                    close(job, mm(b[:, 0:NE], lhsT=ones, rhs=mask[:, 1, :], start=False, stop=True))
                elif job == "combT":
                    pe.wait_ge(sm["comb_ready"], 1)
                    b = open_bank(job)
                    for t in range(ST):
                        ins = tr(b[0:NE, t * P:(t + 1) * P], comb[:, t, :])
                    close(job, ins)
                else:
                    raise ValueError(job)
            pe.wait_ge(sm["combT_ready"], 1)
            for b in range(8):
                last = [n for n in JOBS if BANK[n] == b][-1]
                pe.wait_ge(drained[b], FILL[last])
            for t in range(ST):
                for k in range(2):
                    ins = mm(acc[t][k][:, :], lhsT=combTs[:, t, :], rhs=b2s[:, 512 * k:512 * k + 512], start=True, stop=False, skip_group_check=True)
            ins.then_inc(sm["pt_filled"], 1)
            pe.wait_ge(sm["pt_filled"], 1)
            pe.wait_ge(sm["table_ready"], 1)
            pe.sem_inc(sm["xt_ready"], 2)
            pe.sem_inc(sm["act_ready"], 4)

            def scatter(last=False):
                for t in range(ST):
                    for k in range(2):
                        ins = mm(acc[t][k][:, :], lhsT=ptw[:, t, :], rhs=ys[:, 512 * k:512 * k + 512], start=False, stop=last, skip_group_check=True)
                return ins

            def window(e, g, width, free=True):
                pe.wait_ge(sm["p_ready"], g + 1)
                pe.wait_ge(sm["act_ready"], g * 4 + 4)
                for b, wk in enumerate((wka, wkb)):
                    for k in range(4):
                        for t in range(ST):
                            ins = mm(wk[:, k * width:(k + 1) * width], lhsT=h[:, t, (4 * b + k) * P:(4 * b + k + 1) * P], rhs=pg[:, t, 0:width],
                                     start=t == 0, stop=t == ST - 1)
                    ins.then_inc(sm["gathered"], 1)
                pe.wait_ge(sm["ys_ready"], g * 2 + 2)
                pe.wait_ge(sm["ptw_ready"], g + 1)
                scatter()
                pe.wait_ge(sm["xt_ready"], g * 2 + 3)
                for t in range(ST):
                    ins = tr(wka[:, t * P:(t + 1) * P], pw[:, t, :])
                ins.then_inc(sm["pt_filled"], 1)
                pe.wait_ge(sm["xt_ready"], g * 2 + 4)
                for j in range(W1C):
                    s = (NT + j) % W1C
                    pe.wait_ge(tile_in[s], e * 32 + (16 * tile_total[s] + 32))
                    wk = (wkb, wka)[j % 2]
                    if j == 1:
                        pe.wait_ge(sm["ptw_ready"], g + 2)
                    if j >= 2:
                        pe.wait_ge(sm["h_read"], g * 4 + (j - 1))
                    w = w1s[:, s, :].rearrange("p (k c) -> p k c", k=DC)
                    for n in range(4):
                        for k in range(DC):
                            ins = mm(wk[:, n * width:(n + 1) * width], lhsT=w[:, k, n * P:(n + 1) * P], rhs=xT[:, k, 0:width],
                                     start=k == 0, stop=k == DC - 1)
                    ins.then_inc(sm["h_filled"], 1)
                for f in range(8):
                    q = f // 4
                    if f % 4 == 0:
                        pe.wait_ge(w2_in[q], e * 16 + 16)
                    if f % 2 == 0:
                        pe.wait_ge(sm["act_ready"], g * 4 + (f // 2 + 5))
                    w = w2s[:, q, :].rearrange("p (k c) -> p k c", k=4)
                    for k in range(2):
                        ins = mm(yb[k][0:width, :], lhsT=actT[:, f, 0:width], rhs=w[:, f % 4, 512 * k:512 * k + 512], start=f == 0, stop=f == 7,
                                 skip_group_check=True)
                ins.then_inc(sm["y_filled"], 1)

            with pe.Fori(0, NE) as e:
                g0 = pe.value_load(tab_i[0:1, bass.ds(e, 1)], min_val=0, max_val=2 * NE)
                cnt = pe.value_load(tab_i[0:1, bass.ds(e + NE, 1)], min_val=0, max_val=S)
                with pe.If(cnt > WIDE):
                    window(e, g0, WIDE)
                    window(e, g0 + 1, WIDE)
                with pe.Else():
                    with pe.If(cnt > NARROW):
                        window(e, g0, WIDE)
                    with pe.Else():
                        window(e, g0, NARROW)
            windows = pe.value_load(tab_i[0:1, 3 * NE:3 * NE + 1], min_val=NE, max_val=2 * NE)
            pe.wait_ge(sm["ys_ready"], windows * 2 + 2)
            pe.wait_ge(sm["ptw_ready"], windows + 1)
            scatter(True).then_inc(sm["all_scattered"], 1)



def kernel(**inputs):
    import numpy as _np
    import concourse.bacc as _bacc
    from concourse import mybir as _mybir
    from concourse.bass_utils import run_bass_kernel_spmd as _run

    a = {k: _np.asarray(v) for k, v in inputs.items()}
    chan = _np.concatenate([
        a["a_conv_w"][0].reshape(KA, 12, P).transpose(2, 1, 0).reshape(P, 12 * KA),
        a["b_dw_w"][0].reshape(KB, NB, P).transpose(2, 1, 0).reshape(P, NB * KB),
        a["b_dw_b"][0].reshape(NB, P).T, a["b_ln_g"][0].reshape(NB, P).T, a["b_ln_b"][0].reshape(NB, P).T,
        a["a_norm_g"][0].reshape(P, 1)], axis=1)
    b1 = a["b1"][0].reshape(NE, 2, W1C, 2, P).transpose(4, 0, 2, 1, 3).reshape(P, NE, 16)
    arrays = {
        "x": a["x"][0],
        "lnp": _np.stack([a["ln_in_g"], a["ln_in_b"], a["ln1_g"][0], a["ln1_b"][0], a["ln2_g"][0], a["ln2_b"][0]]),
        "rel": a["rel_bias"], "w_in": a["w_in"][0], "wa": a["w_a_out"][0], "wb": a["w_b_out"][0], "wc": a["w_c_out"][0],
        "wo": a["w_out"][0], "chan": chan,
        "rows": _np.concatenate([a["a_log"][0], a["a_dt_bias"][0], a["c_sinks"][0], a["b_router"][0]])[None],
        "w_router": a["w_router"][0], "w1": a["w1"][0], "b1": b1, "w2": a["w2"][0], "b2": a["b2"][0], "cst": constants(),
    }
    arrays = {k + "_dram": _np.ascontiguousarray(v) for k, v in arrays.items()}
    nc = _bacc.Bacc("TRN2", target_bir_lowering=False, num_devices=1)
    args = [nc.dram_tensor(k, v.shape, _mybir.dt.from_np(v.dtype), kind="ExternalInput").ap() for k, v in arrays.items()]
    args.append(nc.dram_tensor("out_dram", (S, D), _mybir.dt.float32, kind="ExternalOutput").ap())
    build(nc, *args)
    r = _run(nc, [arrays], core_ids=[0])
    return r.results[0]["out_dram"].reshape(1, S, D)
```

```python
import math
import numpy as np
import concourse.bass as bass
from concourse import mybir
from contextlib import ExitStack

P = 128
D = 1024
S = 256
DC = D // P
ST = S // P
AH = 4
CH = 64
NB = 4
KB = 31
KA = 4
NE = 32
F = 1024
W1C = 4
NARROW, WIDE = 64, 128
ALPHA = 2.0 ** 0.25
LEVELS = 6
QH, HD = 8, 64

O_AQ, O_AK, O_AV, O_AZ, O_AB, O_BV, O_BG, O_CQ, O_CK, O_G = 0, 512, 1024, 1536, 2048, 2056, 2568, 3080, 3592, 3848
N_IN = 6920

C_ID, C_TRI, C_SUF, C_STR, C_LVL = 0, 128, 256, 384, 512
C_TRI128 = C_LVL + LEVELS * P
C_ONES = C_TRI128 + P
C_IOTA1 = C_ONES + P
C_IOTA0 = C_IOTA1 + P
C_OH = C_IOTA0 + NE
C_I512 = C_OH + 384
C_I128 = C_I512 + P
N_C = C_I128 + P

H_ACW = 0
H_BW = H_ACW + 12 * KA
H_BB = H_BW + NB * KB
H_BG = H_BB + NB
H_BN = H_BG + NB
H_AN = H_BN + NB
N_H = H_AN + 1

R_ALOG, R_DT, R_SINK, R_BR = 0, 4, 8, 16
N_R = R_BR + NE


def constants():
    i = np.arange(P)
    j, c = i[:, None], i[None, :]
    same = j // CH == c // CH
    out = np.zeros((P, N_C), np.float32)
    out[:, C_ID:C_ID + P] = j == c
    out[:, C_TRI:C_TRI + P] = same & (j <= c)
    out[:, C_SUF:C_SUF + P] = same & (j > c)
    out[:, C_STR:C_STR + P] = same & (j < c)
    for l in range(LEVELS):
        s = 1 << l
        out[:, C_LVL + l * P:C_LVL + (l + 1) * P] = (j // (2 * s) == c // (2 * s)) & (c // s % 2 == 1) & (j // s % 2 == 0)
    out[:, C_TRI128:C_TRI128 + P] = j < c
    out[:, C_ONES:C_ONES + P] = 1.0
    out[:, C_IOTA1:C_IOTA1 + P] = c + 1
    out[:, C_IOTA0:C_IOTA0 + NE] = np.arange(NE)
    out[:, C_I512:C_I512 + P] = 1.0 / 512
    out[:, C_I128:C_I128 + P] = 1.0 / 128
    m = np.arange(384)
    dist = P - (m - 127)
    exact = 16
    large = exact + (np.log(np.maximum(dist, 1).astype(np.float32) / np.float32(exact))
                     / np.float32(math.log(128 / exact)) * np.float32(exact)).astype(np.int32)
    bucket = np.where(dist < exact, dist, np.minimum(large, 31))
    seen = (dist >= 0) & (dist < P)
    out[32, C_OH:C_OH + 384] = ~seen
    for b in range(32):
        out[b, C_OH:C_OH + 384] = seen & (bucket == b)
    return out


def mixer_jobs():
    jobs = [f"hT{t}{h}" for t in range(ST) for h in range(2)]
    jobs += ["relvec"]
    jobs += ["projBV0", "projBV1", "projBG0", "projBG1", "ab", "CK", "CV"]
    jobs += ["gcol", "grow0", "grow1", "brow0", "brow1"]
    jobs += ["projK0", "projK1", "projQ0", "projQ1", "ssK0", "ssK1", "projV0", "projV1", "projZ0", "ssQ0", "ssQ1"]
    jobs += ["kk0", "kk1", "ktok0", "ktok1", "projZ1", "qk0", "qk1", "vtok0", "vtok1", "projC0", "trT0", "trT1", "projC1"]
    fill = [f"projG{g}{h}" for g in range(6) for h in range(2)]
    attn = []
    for n in range(6):
        attn += [[f"sc{n}"], [f"pt{n}"], [f"pv{n}"]]
    attn = [attn[0], attn[3]] + [x for n in range(6) for x in ([attn[3 * n + 1]] + ([attn[3 * n + 6]] if n < 4 else []) + [attn[3 * n + 2]])]
    for l in range(1, LEVELS):
        jobs += [f"lp{l}0", f"lp{l}1"] + (fill[:1] if l == 3 else [])
        fill = fill[1:] if l == 3 else fill
        if l < LEVELS - 1:
            jobs += [f"lt{l}0", f"lt{l}1"]
        jobs += [f"lu{l}0", f"lu{l}1"] + fill[:1]
        fill = fill[1:]
    jobs += ["wT0", "wT1"]
    k = 0
    for n in range(4):
        jobs += [f"vn{n}"] + fill[:1]
        for x in attn[k:k + 2]:
            jobs += x
        k += 2
        if n == 1:
            jobs += ["bmean"]
        if n == 2:
            jobs += ["bvar"]
        jobs += [f"oT{n}"]
        if n < 3:
            jobs += [f"dS{n}"] + fill[1:2]
        fill = fill[2:]
        for x in attn[k:k + 2]:
            jobs += x
        k += 2
    rest = attn[k:]
    for x, y in zip(rest, ["yB0", "yB1", "yB2", "yB3"] + [None] * len(rest)):
        jobs += x + ([y] if y else [])
    jobs += [y for y in ("yB0", "yB1", "yB2", "yB3") if y not in jobs]
    assert not fill
    jobs += ["rms0", "rms1"]
    jobs += ["yC0", "yC1", "yC2", "yC3", "yA0", "yA1", "yA2", "yA3"]
    jobs += ["mix00", "mix01", "mix10", "mix11"]
    for t in range(ST):
        jobs += [f"h1T{t}0", f"h1T{t}1", f"router{t}"]
    jobs += ["rank", "count", "combT"]
    return jobs


JOBS = mixer_jobs()
BANK = {name: n % 8 for n, name in enumerate(JOBS)}
FILL = {name: n // 8 + 1 for n, name in enumerate(JOBS)}
TILES = ["BV", "BG", "M", "K", "Q", "V", "Z", "C", "G0", "G1", "G2", "G3", "G4", "G5", "WB", "WC", "WA", "WO0", "WO1"]
TILE = {name: n for n, name in enumerate(TILES)}
LAST_JOB = {"BV": "projBV1", "BG": "projBG1", "M": "CV", "K": "projK1", "Q": "projQ1", "V": "projV1", "Z": "projZ1",
            "C": "projC1", "WB": "yB3", "WC": "yC3", "WA": "yA3", "WO0": "mix10", "WO1": "mix11"}
LAST_JOB.update({f"G{g}": f"projG{g}1" for g in range(6)})
NT = len(TILES)


def build(nc, x, lnp, rel, w_in, wa, wb, wc, wo, chan, rows, w_router, w1, b1, w2, b2, cst, out):
    f32, i32, u32 = mybir.dt.float32, mybir.dt.int32, mybir.dt.uint32
    ALU, ACT, AX = mybir.AluOpType, mybir.ActivationFunctionType, mybir.AxisListType
    ctx = ExitStack()
    with ctx:
        def sb(name, shape, dt=f32):
            return ctx.enter_context(nc.sbuf_tensor(name, shape, dt))

        def sem(name):
            return ctx.enter_context(nc.semaphore(name))

        w1s = sb("w1s", [P, W1C, 4096])
        w2s = sb("w2s", [P, 2, 4096])
        consts = sb("consts", [P, N_C])
        chp = sb("chp", [P, N_H])
        rowp = sb("rowp", [P, N_R])
        lngb = sb("lngb", [P, 2, D])
        h = sb("h", [P, ST, D])
        gh = sb("gh", [P, 32, S])
        gates = gh[:, 0:24, :]
        hT = gh[:, 24:32, :]
        w2x = gh[:, :, :].rearrange("p a b -> p (a b)").rearrange("p (q c) -> p q c", q=2)
        arena = sb("arena", [P, 13, 1024])
        small = sb("small", [P, 272])
        relw = sb("relw", [33, 8])
        tab_i = sb("tab_i", [1, 3 * NE + 1], i32)
        idx = sb("idx", [P, ST, 8], u32)

        def a4(k, n=4):
            return arena[:, k, :].rearrange("p (n c) -> p n c", n=n)

        def w2v(k, n=4):
            return w2s[:, k // 4, (k % 4) * 1024:(k % 4 + 1) * 1024].rearrange("p (n c) -> p n c", n=n)

        kT, qT, vT = a4(0), a4(1), a4(2)
        az = a4(3)
        cq = a4(4)
        ckv = arena[:, 5, :]
        ck, cv = ckv[:, 0:256], ckv[:, 256:512].rearrange("p (b c) -> p b c", b=2)
        sq = a4(6)
        mst = a4(2, 8)
        convin = gates[:, 0:13, :].rearrange("p a b -> p (a b)")[:, 0:12 * 259].rearrange("p (n c) -> p n c", n=12)
        lnf = lngb[:, :, :].rearrange("p a b -> p (a b)")
        bv = lnf[:, 0:NB * (KB - 1 + S)].rearrange("p (n c) -> p n c", n=NB)
        relv, tmpb = lnf[0:8, 1152:1536], lnf[:, 1536:1792]
        bacc = w2v(0)
        kbt, kdt, vbt = a4(7, 8), a4(8, 8), a4(9, 8)
        at = a4(10, 8)
        tm, um = a4(11, 8), a4(12, 8)
        dt_ = w2v(1, 8)
        eg = w2v(2, 8)
        brow = w2v(3, 8)
        p1 = brow
        bias = w2s[:, 1, 0:2048].rearrange("p (h k) -> p h k", h=8)
        ssc = w2s[:, 1, 2048:3072].rearrange("p (n k) -> p n k", n=2)
        pts = w2s[:, 1, 3072:4096].rearrange("p (n k) -> p n k", n=2)
        wT = at
        oaT = tm
        ocT = kT
        vn = arena[:, 2, 0:512].rearrange("p (n c) -> p n c", n=AH)
        st = arena[:, 2, 512:1024].rearrange("p (n c) -> p n c", n=AH)
        mxT = hT
        xT = arena[:, 0, :].rearrange("p (n c) -> p n c", n=8)
        actT = arena[:, 1, :].rearrange("p (n c) -> p n c", n=8)
        act_tok = arena[:, 2, :]
        gm = arena[:, 3, :].rearrange("p (n c) -> p n c", n=2)
        sg = arena[:, 11, :].rearrange("p (n c) -> p n c", n=2)
        ln_ = arena[:, 12, :].rearrange("p (n c) -> p n c", n=2)
        ys = arena[:, 4, :]
        b2s = arena[0:NE, 7, :]
        b1r = arena[0:NE, 8:10, :].rearrange("p a b -> p (a b)")
        wr = arena[:, 10, 512:768].rearrange("p (k e) -> p k e", k=DC)
        pick = arena[0:NE, 10, 768:896]
        pg = arena[:, 5, 0:256].rearrange("p (n c) -> p n c", n=2)
        pw = arena[:, 5, 256:512].rearrange("p (n c) -> p n c", n=2)
        ptw = arena[:, 5, 512:768].rearrange("p (n c) -> p n c", n=2)
        comb = arena[:, 6, 0:64].rearrange("p (t e) -> p t e", t=2)
        mask = arena[:, 6, 64:128].rearrange("p (t e) -> p t e", t=2)
        rk = arena[:, 6, 128:256].rearrange("p (k t e) -> p k t e", k=2, t=2)
        lg = arena[:, 6, 256:320].rearrange("p (t e) -> p t e", t=2)
        oneh = arena[:, 6, 320:384].rearrange("p (t e) -> p t e", t=2)
        combTs = arena[0:NE, 6, 384:640].rearrange("p (t c) -> p t c", t=2)
        tabf = arena[0:1, 6, 640:768].rearrange("p (t e) -> p t e", t=4)

        def col(a, b):
            return small[:, a:b]

        stats = col(0, 24).rearrange("p (t k s) -> p t k s", t=2, k=2)
        mv = col(24, 28).rearrange("p (t k) -> p t k", t=2)
        rstd = col(28, 30)
        beta = col(32, 40).rearrange("p (t h) -> p t h", t=2)
        gg = col(40, 48).rearrange("p (t h) -> p t h", t=2)
        uu, au, yy, ss, s2, po = (col(48 + 8 * k, 56 + 8 * k) for k in range(6))
        ealog = col(96, 100)
        gcs = col(104, 120).rearrange("p (k t h) -> p k t h", k=2, t=2)
        egc = col(120, 136).rearrange("p (k t h) -> p k t h", k=2, t=2)
        bek = col(136, 144).rearrange("p (t h) -> p t h", t=2)
        mxx = col(144, 168).rearrange("p (n k) -> p n k", n=6)
        smx = col(168, 192).rearrange("p (n k) -> p n k", n=6)
        esk = col(192, 216).rearrange("p (n k) -> p n k", n=6)
        eps5, eps6 = col(216, 217), col(217, 218)
        top = col(224, 240).rearrange("p (t k) -> p t k", t=2)
        ntop = col(240, 242)
        tsum = col(242, 244)
        tw = col(244, 252).rearrange("p (t k) -> p t k", t=2)
        idf = col(252, 268).rearrange("p (t k) -> p t k", t=2)

        ident = consts[:, C_ID:C_ID + P]
        ones = consts[:, C_ONES:C_ONES + P]
        inv512 = consts[:, C_I512:C_I512 + P]
        inv128 = consts[:, C_I128:C_I128 + P]

        rel_d = nc.dram_tensor("relative_vector", (8, P, 384), f32)
        rel_toep = bass.AP(rel_d.ap().tensor, 127, [[383, P], [P * 384, 8], [1, 256]])

        bk = [ctx.enter_context(nc.psum_tensor(f"bank{b}", [P, 512], f32))[:, :] for b in range(8)]
        acc = [[bk[0], bk[1]], [bk[2], bk[3]]]
        ka, kb_, kc, kd = bk[4:8]

        filled = [sem(f"bank_filled{b}") for b in range(8)]
        drained = [sem(f"bank_drained{b}") for b in range(8)]
        x_in = [sem(f"x_in{t}") for t in range(ST)]
        params_in, wr_in = sem("params_in"), sem("wr_in")
        ln_in = [sem(f"ln_in{k}") for k in range(3)]
        tile_in = [sem(f"tile_in{k}") for k in range(W1C)]
        w2_in = [[sem(f"w2_in{par}{q}") for q in range(2)] for par in range(2)]
        rel_out, rel_in, store = sem("rel_out"), sem("rel_in"), sem("stored")
        dve_step, act_step, pool_step = sem("dve_step"), sem("act_step"), sem("pool_step")
        names = ("pad_zero relvec_sb ln_used var_ready sd_ready h_ready hT_ready bvin bgate bglu conv_in conv_out silu_done "
                 "sq_ready l2_sd l2_ready beta_ready aa_ready expu g_ready ealog_rd gcs_ready egc_ready eg_ready "
                 "brow_ready dmin dexp dt_ready at_ready qk_ready kb_ready vb_ready mst_ready t_ready u_ready p1_ready "
                 "qd_ready z_ready cq_ready ck_ready cv_ready gates_ready bconv bcent bsq bsd bnorm bsilu wT_ready vn_ready oT_ready st_ready "
                 "osq rms_sd oa_ready ssc_ready pexp pnorm pt_ready oc_ready mx_ready h1T_ready logits top_ready texp "
                 "comb_ready mask_ready combT_ready table_ready mixer_done "
                 "p_ready gathered xt_ready pt_filled ptw_ready w1_used g_clamped sig_ready swish_ready act_ready turned actT_ready "
                 "y_filled ys_ready acc_open all_scattered").split()
        sm = {n: sem(n) for n in names}

        def wait_fill(eng, job):
            eng.wait_ge(filled[BANK[job]], FILL[job])

        block = ctx.enter_context(nc.Block())

        @block.sync
        def _(sp):
            for t in range(ST):
                sp.dma_start(h[:, t, :], x[t * P:(t + 1) * P, :]).then_inc(x_in[t], 16)

            def load_ln(k):
                sp.dma_start(lngb[:, :, :], bass.AP(lnp.tensor, 2 * D * k, [[0, P], [D, 2], [1, D]])).then_inc(ln_in[k], 16)

            load_ln(0)
            sp.dma_start(consts[:, :], cst).then_inc(params_in, 16)
            sp.dma_start(chp[:, :], chan).then_inc(params_in, 16)
            sp.dma_start(rowp[:, :], bass.AP(rows.tensor, 0, [[0, P], [1, N_R]])).then_inc(params_in, 16)
            sp.dma_start(relw[0:32, :], rel).then_inc(params_in, 16)

            def load_tile(name):
                n = TILE[name]
                if n >= W1C:
                    wait_fill(sp, LAST_JOB[TILES[n - W1C]])
                s = n % W1C
                v8 = w1s[:, s, :].rearrange("p (k c) -> p k c", k=DC)
                v4 = w1s[:, s, :].rearrange("p (k c) -> p k c", k=4)

                def cols(a, b):
                    return w_in[:, a:b].rearrange("(k p) c -> p k c", p=P)

                if name == "M":
                    sp.dma_start(v8[:, :, 0:8], cols(O_AB, O_AB + 8)).then_inc(tile_in[s], 16)
                    sp.dma_start(v8[:, :, 128:384], cols(O_CK, O_CK + 256)).then_inc(tile_in[s], 16)
                elif name in ("WA", "WB"):
                    src = wa if name == "WA" else wb
                    sp.dma_start(v4, src.rearrange("(k p) c -> p k c", p=P)).then_inc(tile_in[s], 16)
                elif name == "WC":
                    for g in range(2):
                        sp.dma_start(v4[64 * g:64 * g + 64, :, :],
                                     wc[256 * g:256 * g + 256, :].rearrange("(j c) n -> c j n", c=64)).then_inc(tile_in[s], 16)
                elif name in ("WO0", "WO1"):
                    c = 512 * int(name[2])
                    sp.dma_start(v8, wo[:, c:c + 512].rearrange("(k p) c -> p k c", p=P)).then_inc(tile_in[s], 16)
                elif name == "C":
                    dst = w1s[:, s, :].rearrange("p (k j g c) -> p k g j c", k=DC, j=4, g=2)
                    for k in range(DC):
                        for g in range(2):
                            sp.dma_start(dst[:, k, g], w_in[k * P:(k + 1) * P, O_CQ + 256 * g:O_CQ + 256 * g + 256]
                                         .rearrange("p (j c) -> p j c", j=4)).then_inc(tile_in[s], 16)
                else:
                    base = {"BV": O_BV, "BG": O_BG, "K": O_AK, "Q": O_AQ, "V": O_AV, "Z": O_AZ}.get(name)
                    if base is None:
                        base = O_G + 512 * int(name[1])
                    sp.dma_start(v8, cols(base, base + 512)).then_inc(tile_in[s], 16)

            for n, name in enumerate(TILES):
                load_tile(name)
                if n == 4:
                    sp.wait_ge(sm["relvec_sb"], 1)
                    sp.dma_start(rel_d[:, :, :], relv.rearrange("h (o c) -> h o c", o=1).broadcast_to([8, P, 384])).then_inc(rel_out, 16)
                    sp.wait_ge(rel_out, 16)
                    sp.dma_start(bias, rel_toep).then_inc(rel_in, 16)

            def load_w1(e, j):
                s = (NT + j) % W1C
                src = w1[e, 256 * j:256 * j + 256, :] if isinstance(e, int) else \
                    w1[bass.ds(e, 1), 256 * j:256 * j + 256, :].rearrange("o d c -> (o d) c")
                sp.dma_start(w1s[:, s, :].rearrange("p (k c) -> p k c", k=2), src.rearrange("(k p) c -> p k c", p=P)).then_inc(tile_in[s], 16)

            def load_w2(e, par, q):
                dst = (w2s, w2x)[par][:, q, :].rearrange("p (k c) -> p k c", k=4)
                src = w2[e, 512 * q:512 * q + 512, :] if isinstance(e, int) else \
                    w2[bass.ds(e, 1), 512 * q:512 * q + 512, :].rearrange("o d c -> (o d) c")
                sp.dma_start(dst, src.rearrange("(k p) c -> p k c", p=P)).then_inc(w2_in[par][q], 16)

            sp.wait_ge(sm["mixer_done"], 2)
            load_ln(1)
            sp.dma_start(wr, w_router.rearrange("(k p) e -> p k e", p=P)).then_inc(wr_in, 16)
            sp.dma_start(b1r, b1).then_inc(wr_in, 16)
            sp.dma_start(b2s, b2).then_inc(wr_in, 16)
            for j in range(W1C):
                wait_fill(sp, LAST_JOB[TILES[NT - W1C + j]])
                load_w1(0, j)
            load_w2(0, 0, 0)
            load_w2(0, 0, 1)
            sp.wait_ge(sm["ln_used"], 2)
            load_ln(2)
            sp.wait_ge(sm["mask_ready"], 1)
            load_w2(1, 1, 0)
            load_w2(1, 1, 1)
            sp.wait_ge(sm["table_ready"], 1)

            def window_before(e):
                return sp.value_load(tab_i[0:1, bass.ds(e + 2 * NE, 1)], min_val=0, max_val=2 * NE)

            def load_first(e):
                last = window_before(e)
                for j in range(W1C):
                    sp.wait_ge(sm["w1_used"], last * 4 + (j + 1))
                    load_w1(e, j)

            first = sp.value_load(tab_i[0:1, 2 * NE + 1:2 * NE + 2], min_val=0, max_val=2 * NE)
            for j in range(W1C):
                sp.wait_ge(sm["w1_used"], first * 4 + (j + 1))
                load_w1(1, j)
            with sp.Fori(1, NE // 2) as i:
                for par in range(2):
                    load_first(i * 2 + par)
                    sp.wait_ge(sm["y_filled"], window_before(i * 2 + (par - 1)) + 1)
                    for q in range(2):
                        load_w2(i * 2 + par, par, q)
            for t in range(ST):
                sp.wait_ge(sm["h_ready"], 2 * ST + t + 1)
                sp.dma_start(out[t * P:(t + 1) * P, :], h[:, t, :]).then_inc(store, 16)
            sp.wait_ge(store, 16 * ST)

        @block.gpsimd
        def _(pool):
            pool.wait_ge(params_in, 64)
            pool.wait_ge(sm["at_ready"], 2)
            wait_fill(pool, "vtok1")
            for l in range(1, LEVELS):
                if l > 1:
                    wait_fill(pool, f"lp{l - 1}1")
                m = consts[:, C_LVL + l * P:C_LVL + (l + 1) * P].rearrange("p (o c) -> p o c", o=1).broadcast_to([P, 8, P])
                pool.tensor_tensor(mst, at, m, ALU.mult).then_inc(sm["mst_ready"], 1)

        @block.scalar
        def _(act):
            def drain(job, ins):
                ins.then_inc(drained[BANK[job]], 1)

            def bank(job):
                wait_fill(act, job)
                return bk[BANK[job]]

            n_act = [0]

            def link(ins):
                n_act[0] += 1
                ins.then_inc(act_step, 1)
                act.wait_ge(act_step, n_act[0])

            A = nc.scalar.activation
            act.wait_ge(sm["pad_zero"], 1)
            for t in range(ST):
                act.wait_ge(sm["var_ready"], t + 1)
                A(rstd[:, t:t + 1], mv[:, t, 1:2], ACT.Sqrt, bias=eps5).then_inc(sm["sd_ready"], 1)
            for t in range(ST):
                for hh in range(2):
                    j = f"hT{t}{hh}"
                    link(A(hT[:, 4 * hh:4 * hh + 4, t * P:(t + 1) * P], bank(j).rearrange("p (k c) -> p k c", k=4), ACT.Copy))
                    act.sem_inc(drained[BANK[j]], 1)
                    act.sem_inc(sm["hT_ready"], 1)
            j = "relvec"
            link(A(relv, bank(j)[0:8, 0:384], ACT.Copy))
            act.sem_inc(drained[BANK[j]], 1)
            act.sem_inc(sm["relvec_sb"], 1)

            def proj(job, dst, func=ACT.Copy):
                drain(job, A(dst, bank(job).rearrange("p (n c) -> p n c", n=2), func))

            proj("projBV0", bv[:, 0:2, KB - 1:])
            proj("projBV1", bv[:, 2:4, KB - 1:])
            proj("projBG0", bacc[:, 0:2, :], ACT.Sigmoid)
            j = "projBG1"
            link(A(bacc[:, 2:4, :], bank(j).rearrange("p (n c) -> p n c", n=2), ACT.Sigmoid))
            act.sem_inc(drained[BANK[j]], 1)
            act.sem_inc(sm["bgate"], 1)
            j = "ab"
            abv = bank(j)[:, 0:16].rearrange("p (t k h) -> p t k h", t=2, k=2)
            link(A(beta, abv[:, :, 0, :], ACT.Sigmoid))
            link(A(uu.rearrange("p (t h) -> p t h", t=2), abv[:, :, 1, :], ACT.Copy))
            act.sem_inc(drained[BANK[j]], 1)
            act.sem_inc(sm["beta_ready"], 1)
            A(ealog, rowp[:, R_ALOG:R_ALOG + 4], ACT.Exp)
            act.wait_ge(sm["aa_ready"], 1)
            A(yy, au, ACT.Exp, scale=-1.0).then_inc(sm["expu"], 1)
            drain("CK", A(ck, bank("CK")[:, 0:256], ACT.Copy))
            j = "CV"
            link(A(cv, bank(j)[:, 0:256].rearrange("p (b c) -> p b c", b=2), ACT.Copy))
            act.sem_inc(drained[BANK[j]], 1)
            act.sem_inc(sm["cv_ready"], 1)
            act.wait_ge(sm["gcs_ready"], 1)
            A(egc, gcs, ACT.Exp).then_inc(sm["egc_ready"], 1)
            act.wait_ge(sm["dmin"], 2)
            for t in range(ST):
                j = f"grow{t}"
                drain(j, A(eg[:, 4 * t:4 * t + 4, :], bank(j).rearrange("p (n c) -> p n c", n=4), ACT.Exp))
            for t in range(ST):
                j = f"brow{t}"
                drain(j, A(brow[:, 4 * t:4 * t + 4, :], bank(j).rearrange("p (n c) -> p n c", n=4), ACT.Copy))
            link(A(dt_, dt_, ACT.Exp))
            act.sem_inc(sm["dexp"], 1)
            base = {"Q": 0, "K": 4, "V": 8}
            dstT = {"K": kT, "Q": qT, "V": vT}

            def conv_in(x_):
                for hh in range(2):
                    j = f"proj{x_}{hh}"
                    link(A(convin[:, base[x_] + 2 * hh:base[x_] + 2 * hh + 2, KA - 1:], bank(j).rearrange("p (n c) -> p n c", n=2), ACT.Copy))
                    act.sem_inc(drained[BANK[j]], 1)
                act.sem_inc(sm["conv_in"], 1)

            def silu(x_, n):
                act.wait_ge(sm["conv_out"], n)
                link(A(dstT[x_], dstT[x_], ACT.Silu))
                act.sem_inc(sm["silu_done"], 1)

            def l2(x_, n):
                if n > 1:
                    wait_fill(act, "ssK1")
                link(A(sq, dstT[x_], ACT.Square))
                act.sem_inc(sm["sq_ready"], 1)

            def l2_root(x_):
                for hh in range(2):
                    j = f"ss{x_}{hh}"
                    link(A(sq[:, 2 * hh:2 * hh + 2, :], bank(j).rearrange("p (n c) -> p n c", n=2), ACT.Sqrt, bias=eps6))
                    act.sem_inc(drained[BANK[j]], 1)
                act.sem_inc(sm["l2_sd"], 1)

            conv_in("K")
            silu("K", 1)
            l2("K", 1)
            conv_in("Q")
            l2_root("K")
            conv_in("V")
            act.wait_ge(sm["l2_ready"], 1)
            silu("Q", 2)
            l2("Q", 2)
            l2_root("Q")

            def gate_z(hh):
                drain(f"projZ{hh}", A(az[:, 2 * hh:2 * hh + 2, :], bank(f"projZ{hh}").rearrange("p (n c) -> p n c", n=2), ACT.Silu))

            gate_z(0)
            silu("V", 3)
            gate_z(1)
            for hh in range(2):
                j = f"projC{hh}"
                link(A(cq[:, 2 * hh:2 * hh + 2, :], bank(j).rearrange("p (n c) -> p n c", n=2), ACT.Copy))
                act.sem_inc(drained[BANK[j]], 1)
            act.sem_inc(sm["cq_ready"], 1)

            def gate(job):
                k = 4 * int(job[5]) + 2 * int(job[6])
                drain(job, A(gates[:, k:k + 2, :], bank(job).rearrange("p (n c) -> p n c", n=2), ACT.Sigmoid))

            def level_p(job):
                t = int(job[3])
                link(A(p1[:, 4 * t:4 * t + 4, :], bank(job).rearrange("p (n c) -> p n c", n=4), ACT.Copy))
                act.sem_inc(drained[BANK[job]], 1)
                act.sem_inc(sm["p1_ready"], 1)

            def w_t(job):
                t = int(job[2])
                link(A(wT[:, 4 * t:4 * t + 4, :], bank(job).rearrange("p (n c) -> p n c", n=4), ACT.Copy, scale=-1.0))
                act.sem_inc(drained[BANK[job]], 1)
                act.sem_inc(sm["wT_ready"], 1)

            def v_new(job):
                r = 64 * (int(job[2]) % 2)
                link(A(vn[r:r + 64, :, :], bank(job)[r:r + 64, :].rearrange("p (n c) -> p n c", n=4), ACT.Copy))
                act.sem_inc(drained[BANK[job]], 1)
                act.sem_inc(sm["vn_ready"], 1)

            def o_t(job):
                n = int(job[2])
                link(A(oaT.rearrange("p a b -> p (a b)").rearrange("p (n c) -> p n c", n=4)[:, :, n * CH:(n + 1) * CH],
                       bank(job)[:, 0:256].rearrange("p (n c) -> p n c", n=4), ACT.Copy))
                act.sem_inc(drained[BANK[job]], 1)
                act.sem_inc(sm["oT_ready"], 1)

            def softmax(n):
                heads, keys = (4, 128) if n < 2 else (2, 256)
                act.wait_ge(sm["ssc_ready"], n + 1)
                for k in range(heads):
                    hd = 4 * n + k if n < 2 else 2 * (n - 2) + k
                    A(ssc[:, n % 2, k * keys:(k + 1) * keys], ssc[:, n % 2, k * keys:(k + 1) * keys], ACT.Exp,
                      bias=mxx[:, n, k:k + 1], accum_out=smx[:, n, k:k + 1])
                    ins = A(esk[:, n, k:k + 1], rowp[:, R_SINK + hd:R_SINK + hd + 1], ACT.Exp, bias=mxx[:, n, k:k + 1])
                ins.then_inc(sm["pexp"], 1)

            def p_t(job):
                n = int(job[2])
                link(A(pts[:, n % 2, :], bank(job), ACT.Copy))
                act.sem_inc(drained[BANK[job]], 1)
                act.sem_inc(sm["pt_ready"], 1)

            def p_v(job):
                n = int(job[2])
                g, j0, nh, q0 = (n, 0, 4, 0) if n < 2 else ((n - 2) // 2, 2 * (n % 2), 2, P)
                r = 64 * g
                link(A(ocT[r:r + 64, j0:j0 + nh, q0:q0 + P], bank(job)[r:r + 64, 0:nh * P].rearrange("p (n c) -> p n c", n=nh), ACT.Copy))
                act.sem_inc(drained[BANK[job]], 1)
                act.sem_inc(sm["oc_ready"], 1)

            def b_var(job):
                drain(job, A(tmpb, bank(job)[:, 0:256], ACT.Sqrt, bias=eps5))
                act.wait_ge(drained[BANK[job]], FILL[job])
                act.sem_inc(sm["bsd"], 1)
                act.wait_ge(sm["bnorm"], 1)
                for c in range(NB):
                    ins = A(bacc[:, c, :], bacc[:, c, :], ACT.Silu, bias=chp[:, H_BN + c:H_BN + c + 1], scale=chp[:, H_BG + c:H_BG + c + 1])
                ins.then_inc(sm["bsilu"], 1)

            def b_square(job):
                act.wait_ge(sm["bcent"], 1)
                A(bv[:, :, 0:S], bacc, ACT.Square).then_inc(sm["bsq"], 1)

            steps = {"projG": gate, "lp": level_p, "wT": w_t, "vn": v_new, "oT": o_t, "pt": p_t, "pv": p_v, "bvar": b_var, "bmean": b_square}
            for job in JOBS[JOBS.index("lp10"):JOBS.index("rms0")]:
                for key, step in steps.items():
                    if job.startswith(key):
                        step(job)
                if job.startswith("sc"):
                    softmax(int(job[2]))
            act.wait_ge(sm["oT_ready"], 4)
            link(A(sq, oaT.rearrange("p a b -> p (a b)").rearrange("p (n c) -> p n c", n=4), ACT.Square))
            act.sem_inc(sm["osq"], 1)
            for hh in range(2):
                j = f"rms{hh}"
                link(A(sq[:, 2 * hh:2 * hh + 2, :], bank(j).rearrange("p (n c) -> p n c", n=2), ACT.Sqrt, bias=eps6))
                act.sem_inc(drained[BANK[j]], 1)
            act.sem_inc(sm["rms_sd"], 1)
            act.sem_inc(sm["mixer_done"], 1)
            for t in range(ST):
                act.wait_ge(sm["var_ready"], ST + t + 1)
                A(rstd[:, t:t + 1], mv[:, t, 1:2], ACT.Sqrt, bias=eps5).then_inc(sm["sd_ready"], 1)
            for t in range(ST):
                for hh in range(2):
                    j = f"h1T{t}{hh}"
                    link(A(hT[:, 4 * hh:4 * hh + 4, t * P:(t + 1) * P], bank(j).rearrange("p (k c) -> p k c", k=4), ACT.Copy))
                    act.sem_inc(drained[BANK[j]], 1)
                    act.sem_inc(sm["h1T_ready"], 1)
            for t in range(ST):
                act.wait_ge(sm["top_ready"], t + 1)
                A(tw[:, t, :], top[:, t, 0:4], ACT.Exp, bias=ntop[:, t:t + 1], accum_out=tsum[:, t:t + 1]).then_inc(sm["texp"], 1)
            act.wait_ge(sm["table_ready"], 1)

            def window(g, width):
                for k, wk in enumerate((kc, kd)):
                    act.wait_ge(sm["gathered"], g * 2 + (k + 1))
                    A(xT[:, 4 * k:4 * k + 4, 0:width], wk[:, 0:4 * width].rearrange("p (n c) -> p n c", n=4), ACT.Copy).then_inc(sm["xt_ready"], 1)
                n = 256 if width == NARROW else 512
                for k in range(2):
                    act.wait_ge(sm["g_clamped"], g * 2 + (k + 1))
                    A(sg[:, k, 0:n], gm[:, k, 0:n], ACT.Sigmoid, scale=1.702).then_inc(sm["sig_ready"], 1)
                for k in range(2):
                    act.wait_ge(sm["turned"], g * 2 + (k + 1))
                    if width == NARROW:
                        dst = actT.rearrange("p (u j) c -> p j u c", u=2)[:, 2 * k:2 * k + 2, :, 0:NARROW]
                        src = (kb_, ka)[k][:, 0:256].rearrange("p (j u c) -> p j u c", j=2, u=2)
                    else:
                        dst = actT[:, 4 * k:4 * k + 4, :]
                        src = (ka, kc)[k].rearrange("p (j c) -> p j c", j=4)
                    A(dst, src, ACT.Copy).then_inc(sm["actT_ready"], 1)
                act.wait_ge(sm["y_filled"], g + 1)
                for k in range(2):
                    src = kd[64 * k:64 * k + 64, :] if width == NARROW else (kb_, kd)[k][:, :]
                    A(ys[0:width, 512 * k:512 * k + 512], src, ACT.Copy).then_inc(sm["ys_ready"], 1)

            with act.Fori(0, NE // 2) as i:
                for par in range(2):
                    g0 = act.value_load(tab_i[0:1, bass.ds(i * 2 + par, 1)], min_val=0, max_val=2 * NE)
                    cnt = act.value_load(tab_i[0:1, bass.ds(i * 2 + (par + NE), 1)], min_val=0, max_val=S)
                    with act.If(cnt > WIDE):
                        window(g0, WIDE)
                        window(g0 + 1, WIDE)
                    with act.Else():
                        with act.If(cnt > NARROW):
                            window(g0, WIDE)
                        with act.Else():
                            window(g0, NARROW)
            for t in range(ST):
                act.wait_ge(sm["var_ready"], 2 * ST + t + 1)
                A(rstd[:, t:t + 1], mv[:, t, 1:2], ACT.Sqrt, bias=eps5).then_inc(sm["sd_ready"], 1)

        @block.vector
        def _(dve):
            V = nc.vector
            n_dve = [0]

            def link(ins):
                n_dve[0] += 1
                ins.then_inc(dve_step, 1)
                dve.wait_ge(dve_step, n_dve[0])

            def signal(ins, *sems):
                link(ins)
                for s in sems:
                    dve.sem_inc(s, 1)

            def bank(job):
                wait_fill(dve, job)
                return bk[BANK[job]]

            def layer_norm(k, t):
                for q in range(2):
                    V.bn_stats(stats[:, t, q, :], h[:, t, 512 * q:512 * q + 512]).then_inc(dve_step, 1)
                    n_dve[0] += 1
                dve.wait_ge(dve_step, n_dve[0])
                V.bn_aggr(mv[:, t, :], stats[:, t, :, :].rearrange("p a b -> p (a b)")).then_inc(sm["var_ready"], 1)
                dve.wait_ge(ln_in[k], 16)
                dve.wait_ge(sm["sd_ready"], ST * k + t + 1)
                link(V.reciprocal(rstd[:, t:t + 1], rstd[:, t:t + 1]))
                link(V.tensor_scalar(h[:, t, :], h[:, t, :], mv[:, t, 0:1], rstd[:, t:t + 1], ALU.subtract, ALU.mult))
                link(V.tensor_tensor(h[:, t, :], h[:, t, :], lngb[:, 0, :], ALU.mult))
                signal(V.tensor_tensor(h[:, t, :], h[:, t, :], lngb[:, 1, :], ALU.add), sm["h_ready"])
                if t == ST - 1:
                    dve.sem_inc(sm["ln_used"], 1)

            link(V.memset(small[:, :], 0.0))
            V.memset(eps5, 1e-5)
            V.memset(eps6, 1e-6)
            V.memset(relw[32:33, :], -1e30)
            signal(V.memset(convin[:, :, 0:KA - 1], 0.0), sm["pad_zero"])
            for t in range(ST):
                dve.wait_ge(x_in[t], 16)
                layer_norm(0, t)
            signal(V.memset(bv[:, :, 0:KB - 1], 0.0))
            dve.wait_ge(params_in, 64)
            dve.wait_ge(sm["bgate"], 1)
            link(V.tensor_tensor(bv[:, :, KB - 1:], bv[:, :, KB - 1:], bacc, ALU.mult))
            dve.wait_ge(sm["beta_ready"], 1)
            v42 = "p (t h) -> p t h"
            dtb = rowp[:, R_DT:R_DT + 4].rearrange("p (o h) -> p o h", o=1).broadcast_to([P, 2, 4])
            link(V.tensor_tensor(uu.rearrange(v42, t=2), uu.rearrange(v42, t=2), dtb, ALU.add))
            link(V.tensor_scalar(au, uu, -1.0, None, ALU.mult))
            signal(V.tensor_tensor(au, au, uu, ALU.max), sm["aa_ready"])
            dve.wait_ge(sm["expu"], 1)
            link(V.tensor_scalar(ss, yy, 2.0, None, ALU.add))
            link(V.reciprocal(ss, ss))
            link(V.tensor_tensor(ss, ss, yy, ALU.mult))
            link(V.tensor_tensor(s2, ss, ss, ALU.mult))
            link(V.tensor_scalar(po, s2, 1.0 / 17, 1.0 / 15, ALU.mult, ALU.add))
            for k in (13, 11, 9, 7, 5, 3, 1):
                link(V.tensor_tensor(po, po, s2, ALU.mult))
                link(V.tensor_scalar(po, po, 1.0 / k, None, ALU.add))
            link(V.scalar_tensor_tensor(po, po, 2.0, ss, ALU.mult, ALU.mult))
            link(V.scalar_tensor_tensor(po, uu, 0.0, po, ALU.max, ALU.add))
            eal = ealog.rearrange("p (o h) -> p o h", o=1).broadcast_to([P, 2, 4])
            signal(V.scalar_tensor_tensor(gg, po.rearrange(v42, t=2), -1.0, eal, ALU.mult, ALU.mult), sm["g_ready"])
            j = "gcol"
            signal(V.tensor_copy(gcs, bank(j)[:, 0:16].rearrange("p (k t h) -> p k t h", k=2, t=2)),
                   sm["gcs_ready"], drained[BANK[j]])
            strict = consts[:, C_STR:C_STR + P]
            for t in range(ST):
                b_ = bank(f"grow{t}")
                for hh in range(AH):
                    link(V.scalar_tensor_tensor(dt_[:, 4 * t + hh, :], b_[:, hh * P:(hh + 1) * P], gcs[:, 0, t, hh:hh + 1],
                                                strict, ALU.subtract, ALU.mult))
                signal(V.tensor_scalar(dt_[:, 4 * t:4 * t + 4, :], dt_[:, 4 * t:4 * t + 4, :], 0.0, None, ALU.min), sm["dmin"])
            dve.wait_ge(sm["egc_ready"], 1)
            link(V.tensor_tensor(bek, beta, egc[:, 0], ALU.mult))

            n_conv = [0]

            def conv_a(x_, k0, dstT):
                dve.wait_ge(sm["conv_in"], n_conv[0] + 1)
                for c in range(4):
                    w = chp[:, H_ACW + (k0 + c) * KA:H_ACW + (k0 + c + 1) * KA]
                    V.tensor_scalar(dstT[:, c, :], convin[:, k0 + c, 0:S], w[:, 0:1], None, ALU.mult).then_inc(dve_step, 1)
                n_dve[0] += 4
                for k in range(1, KA):
                    for c in range(4):
                        w = chp[:, H_ACW + (k0 + c) * KA:H_ACW + (k0 + c + 1) * KA]
                        dve.wait_ge(dve_step, n_dve[0] - 3)
                        V.scalar_tensor_tensor(dstT[:, c, :], convin[:, k0 + c, k:k + S], w[:, k:k + 1], dstT[:, c, :],
                                               ALU.mult, ALU.add).then_inc(dve_step, 1)
                        n_dve[0] += 1
                dve.wait_ge(dve_step, n_dve[0])
                n_conv[0] += 1
                dve.sem_inc(sm["conv_out"], 1)

            def l2(dstT, n, scale):
                dve.wait_ge(sm["l2_sd"], n)
                link(V.reciprocal(sq, sq))
                signal(V.scalar_tensor_tensor(dstT, dstT, scale, sq, ALU.mult, ALU.mult), sm["l2_ready"])

            conv_a("K", 4, kT)
            conv_a("Q", 0, qT)
            l2(kT, 1, 1.0)
            dve.wait_ge(sm["dexp"], 1)
            incl = consts[:, C_TRI:C_TRI + P].rearrange("p (o c) -> p o c", o=1).broadcast_to([P, 8, P])
            link(V.tensor_tensor(dt_, dt_, incl, ALU.mult))
            conv_a("V", 8, vT)
            l2(qT, 2, 128 ** -0.5)
            for t in range(ST):
                j = f"kk{t}"
                link(V.tensor_tensor(at[:, 4 * t:4 * t + 4, :], bank(j).rearrange("p (n c) -> p n c", n=4), brow[:, 4 * t:4 * t + 4, :], ALU.mult))
                dve.sem_inc(drained[BANK[j]], 1)
                signal(V.tensor_tensor(at[:, 4 * t:4 * t + 4, :], at[:, 4 * t:4 * t + 4, :], dt_[:, 4 * t:4 * t + 4, :], ALU.mult), sm["at_ready"])
            m0 = consts[:, C_LVL:C_LVL + P].rearrange("p (o c) -> p o c", o=1).broadcast_to([P, 8, P])
            idb = ident.rearrange("p (o c) -> p o c", o=1).broadcast_to([P, 8, P])
            link(V.tensor_tensor(um, at, m0, ALU.mult))
            signal(V.tensor_tensor(um, idb, um, ALU.subtract), sm["u_ready"])
            for t in range(ST):
                j = f"ktok{t}"
                b_ = bank(j).rearrange("p (n c) -> p n c", n=4)
                V.tensor_tensor(kbt[:, 4 * t:4 * t + 4, :], b_, bek[:, t, :].rearrange("p (h o) -> p h o", o=1).broadcast_to([P, 4, P]), ALU.mult)
                signal(V.tensor_tensor(kdt[:, 4 * t:4 * t + 4, :], b_, egc[:, 1, t, :].rearrange("p (h o) -> p h o", o=1).broadcast_to([P, 4, P]), ALU.mult),
                       drained[BANK[j]], sm["kb_ready"])
            for t in range(ST):
                j = f"qk{t}"
                signal(V.tensor_tensor(dt_[:, 4 * t:4 * t + 4, :], bank(j).rearrange("p (n c) -> p n c", n=4), dt_[:, 4 * t:4 * t + 4, :], ALU.mult),
                       drained[BANK[j]], sm["qk_ready"])
            for t in range(ST):
                signal(V.tensor_tensor(qT[:, :, t * P:(t + 1) * P], qT[:, :, t * P:(t + 1) * P], eg[:, 4 * t:4 * t + 4, :], ALU.mult), sm["qd_ready"])
            for t in range(ST):
                j = f"vtok{t}"
                signal(V.tensor_tensor(vbt[:, 4 * t:4 * t + 4, :], bank(j).rearrange("p (n c) -> p n c", n=4),
                                       beta[:, t, :].rearrange("p (h o) -> p h o", o=1).broadcast_to([P, 4, P]), ALU.mult),
                       drained[BANK[j]], sm["vb_ready"])
            for t in range(ST):
                j = f"trT{t}"
                signal(V.tensor_copy(tm[:, 4 * t:4 * t + 4, :], bank(j).rearrange("p (n c) -> p n c", n=4)), drained[BANK[j]], sm["t_ready"])

            taps = [(k, c) for k in range(KB) for c in range(NB)]
            sem_conv = sm["bconv"]
            done = [0]

            def conv_b(count):
                for k, c in taps[done[0]:done[0] + count]:
                    w = chp[:, H_BW + c * KB + k:H_BW + c * KB + k + 1]
                    if k == 0:
                        V.tensor_scalar(bacc[:, c, :], bv[:, c, 0:S], w, chp[:, H_BB + c:H_BB + c + 1], ALU.mult, ALU.add).then_inc(sem_conv, 1)
                    else:
                        dve.wait_ge(sem_conv, done[0] - 3)
                        V.scalar_tensor_tensor(bacc[:, c, :], bv[:, c, k:k + S], w, bacc[:, c, :], ALU.mult, ALU.add).then_inc(sem_conv, 1)
                    done[0] += 1

            def level(job, buf, ready):
                t = int(job[3])
                v = buf[:, 4 * t:4 * t + 4, :]
                signal(V.tensor_tensor(v, v, bank(job).rearrange("p (n c) -> p n c", n=4), ALU.subtract), drained[BANK[job]], sm[ready])

            def scores(n):
                heads, keys = (4, 128) if n < 2 else (2, 256)
                job = f"sc{n}"
                if n >= 2:
                    wait_fill(dve, f"pt{n - 2}")
                b_ = bank(job)[:, 0:heads * keys].rearrange("p (n c) -> p n c", n=heads)
                s_ = ssc[:, n % 2, :].rearrange("p (n c) -> p n c", n=heads)
                h0 = 4 * n if n < 2 else 2 * (n - 2)
                if n == 0:
                    dve.wait_ge(rel_in, 16)
                signal(V.scalar_tensor_tensor(s_, b_, HD ** -0.5, bias[:, h0:h0 + heads, 256 - keys:256], ALU.mult, ALU.add), drained[BANK[job]])
                link(V.tensor_reduce(mxx[:, n, 0:heads], s_, AX.X, ALU.max))
                link(V.tensor_tensor(mxx[:, n, 0:heads], mxx[:, n, 0:heads], rowp[:, R_SINK + h0:R_SINK + h0 + heads], ALU.max))
                signal(V.tensor_scalar(mxx[:, n, 0:heads], mxx[:, n, 0:heads], -1.0, None, ALU.mult), sm["ssc_ready"])
                conv_b(4)
                dve.wait_ge(sm["pexp"], n + 1)
                link(V.tensor_tensor(smx[:, n, 0:heads], smx[:, n, 0:heads], esk[:, n, 0:heads], ALU.add))
                link(V.reciprocal(smx[:, n, 0:heads], smx[:, n, 0:heads]))
                signal(V.tensor_tensor(s_, s_, smx[:, n, 0:heads].rearrange("p (h o) -> p h o", o=1).broadcast_to([P, heads, keys]), ALU.mult), sm["pnorm"])

            def state(n):
                job = f"dS{n}"
                t, r = n // 2, n % 2
                if n == 0:
                    signal(V.tensor_copy(st, bank(job).rearrange("p (n c) -> p n c", n=4)), drained[BANK[job]], sm["st_ready"])
                    return
                for hh in range(AH):
                    ins = V.scalar_tensor_tensor(st[:, hh, :], st[:, hh, :], eg[:, 4 * t + hh, 64 * r + 63:64 * r + 64],
                                                 bank(job)[:, hh * P:(hh + 1) * P], ALU.mult, ALU.add)
                signal(ins, drained[BANK[job]], sm["st_ready"])

            def merge(br, b, q):
                job = f"y{br}{q}"
                g_ = gates[:, 8 * b + 2 * q:8 * b + 2 * q + 2, :]
                b_ = bank(job).rearrange("p (n c) -> p n c", n=2)
                dst = mxT[:, 2 * q:2 * q + 2, :]
                if br == "B":
                    signal(V.tensor_tensor(dst, b_, g_, ALU.mult), drained[BANK[job]])
                else:
                    signal(V.tensor_tensor(g_, b_, g_, ALU.mult), drained[BANK[job]])
                    signal(V.tensor_tensor(dst, dst, g_, ALU.add), *([sm["mx_ready"]] if br == "A" else []))

            for job in JOBS[JOBS.index("lp10"):JOBS.index("rms0")]:
                if job[0] == "y":
                    merge("B", 1, int(job[2]))
                elif job[:2] == "lt":
                    level(job, tm, "t_ready")
                elif job[:2] == "lu":
                    level(job, um, "u_ready")
                elif job[:5] == "projG":
                    conv_b(14)
                elif job[:2] == "sc":
                    scores(int(job[2]))
                elif job[:2] == "dS":
                    state(int(job[2]))
                elif job == "bmean":
                    conv_b(len(taps))
                    dve.wait_ge(sem_conv, len(taps))
                    dve.sem_inc(sm["conv_out"], 1)
                    b_ = bank(job)[:, 0:256].rearrange("p (o c) -> p o c", o=1).broadcast_to([P, 4, 256])
                    signal(V.tensor_tensor(bacc, bacc, b_, ALU.subtract), drained[BANK[job]], sm["bcent"])
                elif job == "bvar":
                    dve.wait_ge(sm["bsd"], 1)
                    link(V.reciprocal(tmpb, tmpb))
                    signal(V.tensor_tensor(bacc, bacc, tmpb.rearrange("p (o c) -> p o c", o=1).broadcast_to([P, 4, 256]), ALU.mult), sm["bnorm"])

            dve.wait_ge(sm["rms_sd"], 1)
            oa4 = oaT.rearrange("p a b -> p (a b)").rearrange("p (n c) -> p n c", n=4)
            link(V.reciprocal(sq, sq))
            link(V.tensor_tensor(oa4, oa4, sq, ALU.mult))
            signal(V.scalar_tensor_tensor(oa4, oa4, chp[:, H_AN:H_AN + 1], az, ALU.mult, ALU.mult), sm["oa_ready"], sm["mixer_done"])
            for q in range(4):
                merge("C", 2, q)
            for q in range(4):
                merge("A", 0, q)
            for t in range(ST):
                for hf in range(2):
                    job = f"mix{t}{hf}"
                    v = h[:, t, 512 * hf:512 * hf + 512]
                    signal(V.scalar_tensor_tensor(v, v, ALPHA, bank(job), ALU.mult, ALU.add), drained[BANK[job]])
                layer_norm(1, t)
            dve.wait_ge(wr_in, 48)
            V.memset(ys, 0.0)
            signal(V.memset(ptw, 0.0))
            dve.sem_inc(sm["ys_ready"], 2)
            dve.sem_inc(sm["ptw_ready"], 1)
            for t in range(ST):
                j = f"router{t}"
                signal(V.tensor_tensor(lg[:, t, :], bank(j)[:, 0:NE], rowp[:, R_BR:R_BR + NE], ALU.add), drained[BANK[j]])
                link(V.max(top[:, t, :], lg[:, t, :]))
                link(V.max_index(idx[:, t, :], top[:, t, :], lg[:, t, :]))
                link(V.tensor_copy(idf[:, t, :], idx[:, t, :]))
                signal(V.tensor_scalar(ntop[:, t:t + 1], top[:, t, 0:1], -1.0, None, ALU.mult), sm["top_ready"])
            io = consts[:, C_IOTA0:C_IOTA0 + NE]
            for t in range(ST):
                link(V.tensor_scalar(mask[:, t, :], io, idf[:, t, 0:1], None, ALU.is_equal))
                for k in range(1, 4):
                    link(V.scalar_tensor_tensor(mask[:, t, :], io, idf[:, t, k:k + 1], mask[:, t, :], ALU.is_equal, ALU.add))
            dve.sem_inc(sm["mask_ready"], 1)
            for t in range(ST):
                dve.wait_ge(sm["texp"], t + 1)
                link(V.reciprocal(tsum[:, t:t + 1], tsum[:, t:t + 1]))
                link(V.tensor_scalar(tw[:, t, :], tw[:, t, :], tsum[:, t:t + 1], None, ALU.mult))
                link(V.tensor_scalar(comb[:, t, :], io, idf[:, t, 0:1], tw[:, t, 0:1], ALU.is_equal, ALU.mult))
                for k in range(1, 4):
                    link(V.tensor_scalar(oneh[:, t, :], io, idf[:, t, k:k + 1], tw[:, t, k:k + 1], ALU.is_equal, ALU.mult))
                    link(V.tensor_tensor(comb[:, t, :], comb[:, t, :], oneh[:, t, :], ALU.add))
            dve.sem_inc(sm["comb_ready"], 1)
            j = "combT"
            signal(V.tensor_copy(combTs, bank(j)[0:NE, 0:256].rearrange("p (t c) -> p t c", t=2)), drained[BANK[j]], sm["combT_ready"])
            j = "rank"
            link(V.scalar_tensor_tensor(rk[:, 0], bank(j)[:, 0:2 * NE].rearrange("p (t e) -> p t e", t=2), 1.0, mask, ALU.add, ALU.mult))
            dve.sem_inc(drained[BANK[j]], 1)
            link(V.tensor_scalar(rk[:, 1], rk[:, 0], float(WIDE), None, ALU.subtract))
            j = "count"
            link(V.tensor_copy(tabf[:, 1, :], bank(j)[0:1, 0:NE]))
            dve.sem_inc(drained[BANK[j]], 1)
            link(V.tensor_copy(tab_i[0:1, NE:2 * NE], tabf[:, 1, :]))
            link(V.tensor_scalar(tabf[:, 2, :], tabf[:, 1, :], float(WIDE), 1.0, ALU.is_gt, ALU.add))
            link(V.memset(tabf[:, 3, :], 1.0))
            link(V.tensor_tensor_scan(tabf[:, 0, :], tabf[:, 3, :], tabf[:, 2, :], 0.0, ALU.mult, ALU.add))
            link(V.tensor_copy(tab_i[0:1, 3 * NE:3 * NE + 1], tabf[:, 0, NE - 1:NE]))
            link(V.tensor_tensor(tabf[:, 0, :], tabf[:, 0, :], tabf[:, 2, :], ALU.subtract))
            link(V.tensor_copy(tab_i[0:1, 0:NE], tabf[:, 0, :]))
            link(V.tensor_scalar(tabf[:, 0, :], tabf[:, 0, :], -1.0, 0.0, ALU.add, ALU.max))
            link(V.tensor_copy(tab_i[0:1, 2 * NE:3 * NE], tabf[:, 0, :]))
            dve.sem_inc(sm["table_ready"], 1)
            io1 = consts[:, C_IOTA1:C_IOTA1 + P]

            def window(e, g, width, part):
                for t in range(ST):
                    V.tensor_scalar(pg[:, t, :], io1, rk[:, part, t, bass.ds(e, 1)], None, ALU.is_equal)
                    V.tensor_scalar(pw[:, t, :], io1, rk[:, part, t, bass.ds(e, 1)], comb[:, t, bass.ds(e, 1)], ALU.is_equal, ALU.mult)
                V.tensor_copy(pick, ident[0:NE, bass.ds(e, 1)].broadcast_to([NE, P])).then_inc(sm["p_ready"], 1)
                dve.wait_ge(sm["w1_used"], g * 4 + 4)
                n = 256 if width == NARROW else 512
                parts = [(ka[:, 0:256], kc[:, 0:256]), (ka[:, 256:512], kc[:, 256:512])] if width == NARROW else [(ka, kc), (kb_, kd)]
                for k in range(2):
                    V.tensor_scalar(gm[:, k, 0:n], parts[k][0], 7.0, None, ALU.min).then_inc(sm["g_clamped"], 1)
                for k in range(2):
                    V.tensor_scalar(ln_[:, k, 0:n], parts[k][1], 7.0, -7.0, ALU.min, ALU.max)
                    dve.wait_ge(sm["sig_ready"], g * 2 + (k + 1))
                    V.tensor_tensor(gm[:, k, 0:n], gm[:, k, 0:n], sg[:, k, 0:n], ALU.mult).then_inc(sm["swish_ready"], 1)
                    dve.wait_ge(sm["swish_ready"], g * 2 + (k + 1))
                    V.scalar_tensor_tensor(act_tok[:, n * k:n * k + n], ln_[:, k, 0:n], 1.0, gm[:, k, 0:n], ALU.add, ALU.mult).then_inc(sm["act_ready"], 1)
                dve.wait_ge(sm["pt_filled"], g + 1)
                V.tensor_copy(ptw, (kd if width == NARROW else ka)[:, 0:256].rearrange("p (t c) -> p t c", t=2)).then_inc(sm["ptw_ready"], 1)

            with dve.Fori(0, NE // 2) as i:
                for par in range(2):
                    g0 = dve.value_load(tab_i[0:1, bass.ds(i * 2 + par, 1)], min_val=0, max_val=2 * NE)
                    cnt = dve.value_load(tab_i[0:1, bass.ds(i * 2 + (par + NE), 1)], min_val=0, max_val=S)
                    e = i * 2 + par
                    with dve.If(cnt > WIDE):
                        window(e, g0, WIDE, 0)
                        window(e, g0 + 1, WIDE, 1)
                    with dve.Else():
                        with dve.If(cnt > NARROW):
                            window(e, g0, WIDE, 0)
                        with dve.Else():
                            window(e, g0, NARROW, 0)
            dve.wait_ge(sm["all_scattered"], 1)
            for t in range(ST):
                for k in range(2):
                    v = h[:, t, 512 * k:512 * k + 512]
                    link(V.scalar_tensor_tensor(v, v, ALPHA, acc[t][k][:, :], ALU.mult, ALU.add))
                layer_norm(2, t)

        @block.tensor
        def _(pe):
            mm = nc.tensor.matmul

            def tr(o, i):
                return nc.tensor.transpose(o, i, ident)

            def open_bank(job):
                if FILL[job] > 1:
                    pe.wait_ge(drained[BANK[job]], FILL[job] - 1)
                return bk[BANK[job]]

            def close(job, ins):
                ins.then_inc(filled[BANK[job]], 1)

            seen = {}

            def tile(name):
                n = TILE[name]
                s = n % W1C
                if name not in seen:
                    parts = {"M": 2, "WC": 2, "C": 16}
                    total = sum(parts.get(TILES[m], 1) for m in range(s, n + 1, W1C))
                    pe.wait_ge(tile_in[s], 16 * total)
                    seen[name] = True
                return w1s[:, s, :]

            tile_total = [sum({"M": 2, "WC": 2, "C": 16}.get(TILES[m], 1) for m in range(s, NT, W1C)) for s in range(W1C)]

            def proj(job, name, cols):
                w = tile(name).rearrange("p (k c) -> p k c", k=DC)
                b = open_bank(job)
                for n, c in enumerate(cols):
                    for k in range(DC):
                        ins = mm(b[:, n * S:(n + 1) * S], lhsT=w[:, k, c:c + P], rhs=hT[:, k, :], start=k == 0, stop=k == DC - 1)
                close(job, ins)

            srcT = {"K": kT, "Q": qT}
            level_n = {}
            for job in JOBS:
                if job[:2] == "hT" or job[:3] == "h1T":
                    t, hh = int(job[-2]), int(job[-1])
                    pe.wait_ge(params_in, 64)
                    pe.wait_ge(sm["h_ready"], t + 1 + (ST if job[1] == "1" else 0))
                    b = open_bank(job)
                    for k in range(4):
                        ins = tr(b[:, k * P:(k + 1) * P], h[:, t, (4 * hh + k) * P:(4 * hh + k + 1) * P])
                    close(job, ins)
                elif job == "relvec":
                    pe.wait_ge(sm["pad_zero"], 1)
                    close(job, mm(open_bank(job)[0:8, 0:384], lhsT=relw[:, :], rhs=consts[0:33, C_OH:C_OH + 384], start=True, stop=True))
                    pe.wait_ge(sm["hT_ready"], 4)
                elif job[:4] == "proj":
                    x_ = job[4:-1]
                    name = {"BV": "BV", "BG": "BG", "K": "K", "Q": "Q", "V": "V", "Z": "Z", "C": "C"}.get(x_, x_)
                    c0 = 256 * int(job[-1])
                    proj(job, name, (c0, c0 + P))
                elif job == "ab":
                    w = tile("M").rearrange("p (k c) -> p k c", k=DC)
                    b = open_bank(job)
                    for t in range(ST):
                        for k in range(DC):
                            ins = mm(b[:, 8 * t:8 * t + 8], lhsT=hT[:, k, t * P:(t + 1) * P], rhs=w[:, k, 0:8], start=k == 0, stop=k == DC - 1)
                    close(job, ins)
                elif job == "CK":
                    proj(job, "M", (P,))
                elif job == "CV":
                    w = tile("M").rearrange("p (k c) -> p k c", k=DC)
                    b = open_bank(job)
                    for t in range(ST):
                        for k in range(DC):
                            ins = mm(b[:, P * t:P * t + P], lhsT=hT[:, k, t * P:(t + 1) * P], rhs=w[:, k, 2 * P:3 * P], start=k == 0, stop=k == DC - 1)
                    close(job, ins)
                elif job == "gcol":
                    pe.wait_ge(sm["g_ready"], 1)
                    b = open_bank(job)
                    for k, m in enumerate((C_TRI, C_SUF)):
                        for t in range(ST):
                            ins = mm(b[:, 8 * k + 4 * t:8 * k + 4 * t + 4], lhsT=consts[:, m:m + P], rhs=gg[:, t, :], start=True, stop=True)
                    close(job, ins)
                elif job[:4] in ("grow", "brow"):
                    t = int(job[4])
                    b = open_bank(job)
                    src, m = (gg, C_TRI) if job[0] == "g" else (beta, C_ID)
                    for hh in range(AH):
                        ins = mm(b[:, hh * P:(hh + 1) * P], lhsT=src[:, t, hh:hh + 1].broadcast_to([P, P]), rhs=consts[:, m:m + P], start=True, stop=True)
                    close(job, ins)
                elif job[:2] == "ss":
                    hh = int(job[3])
                    pe.wait_ge(sm["sq_ready"], 1 if job[2] == "K" else 2)
                    b = open_bank(job)
                    close(job, mm(b[:, :], lhsT=ones, rhs=sq[:, 2 * hh:2 * hh + 2, :], start=True, stop=True))
                elif job[:2] in ("kk", "qk"):
                    t = int(job[2])
                    pe.wait_ge(sm["l2_ready"], 1 if job[0] == "k" else 2)
                    b = open_bank(job)
                    for hh in range(AH):
                        tt = slice(t * P, (t + 1) * P)
                        ins = mm(b[:, hh * P:(hh + 1) * P], lhsT=kT[:, hh, tt], rhs=(kT if job[0] == "k" else qT)[:, hh, tt], start=True, stop=True)
                    close(job, ins)
                elif job[1:4] == "tok":
                    t = int(job[4])
                    if job[0] == "v":
                        pe.wait_ge(sm["silu_done"], 3)
                    b = open_bank(job)
                    for hh in range(AH):
                        ins = tr(b[:, hh * P:(hh + 1) * P], (kT if job[0] == "k" else vT)[:, hh, t * P:(t + 1) * P])
                    close(job, ins)
                elif job[:3] == "trT":
                    t = int(job[3])
                    pe.wait_ge(sm["u_ready"], 1)
                    b = open_bank(job)
                    for hh in range(AH):
                        ins = tr(b[:, hh * P:(hh + 1) * P], um[:, 4 * t + hh, :])
                    close(job, ins)
                elif job[:2] in ("lp", "lt", "lu"):
                    l, t = int(job[2]), int(job[3])
                    if job[1] == "p":
                        pe.wait_ge(sm["mst_ready"], l)
                        pe.wait_ge(sm["t_ready"], 2 * (l - 1) + t + 1)
                        lhs, rhs = mst, tm
                    else:
                        pe.wait_ge(sm["p1_ready"], 2 * (l - 1) + t + 1)
                        pe.wait_ge(sm["u_ready"], 1 + 2 * (l - 1))
                        lhs, rhs = (um, p1) if job[1] == "t" else (p1, um)
                    b = open_bank(job)
                    for hh in range(AH):
                        ins = mm(b[:, hh * P:(hh + 1) * P], lhsT=lhs[:, 4 * t + hh, :], rhs=rhs[:, 4 * t + hh, :], start=True, stop=True)
                    close(job, ins)
                elif job == "bmean":
                    pe.wait_ge(sm["conv_out"], 4)
                    b = open_bank(job)
                    for c in range(NB):
                        ins = mm(b[:, 0:S], lhsT=inv512[:, :], rhs=bacc[:, c, :], start=c == 0, stop=c == NB - 1)
                    close(job, ins)
                elif job == "bvar":
                    pe.wait_ge(sm["bsq"], 1)
                    b = open_bank(job)
                    for c in range(NB):
                        ins = mm(b[:, 0:S], lhsT=inv512[:, :], rhs=bv[:, c, 0:S], start=c == 0, stop=c == NB - 1)
                    close(job, ins)
                elif job[:2] == "wT":
                    t = int(job[2])
                    pe.wait_ge(sm["u_ready"], 1 + 2 * (LEVELS - 1))
                    pe.wait_ge(sm["kb_ready"], 2)
                    b = open_bank(job)
                    for hh in range(AH):
                        ins = mm(b[:, hh * P:(hh + 1) * P], lhsT=kbt[:, 4 * t + hh, :], rhs=um[:, 4 * t + hh, :], start=True, stop=True)
                    close(job, ins)
                elif job[:2] == "vn":
                    n = int(job[2])
                    t, r = n // 2, 64 * (n % 2)
                    pe.wait_ge(sm["wT_ready"], t + 1)
                    pe.wait_ge(sm["vb_ready"], 2)
                    if n:
                        pe.wait_ge(sm["st_ready"], n)
                    b = open_bank(job)
                    for hh in range(AH):
                        o = b[r:r + 64, hh * P:(hh + 1) * P]
                        ins = mm(o, lhsT=um[r:r + 64, 4 * t + hh, r:r + 64], rhs=vbt[r:r + 64, 4 * t + hh, :], start=True, stop=n == 0)
                        if n:
                            ins = mm(o, lhsT=wT[:, 4 * t + hh, r:r + 64], rhs=st[:, hh, :], start=False, stop=True)
                    close(job, ins)
                elif job[:2] == "oT":
                    n = int(job[2])
                    t, r = n // 2, 64 * (n % 2)
                    pe.wait_ge(sm["vn_ready"], n + 1)
                    pe.wait_ge(sm["qk_ready"], 2)
                    pe.wait_ge(sm["qd_ready"], 2)
                    b = open_bank(job)
                    for hh in range(AH):
                        o = b[:, hh * CH:(hh + 1) * CH]
                        ins = mm(o, lhsT=vn[r:r + 64, hh, :], rhs=dt_[r:r + 64, 4 * t + hh, r:r + 64], start=True, stop=n == 0)
                        if n:
                            ins = mm(o, lhsT=st[:, hh, :], rhs=qT[:, hh, n * CH:(n + 1) * CH], start=False, stop=True)
                    close(job, ins)
                elif job[:2] == "dS":
                    n = int(job[2])
                    t, r = n // 2, 64 * (n % 2)
                    b = open_bank(job)
                    for hh in range(AH):
                        ins = mm(b[:, hh * P:(hh + 1) * P], lhsT=kdt[r:r + 64, 4 * t + hh, :], rhs=vn[r:r + 64, hh, :], start=True, stop=True)
                    close(job, ins)
                elif job[:2] == "sc":
                    n = int(job[2])
                    pe.wait_ge(sm["cq_ready"], 1)
                    pe.wait_ge(sm["cv_ready"], 1)
                    g, j0, nh, q0 = (n, 0, 4, 0) if n < 2 else ((n - 2) // 2, 2 * (n % 2), 2, P)
                    keys = P if n < 2 else 2 * P
                    b = open_bank(job)
                    for k in range(nh):
                        ins = mm(b[:, k * keys:(k + 1) * keys], lhsT=cq[64 * g:64 * g + 64, j0 + k, q0:q0 + P],
                                 rhs=ck[64 * g:64 * g + 64, 0:keys], start=True, stop=True)
                    close(job, ins)
                elif job[:2] == "pt":
                    n = int(job[2])
                    pe.wait_ge(sm["pnorm"], n + 1)
                    b = open_bank(job)
                    for k in range(4):
                        ins = tr(b[:, k * P:(k + 1) * P], ssc[:, n % 2, k * P:(k + 1) * P])
                    close(job, ins)
                elif job[:2] == "pv":
                    n = int(job[2])
                    g, j0, nh, q0 = (n, 0, 4, 0) if n < 2 else ((n - 2) // 2, 2 * (n % 2), 2, P)
                    pe.wait_ge(sm["pt_ready"], n + 1)
                    b = open_bank(job)
                    nk = 1 if n < 2 else 2
                    for k in range(nh):
                        for kb in range(nk):
                            ins = mm(b[64 * g:64 * g + 64, k * P:(k + 1) * P], lhsT=cv[:, kb, 64 * g:64 * g + 64],
                                     rhs=pts[:, n % 2, (k * nk + kb) * P:(k * nk + kb + 1) * P], start=kb == 0, stop=kb == nk - 1)
                    close(job, ins)
                elif job[:3] == "rms":
                    hh = int(job[3])
                    pe.wait_ge(sm["osq"], 1)
                    b = open_bank(job)
                    close(job, mm(b[:, :], lhsT=inv128[:, :], rhs=sq[:, 2 * hh:2 * hh + 2, :], start=True, stop=True))
                elif job[0] == "y":
                    q = int(job[2])
                    src, ready, cnt_ = {"B": (bacc, "bsilu", 1), "C": (ocT, "oc_ready", 6), "A": (oaT.rearrange("p a b -> p (a b)").rearrange("p (n c) -> p n c", n=4), "oa_ready", 1)}[job[1]]
                    pe.wait_ge(sm[ready], cnt_)
                    w = tile("W" + job[1]).rearrange("p (k c) -> p k c", k=4)
                    b = open_bank(job)
                    for n in range(2):
                        c = (2 * q + n) * P
                        for k in range(4):
                            ins = mm(b[:, n * S:(n + 1) * S], lhsT=w[:, k, c:c + P], rhs=src[:, k, :], start=k == 0, stop=k == 3)
                    close(job, ins)
                elif job[:3] == "mix":
                    t, hf = int(job[3]), int(job[4])
                    pe.wait_ge(sm["mx_ready"], 4)
                    w = tile(f"WO{hf}").rearrange("p (k c) -> p k c", k=DC)
                    b = open_bank(job)
                    for k in range(DC):
                        ins = mm(b[:, :], lhsT=mxT[:, k, t * P:(t + 1) * P], rhs=w[:, k, :], start=k == 0, stop=k == DC - 1)
                    close(job, ins)
                elif job[:6] == "router":
                    t = int(job[6])
                    pe.wait_ge(sm["h1T_ready"], 2 * t + 2)
                    pe.wait_ge(wr_in, 48)
                    b = open_bank(job)
                    for k in range(DC):
                        ins = mm(b[:, 0:NE], lhsT=hT[:, k, t * P:(t + 1) * P], rhs=wr[:, k, :], start=k == 0, stop=k == DC - 1)
                    close(job, ins)
                elif job == "rank":
                    pe.wait_ge(sm["mask_ready"], 1)
                    b = open_bank(job)
                    tri = consts[:, C_TRI128:C_TRI128 + P]
                    mm(b[:, 0:NE], lhsT=tri, rhs=mask[:, 0, :], start=True, stop=True)
                    mm(b[:, NE:2 * NE], lhsT=ones, rhs=mask[:, 0, :], start=True, stop=False)
                    close(job, mm(b[:, NE:2 * NE], lhsT=tri, rhs=mask[:, 1, :], start=False, stop=True))
                elif job == "count":
                    b = open_bank(job)
                    mm(b[:, 0:NE], lhsT=ones, rhs=mask[:, 0, :], start=True, stop=False)
                    close(job, mm(b[:, 0:NE], lhsT=ones, rhs=mask[:, 1, :], start=False, stop=True))
                elif job == "combT":
                    pe.wait_ge(sm["comb_ready"], 1)
                    b = open_bank(job)
                    for t in range(ST):
                        ins = tr(b[0:NE, t * P:(t + 1) * P], comb[:, t, :])
                    close(job, ins)
                else:
                    raise ValueError(job)
            pe.wait_ge(sm["combT_ready"], 1)
            for b in range(8):
                last = [n for n in JOBS if BANK[n] == b][-1]
                pe.wait_ge(drained[b], FILL[last])
            for t in range(ST):
                for k in range(2):
                    ins = mm(acc[t][k][:, :], lhsT=combTs[:, t, :], rhs=b2s[:, 512 * k:512 * k + 512], start=True, stop=False, skip_group_check=True)
            ins.then_inc(sm["acc_open"], 1)
            pe.wait_ge(sm["table_ready"], 1)

            def scatter(last=False):
                for t in range(ST):
                    for k in range(2):
                        ins = mm(acc[t][k][:, :], lhsT=ptw[:, t, :], rhs=ys[:, 512 * k:512 * k + 512], start=False, stop=last, skip_group_check=True)
                return ins

            def turn_weights(g, bank_):
                for t in range(ST):
                    ins = tr(bank_[:, t * P:(t + 1) * P], pw[:, t, :])
                ins.then_inc(sm["pt_filled"], 1)

            def window(i, par, g, width):
                narrow = width == NARROW
                pe.wait_ge(sm["p_ready"], g + 1)
                for b, wk in enumerate((kc, kd)):
                    if b == 1:
                        pe.wait_ge(sm["ys_ready"], g * 2 + 2)
                    for k in range(4):
                        for t in range(ST):
                            ins = mm(wk[:, k * width:(k + 1) * width], lhsT=h[:, t, (4 * b + k) * P:(4 * b + k + 1) * P], rhs=pg[:, t, 0:width],
                                     start=t == 0, stop=t == ST - 1)
                    ins.then_inc(sm["gathered"], 1)
                if narrow:
                    hidden = [(ka[0:64, :], 0), (ka[64:128, :], 512), (kc[0:64, :], F), (kc[64:128, :], F + 512)]
                else:
                    hidden = [(ka, 0), (kb_, 512), (kc, F), (kd, F + 512)]
                pe.wait_ge(sm["ptw_ready"], g + 1)
                for n, (o, c) in enumerate(hidden):
                    if n == 2:
                        pe.wait_ge(sm["xt_ready"], g * 2 + 2)
                    mm(o, lhsT=pick[:, 0:width], rhs=b1r[:, c:c + 512], start=True, stop=False, skip_group_check=True)
                for j in range(W1C):
                    s = (NT + j) % W1C
                    pe.wait_ge(tile_in[s], i * 32 + (16 * tile_total[s] + 16 * (par + 1)))
                    for k in range(2):
                        for o, c in hidden:
                            ins = mm(o, lhsT=xT[:, 2 * j + k, 0:width], rhs=w1s[:, s, 2048 * k + c:2048 * k + c + 512], start=False,
                                     stop=j == W1C - 1 and k == 1, skip_group_check=True)
                    ins.then_inc(sm["w1_used"], 1)
                scatter()
                if narrow:
                    turn_weights(g, kd)
                for k in range(2):
                    pe.wait_ge(sm["act_ready"], g * 2 + (k + 1))
                    bank_ = (kb_, ka)[k] if narrow else (ka, kc)[k]
                    nj = 2 if narrow else 4
                    for j in range(nj):
                        ins = tr(bank_[:, j * P:(j + 1) * P], act_tok[:, (nj * k + j) * P:(nj * k + j + 1) * P])
                    ins.then_inc(sm["turned"], 1)
                if narrow:
                    pe.wait_ge(sm["ptw_ready"], g + 2)
                    outs = [(kd[0:64, :], 0), (kd[64:128, :], 512)]
                    order = (0, 1, 4, 5, 2, 3, 6, 7)
                else:
                    outs = [(kb_, 0), (kd, 512)]
                    order = range(8)
                for n, f in enumerate(order):
                    if n == 0:
                        pe.wait_ge(w2_in[par][0], i * 16 + 16)
                    if n == (2 if narrow else 4):
                        pe.wait_ge(w2_in[par][1], i * 16 + 16)
                    if n % 4 == 0:
                        pe.wait_ge(sm["actT_ready"], g * 2 + (n // 4 + 1))
                    w = (w2s, w2x)[par][:, f // 4, :]
                    for o, c in outs:
                        ins = mm(o, lhsT=actT[:, f, 0:width], rhs=w[:, 1024 * (f % 4) + c:1024 * (f % 4) + c + 512], start=n == 0, stop=n == 7,
                                 skip_group_check=True)
                ins.then_inc(sm["y_filled"], 1)
                if not narrow:
                    turn_weights(g, ka)

            with pe.Fori(0, NE // 2) as i:
                for par in range(2):
                    g0 = pe.value_load(tab_i[0:1, bass.ds(i * 2 + par, 1)], min_val=0, max_val=2 * NE)
                    cnt = pe.value_load(tab_i[0:1, bass.ds(i * 2 + (par + NE), 1)], min_val=0, max_val=S)
                    with pe.If(cnt > WIDE):
                        window(i, par, g0, WIDE)
                        window(i, par, g0 + 1, WIDE)
                    with pe.Else():
                        with pe.If(cnt > NARROW):
                            window(i, par, g0, WIDE)
                        with pe.Else():
                            window(i, par, g0, NARROW)
            windows = pe.value_load(tab_i[0:1, 3 * NE:3 * NE + 1], min_val=NE, max_val=2 * NE)
            pe.wait_ge(sm["ys_ready"], windows * 2 + 2)
            pe.wait_ge(sm["ptw_ready"], windows + 1)
            scatter(True).then_inc(sm["all_scattered"], 1)



def kernel(**inputs):
    import numpy as _np
    import concourse.bacc as _bacc
    from concourse import mybir as _mybir
    from concourse.bass_utils import run_bass_kernel_spmd as _run

    a = {k: _np.asarray(v) for k, v in inputs.items()}
    chan = _np.concatenate([
        a["a_conv_w"][0].reshape(KA, 12, P).transpose(2, 1, 0).reshape(P, 12 * KA),
        a["b_dw_w"][0].reshape(KB, NB, P).transpose(2, 1, 0).reshape(P, NB * KB),
        a["b_dw_b"][0].reshape(NB, P).T, a["b_ln_g"][0].reshape(NB, P).T, a["b_ln_b"][0].reshape(NB, P).T,
        a["a_norm_g"][0].reshape(P, 1)], axis=1)
    arrays = {
        "x": a["x"][0],
        "lnp": _np.stack([a["ln_in_g"], a["ln_in_b"], a["ln1_g"][0], a["ln1_b"][0], a["ln2_g"][0], a["ln2_b"][0]]),
        "rel": a["rel_bias"], "w_in": a["w_in"][0], "wa": a["w_a_out"][0], "wb": a["w_b_out"][0], "wc": a["w_c_out"][0],
        "wo": a["w_out"][0], "chan": chan,
        "rows": _np.concatenate([a["a_log"][0], a["a_dt_bias"][0], a["c_sinks"][0], a["b_router"][0]])[None],
        "w_router": a["w_router"][0], "w1": a["w1"][0], "b1": a["b1"][0], "w2": a["w2"][0], "b2": a["b2"][0], "cst": constants(),
    }
    arrays = {k + "_dram": _np.ascontiguousarray(v) for k, v in arrays.items()}
    nc = _bacc.Bacc("TRN2", target_bir_lowering=False, num_devices=1)
    args = [nc.dram_tensor(k, v.shape, _mybir.dt.from_np(v.dtype), kind="ExternalInput").ap() for k, v in arrays.items()]
    args.append(nc.dram_tensor("out_dram", (S, D), _mybir.dt.float32, kind="ExternalOutput").ap())
    build(nc, *args)
    r = _run(nc, [arrays], core_ids=[0])
    return r.results[0]["out_dram"].reshape(1, S, D)
```

```python
import math
import numpy as np
import concourse.bass as bass
from concourse import mybir
from contextlib import ExitStack

P = 128
D = 1024
S = 256
DC = D // P
ST = S // P
AH = 4
CH = 64
NB = 4
KB = 31
KA = 4
NE = 32
F = 1024
W1C = 4
NARROW, WIDE = 64, 128
ALPHA = 2.0 ** 0.25
LEVELS = 6
QH, HD = 8, 64

O_AQ, O_AK, O_AV, O_AZ, O_AB, O_BV, O_BG, O_CQ, O_CK, O_G = 0, 512, 1024, 1536, 2048, 2056, 2568, 3080, 3592, 3848
N_IN = 6920

C_ID, C_TRI, C_SUF, C_STR, C_LVL = 0, 128, 256, 384, 512
C_TRI128 = C_LVL + LEVELS * P
C_ONES = C_TRI128 + P
C_IOTA1 = C_ONES + P
C_IOTA0 = C_IOTA1 + P
C_OH = C_IOTA0 + NE
C_I512 = C_OH + 384
C_I128 = C_I512 + P
C_PICK = C_I128 + P
N_C = C_PICK + NE

H_ACW = 0
H_BW = H_ACW + 12 * KA
H_BB = H_BW + NB * KB
H_BG = H_BB + NB
H_BN = H_BG + NB
H_AN = H_BN + NB
N_H = H_AN + 1

R_ALOG, R_DT, R_SINK, R_BR = 0, 4, 8, 16
N_R = R_BR + NE


def constants():
    i = np.arange(P)
    j, c = i[:, None], i[None, :]
    same = j // CH == c // CH
    out = np.zeros((P, N_C), np.float32)
    out[:, C_ID:C_ID + P] = j == c
    out[:, C_TRI:C_TRI + P] = same & (j <= c)
    out[:, C_SUF:C_SUF + P] = same & (j > c)
    out[:, C_STR:C_STR + P] = same & (j < c)
    for l in range(LEVELS):
        s = 1 << l
        out[:, C_LVL + l * P:C_LVL + (l + 1) * P] = (j // (2 * s) == c // (2 * s)) & (c // s % 2 == 1) & (j // s % 2 == 0)
    out[:, C_TRI128:C_TRI128 + P] = j < c
    out[:, C_ONES:C_ONES + P] = 1.0
    out[:, C_IOTA1:C_IOTA1 + P] = c + 1
    out[:, C_IOTA0:C_IOTA0 + NE] = np.arange(NE)
    out[:, C_I512:C_I512 + P] = 1.0 / 512
    out[:, C_I128:C_I128 + P] = 1.0 / 128
    out[0:2 * NE, C_PICK:C_PICK + NE] = i[0:2 * NE, None] % NE == np.arange(NE)
    m = np.arange(384)
    dist = P - (m - 127)
    exact = 16
    large = exact + (np.log(np.maximum(dist, 1).astype(np.float32) / np.float32(exact))
                     / np.float32(math.log(128 / exact)) * np.float32(exact)).astype(np.int32)
    bucket = np.where(dist < exact, dist, np.minimum(large, 31))
    seen = (dist >= 0) & (dist < P)
    out[32, C_OH:C_OH + 384] = ~seen
    for b in range(32):
        out[b, C_OH:C_OH + 384] = seen & (bucket == b)
    return out


def mixer_jobs():
    jobs = [f"hT{t}{h}" for t in range(ST) for h in range(2)]
    jobs += ["projBV0", "projBV1", "projBG0", "projBG1", "relvec", "ab", "CK", "CV"]
    jobs += ["gcol", "grow0", "grow1", "brow0", "brow1"]
    jobs += ["projK0", "projK1", "projQ0", "projQ1", "ssK0", "ssK1", "projV0", "projV1", "projZ0", "ssQ0", "ssQ1"]
    jobs += ["kk0", "kk1", "ktok0", "ktok1", "projZ1", "qk0", "qk1", "vtok0", "vtok1", "projC0", "trT0", "trT1", "projC1"]
    fill = [f"projG{g}{h}" for g in range(6) for h in range(2)]
    attn = []
    for n in range(6):
        attn += [[f"sc{n}"], [f"pt{n}"], [f"pv{n}"]]
    attn = [attn[0], attn[3]] + [x for n in range(6) for x in ([attn[3 * n + 1]] + ([attn[3 * n + 6]] if n < 4 else []) + [attn[3 * n + 2]])]
    for l in range(1, LEVELS):
        jobs += [f"lp{l}0", f"lp{l}1"] + (fill[:1] if l == 3 else [])
        fill = fill[1:] if l == 3 else fill
        if l < LEVELS - 1:
            jobs += [f"lt{l}0", f"lt{l}1"]
        jobs += [f"lu{l}0", f"lu{l}1"] + fill[:1]
        fill = fill[1:]
    jobs += ["wT0", "wT1"]
    k = 0
    for n in range(4):
        jobs += [f"vn{n}"] + fill[:1]
        for x in attn[k:k + 2]:
            jobs += x
        k += 2
        jobs += [f"oT{n}"]
        if n < 3:
            jobs += [f"dS{n}"] + fill[1:2] + {0: [], 1: ["bmean"], 2: ["bvar"]}[n]
        fill = fill[2:]
        for x in attn[k:k + 2]:
            jobs += x
        k += 2
    rest = attn[k:]
    for x, y in zip(rest, ["yB0", "yB1", "yB2", "yB3"] + [None] * len(rest)):
        jobs += x + ([y] if y else [])
    jobs += [y for y in ("yB0", "yB1", "yB2", "yB3") if y not in jobs]
    assert not fill
    jobs += ["rms0", "rms1"]
    jobs += ["yC0", "yC1", "yC2", "yC3", "yA0", "yA1", "yA2", "yA3"]
    jobs += ["mix00", "mix01", "mix10", "mix11"]
    for t in range(ST):
        jobs += [f"h1T{t}0", f"h1T{t}1", f"router{t}"]
    jobs += ["rank", "count", "combT"]
    return jobs


JOBS = mixer_jobs()
BANK = {name: n % 8 for n, name in enumerate(JOBS)}
FILL = {name: n // 8 + 1 for n, name in enumerate(JOBS)}
PROJ = [name for name in JOBS if name.startswith("proj")]
RAW, SPLIT = 3, 2
DVE_LOW = range(2, 7)
PARTS = {"projC0": 4, "projC1": 4}
TILES = ["WB", "WC", "WA", "WO0", "WO1"]
TILE = {name: n for n, name in enumerate(TILES)}
LAST_JOB = {"WB": "yB3", "WC": "yC3", "WA": "yA3", "WO0": "mix10", "WO1": "mix11"}
NT = len(TILES)


def build(nc, x, lnp, rel, w_in, wa, wb, wc, wo, chan, rows, w_router, w1, b1, w2, b2, cst, out):
    f32, i32, u32 = mybir.dt.float32, mybir.dt.int32, mybir.dt.uint32
    ALU, ACT, AX = mybir.AluOpType, mybir.ActivationFunctionType, mybir.AxisListType
    ctx = ExitStack()
    with ctx:
        def sb(name, shape, dt=f32):
            return ctx.enter_context(nc.sbuf_tensor(name, shape, dt))

        def sem(name):
            return ctx.enter_context(nc.semaphore(name))

        f32r = mybir.dt.float32r
        with nc.sbuf_tensor("raw_w", [P, RAW, 2048], f32) as raw_w, \
                nc.sbuf_tensor("hT_lo", [P, DC, S], f32r) as hT_lo, \
                nc.sbuf_tensor("w_hi", [P, SPLIT, DC, 256], f32r) as w_hi, \
                nc.sbuf_tensor("w_lo", [P, SPLIT, DC, 256], f32r) as w_lo:
            pass
        w1s = sb("w1s", [P, W1C, 4096])
        w2s = sb("w2s", [P, 2, 4096])
        consts = sb("consts", [P, N_C])
        chp = sb("chp", [P, N_H])
        rowp = sb("rowp", [P, N_R])
        lngb = sb("lngb", [P, 2, D])
        h = sb("h", [P, ST, D])
        with nc.sbuf_tensor("below_hT", [P, 24, S], f32), nc.sbuf_tensor("hT_hi", [P, DC, S], f32r) as hT_hi:
            pass
        gh = sb("gh", [P, 32, S])
        gates = gh[:, 0:24, :]
        hT = gh[:, 24:32, :]
        w2x = gh[:, :, :].rearrange("p a b -> p (a b)").rearrange("p (q c) -> p q c", q=2)
        with nc.sbuf_tensor("below_b1", [P, 8, 1024], f32), nc.sbuf_tensor("b1_parts", [P, 2 * F], f32r) as b1p, \
                nc.sbuf_tensor("below_pick", [P, 768], f32), nc.sbuf_tensor("pick", [P, P], f32r) as pick:
            pass
        b1p, pick = b1p[:, :], pick[:, :]
        arena = sb("arena", [P, 13, 1024])
        small = sb("small", [P, 272])
        relw = sb("relw", [33, 8])
        tab_i = sb("tab_i", [1, 3 * NE + 1], i32)
        idx = sb("idx", [P, ST, 8], u32)

        def a4(k, n=4):
            return arena[:, k, :].rearrange("p (n c) -> p n c", n=n)

        def w2v(k, n=4):
            return w2s[:, k // 4, (k % 4) * 1024:(k % 4 + 1) * 1024].rearrange("p (n c) -> p n c", n=n)

        kT, qT, vT = a4(0), a4(1), a4(2)
        az = a4(3)
        cq = a4(4)
        ckv = arena[:, 5, :]
        ck, cv = ckv[:, 0:256], ckv[:, 256:512].rearrange("p (b c) -> p b c", b=2)
        sq = a4(6)
        mst = a4(2, 8)
        convin = gates[:, 0:13, :].rearrange("p a b -> p (a b)")[:, 0:12 * 259].rearrange("p (n c) -> p n c", n=12)
        lnf = lngb[:, :, :].rearrange("p a b -> p (a b)")
        bv = lnf[:, 0:NB * (KB - 1 + S)].rearrange("p (n c) -> p n c", n=NB)
        relv, tmpb = lnf[0:8, 1152:1536], lnf[:, 1536:1792]
        bacc = w2v(0)
        kbt, kdt, vbt = a4(7, 8), a4(8, 8), a4(9, 8)
        at = a4(10, 8)
        tm, um = a4(11, 8), a4(12, 8)
        dt_ = w2v(1, 8)
        eg = w2v(2, 8)
        brow = w2v(3, 8)
        p1 = brow
        bias = w2s[:, 1, 0:2048].rearrange("p (h k) -> p h k", h=8)
        ssc = w2s[:, 1, 2048:3072].rearrange("p (n k) -> p n k", n=2)
        pts = w2s[:, 1, 3072:4096].rearrange("p (n k) -> p n k", n=2)
        hT0 = arena[:, 11:13, :].rearrange("p a b -> p (a b)").rearrange("p (k c) -> p k c", k=DC)
        wM = arena[:, 7:11, :].rearrange("p a b -> p (a b)").rearrange("p (k c) -> p k c", k=DC)
        wT = at
        oaT = tm
        ocT = kT
        vn = arena[:, 2, 0:512].rearrange("p (n c) -> p n c", n=AH)
        st = arena[:, 2, 512:1024].rearrange("p (n c) -> p n c", n=AH)
        mxT = hT
        xT = arena[:, 0, :].rearrange("p (n c) -> p n c", n=8)
        actT = arena[:, 1, :].rearrange("p (n c) -> p n c", n=8)
        act_tok = arena[:, 2, :]
        gm = arena[:, 3, :].rearrange("p (n c) -> p n c", n=2)
        sg = arena[:, 11, :].rearrange("p (n c) -> p n c", n=2)
        ln_ = arena[:, 12, :].rearrange("p (n c) -> p n c", n=2)
        ys = arena[:, 4, :]
        b2s = arena[0:NE, 7, :]
        b1w = arena[:, 1:3, :].rearrange("p a b -> p (a b)")
        wr = arena[:, 10, 512:768].rearrange("p (k e) -> p k e", k=DC)
        pg = arena[:, 5, 0:256].rearrange("p (n c) -> p n c", n=2)
        pw = arena[:, 5, 256:512].rearrange("p (n c) -> p n c", n=2)
        ptw = arena[:, 5, 512:768].rearrange("p (n c) -> p n c", n=2)
        comb = arena[:, 6, 0:64].rearrange("p (t e) -> p t e", t=2)
        mask = arena[:, 6, 64:128].rearrange("p (t e) -> p t e", t=2)
        rk = arena[:, 6, 128:256].rearrange("p (k t e) -> p k t e", k=2, t=2)
        lg = arena[:, 6, 256:320].rearrange("p (t e) -> p t e", t=2)
        oneh = arena[:, 6, 320:384].rearrange("p (t e) -> p t e", t=2)
        combTs = arena[0:NE, 6, 384:640].rearrange("p (t c) -> p t c", t=2)
        tabf = arena[0:1, 6, 640:768].rearrange("p (t e) -> p t e", t=4)

        def col(a, b):
            return small[:, a:b]

        stats = col(0, 24).rearrange("p (t k s) -> p t k s", t=2, k=2)
        mv = col(24, 28).rearrange("p (t k) -> p t k", t=2)
        rstd, shift = col(28, 30), col(30, 32)
        beta = col(32, 40).rearrange("p (t h) -> p t h", t=2)
        gg = col(40, 48).rearrange("p (t h) -> p t h", t=2)
        uu, au, yy, ss, s2, po = (col(48 + 8 * k, 56 + 8 * k) for k in range(6))
        ealog = col(96, 100)
        gcs = col(104, 120).rearrange("p (k t h) -> p k t h", k=2, t=2)
        egc = col(120, 136).rearrange("p (k t h) -> p k t h", k=2, t=2)
        bek = col(136, 144).rearrange("p (t h) -> p t h", t=2)
        mxx = col(144, 168).rearrange("p (n k) -> p n k", n=6)
        smx = col(168, 192).rearrange("p (n k) -> p n k", n=6)
        esk = col(192, 216).rearrange("p (n k) -> p n k", n=6)
        eps5, eps6 = col(216, 217), col(217, 218)
        top = col(224, 240).rearrange("p (t k) -> p t k", t=2)
        ntop = col(240, 242)
        tsum = col(242, 244)
        tw = col(244, 252).rearrange("p (t k) -> p t k", t=2)
        idf = col(252, 268).rearrange("p (t k) -> p t k", t=2)

        ident = consts[:, C_ID:C_ID + P]
        ones = consts[:, C_ONES:C_ONES + P]
        inv512 = consts[:, C_I512:C_I512 + P]
        inv128 = consts[:, C_I128:C_I128 + P]

        rel_d = nc.dram_tensor("relative_vector", (8, P, 384), f32)
        rel_toep = bass.AP(rel_d.ap().tensor, 127, [[383, P], [P * 384, 8], [1, 256]])

        bk = [ctx.enter_context(nc.psum_tensor(f"bank{b}", [P, 512], f32))[:, :] for b in range(8)]
        acc = [[bk[0], bk[1]], [bk[2], bk[3]]]
        ka, kb_, kc, kd = bk[4:8]

        filled = [sem(f"bank_filled{b}") for b in range(8)]
        drained = [sem(f"bank_drained{b}") for b in range(8)]
        x_in = [sem(f"x_in{t}") for t in range(ST)]
        params_in, ident_in, wr_in = sem("params_in"), sem("ident_in"), sem("wr_in")
        ln_in = [sem(f"ln_in{k}") for k in range(3)]
        raw_in = [sem(f"raw_in{k}") for k in range(RAW)]
        m_in = sem("m_tile_in")
        lo_ready = [sem(f"lo_ready{k}") for k in range(SPLIT)]
        tile_in = [sem(f"tile_in{k}") for k in range(W1C)]
        w2_in = [[sem(f"w2_in{par}{q}") for q in range(2)] for par in range(2)]
        rel_out, rel_in, store = sem("rel_out"), sem("rel_in"), sem("stored")
        dve_step, act_step, pool_step = sem("dve_step"), sem("act_step"), sem("pool_step")
        names = ("b1_pad b1_high b1_split shift_ready normed hT0_ready hT_split hi_ready pad_zero relvec_sb "
                 "ln_used var_ready sd_ready h_ready hT_ready bgate conv_in conv_out silu_done sq_ready l2_sd "
                 "l2_ready beta_ready aa_ready expu g_ready gcs_ready egc_ready dmin dexp at_ready qk_ready "
                 "kb_ready vb_ready mst_ready t_ready u_ready p1_ready qd_ready cq_ready cv_ready bconv bcent bsq "
                 "bsd bnorm bsilu wT_ready vn_ready oT_ready st_ready osq rms_sd oa_ready ssc_ready pexp pnorm "
                 "pt_ready oc_ready mx_ready h1T_ready top_ready texp comb_ready mask_ready combT_ready "
                 "table_ready mixer_done p_ready gathered xt_ready pt_filled ptw_ready w1_used g_clamped "
                 "sig_ready swish_ready act_ready turned actT_ready y_filled ys_ready all_scattered").split()
        sm = {n: sem(n) for n in names}

        def wait_fill(eng, job):
            eng.wait_ge(filled[BANK[job]], FILL[job])

        def wait_low(eng, n):
            eng.wait_ge(lo_ready[n % SPLIT], n // SPLIT + 1)

        def low(eng, n):
            eng.wait_ge(sm["hi_ready"], n + 1)
            eng.tensor_tensor(w_lo[:, n % SPLIT, :, :], raw_w[:, n % RAW, :].rearrange("p (k c) -> p k c", k=DC),
                              w_hi[:, n % SPLIT, :, :], ALU.subtract).then_inc(lo_ready[n % SPLIT], 1)

        block = ctx.enter_context(nc.Block())

        @block.sync
        def _(sp):
            for t in range(ST):
                sp.dma_start(h[:, t, :], x[t * P:(t + 1) * P, :]).then_inc(x_in[t], 16)

            def load_ln(k):
                sp.dma_start(lngb[:, :, :], bass.AP(lnp.tensor, 2 * D * k, [[0, P], [D, 2], [1, D]])).then_inc(ln_in[k], 16)

            sp.dma_start(consts[:, C_ID:C_ID + P], cst[:, C_ID:C_ID + P]).then_inc(ident_in, 16)
            load_ln(0)

            def load_params():
                sp.dma_start(consts[:, P:N_C], cst[:, P:N_C]).then_inc(params_in, 16)
                sp.dma_start(chp[:, :], chan).then_inc(params_in, 16)
                sp.dma_start(rowp[:, :], bass.AP(rows.tensor, 0, [[0, P], [1, N_R]])).then_inc(params_in, 16)
                sp.dma_start(relw[0:32, :], rel).then_inc(params_in, 16)

            def cols(a, b):
                return w_in[:, a:b].rearrange("(k p) c -> p k c", p=P)

            def load_half(n):
                name = PROJ[n][4:-1]
                if n >= RAW:
                    wait_low(sp, n - RAW)
                dst = raw_w[:, n % RAW, :].rearrange("p (k c) -> p k c", k=DC)
                hh = int(PROJ[n][-1])
                if name == "C":
                    for j in range(2):
                        for g in range(2):
                            a = O_CQ + 256 * g + 64 * (2 * hh + j)
                            sp.dma_start(dst[:, :, 128 * j + 64 * g:128 * j + 64 * g + 64], cols(a, a + 64)).then_inc(raw_in[n % RAW], 16)
                else:
                    base = {"BV": O_BV, "BG": O_BG, "K": O_AK, "Q": O_AQ, "V": O_AV, "Z": O_AZ}.get(name)
                    if base is None:
                        base = O_G + 512 * int(name[1])
                    sp.dma_start(dst, cols(base + 256 * hh, base + 256 * hh + 256)).then_inc(raw_in[n % RAW], 16)

            def load_tile(name):
                n = TILE[name]
                if name == "WB":
                    for m in range(len(PROJ) - SPLIT, len(PROJ)):
                        wait_low(sp, m)
                elif n < W1C:
                    wait_fill(sp, PROJ[-1])
                else:
                    wait_fill(sp, LAST_JOB[TILES[n - W1C]])
                s = n % W1C
                v8 = w1s[:, s, :].rearrange("p (k c) -> p k c", k=DC)
                v4 = w1s[:, s, :].rearrange("p (k c) -> p k c", k=4)
                if name in ("WA", "WB"):
                    src = wa if name == "WA" else wb
                    sp.dma_start(v4, src.rearrange("(k p) c -> p k c", p=P)).then_inc(tile_in[s], 16)
                elif name == "WC":
                    for g in range(2):
                        sp.dma_start(v4[64 * g:64 * g + 64, :, :],
                                     wc[256 * g:256 * g + 256, :].rearrange("(j c) n -> c j n", c=64)).then_inc(tile_in[s], 16)
                else:
                    c = 512 * int(name[2])
                    sp.dma_start(v8, wo[:, c:c + 512].rearrange("(k p) c -> p k c", p=P)).then_inc(tile_in[s], 16)

            for n in range(len(PROJ)):
                load_half(n)
                if n == 1:
                    load_params()
                if n == 2:
                    sp.dma_start(wM[:, :, 0:8], cols(O_AB, O_AB + 8)).then_inc(m_in, 16)
                    sp.dma_start(wM[:, :, 128:384], cols(O_CK, O_CK + 256)).then_inc(m_in, 16)
                if n == 7:
                    sp.wait_ge(sm["relvec_sb"], 1)
                    sp.dma_start(rel_d[:, :, :], relv.rearrange("h (o c) -> h o c", o=1).broadcast_to([8, P, 384])).then_inc(rel_out, 16)
                if n == 15:
                    sp.wait_ge(rel_out, 16)
                    sp.dma_start(bias, rel_toep).then_inc(rel_in, 16)
            for name in TILES:
                load_tile(name)

            def load_w1(e, j):
                s = (NT + j) % W1C
                src = w1[e, 256 * j:256 * j + 256, :] if isinstance(e, int) else \
                    w1[bass.ds(e, 1), 256 * j:256 * j + 256, :].rearrange("o d c -> (o d) c")
                sp.dma_start(w1s[:, s, :].rearrange("p (k c) -> p k c", k=2), src.rearrange("(k p) c -> p k c", p=P)).then_inc(tile_in[s], 16)

            def load_w2(e, par, q):
                dst = (w2s, w2x)[par][:, q, :].rearrange("p (k c) -> p k c", k=4)
                src = w2[e, 512 * q:512 * q + 512, :] if isinstance(e, int) else \
                    w2[bass.ds(e, 1), 512 * q:512 * q + 512, :].rearrange("o d c -> (o d) c")
                sp.dma_start(dst, src.rearrange("(k p) c -> p k c", p=P)).then_inc(w2_in[par][q], 16)

            sp.wait_ge(sm["mixer_done"], 2)
            load_ln(1)
            sp.dma_start(wr, w_router.rearrange("(k p) e -> p k e", p=P)).then_inc(wr_in, 16)
            for k in range(2):
                sp.dma_start(b1w[NE * k:NE * k + NE, :], b1).then_inc(wr_in, 16)
            sp.dma_start(b2s, b2).then_inc(wr_in, 16)
            load_w2(0, 0, 0)
            load_w2(0, 0, 1)
            for j in range(W1C):
                wait_fill(sp, LAST_JOB[TILES[NT - W1C + j]])
                load_w1(0, j)
            sp.wait_ge(sm["ln_used"], 2)
            load_ln(2)
            sp.wait_ge(sm["mask_ready"], 2)
            load_w2(1, 1, 0)
            load_w2(1, 1, 1)
            sp.wait_ge(sm["table_ready"], 1)

            def window_before(e):
                return sp.value_load(tab_i[0:1, bass.ds(e + 2 * NE, 1)], min_val=0, max_val=2 * NE)

            def first_matrix(e):
                last = window_before(e)
                for j in range(W1C):
                    sp.wait_ge(sm["w1_used"], last * 4 + (j + 1))
                    load_w1(e, j)

            def second_matrix(e, par, before):
                sp.wait_ge(sm["y_filled"], before + 1)
                for q in range(2):
                    load_w2(e, par, q)

            first_matrix(1)
            with sp.Fori(1, NE // 2 - 1) as i:
                for par in range(2):
                    second_matrix(i * 2 + par, par, window_before(i * 2 + (par - 1)))
                    first_matrix(i * 2 + par)
            second_matrix(NE - 2, 0, window_before(NE - 3))
            first_matrix(NE - 2)
            first_matrix(NE - 1)
            second_matrix(NE - 1, 1, window_before(NE - 2))
            for t in range(ST):
                sp.wait_ge(sm["h_ready"], 2 * ST + t + 1)
                sp.dma_start(out[t * P:(t + 1) * P, :], h[:, t, :]).then_inc(store, 16)
            sp.wait_ge(store, 16 * ST)

        @block.gpsimd
        def _(pool):
            def level(l):
                if l > 1:
                    wait_fill(pool, f"lp{l - 1}1")
                else:
                    pool.wait_ge(params_in, 64)
                    pool.wait_ge(sm["at_ready"], 2)
                    wait_fill(pool, "vtok1")
                m = consts[:, C_LVL + l * P:C_LVL + (l + 1) * P].rearrange("p (o c) -> p o c", o=1).broadcast_to([P, 8, P])
                pool.tensor_tensor(mst, at, m, ALU.mult).then_inc(sm["mst_ready"], 1)

            for n in range(SPLIT):
                low(pool, n)
            for job in JOBS:
                if job == "projC1":
                    level(1)
                if job in PROJ[:-SPLIT] and PROJ.index(job) + SPLIT not in DVE_LOW:
                    low(pool, PROJ.index(job) + SPLIT)
                if job[:2] == "lp" and job[3] == "1" and int(job[2]) + 1 < LEVELS:
                    level(int(job[2]) + 1)
            pool.wait_ge(sm["mixer_done"], 2)
            pool.memset(b1w[2 * NE:P, :], 0.0).then_inc(sm["b1_pad"], 1)

        @block.scalar
        def _(act):
            def drain(job, ins):
                ins.then_inc(drained[BANK[job]], 1)

            def bank(job):
                wait_fill(act, job)
                return bk[BANK[job]]

            n_act = [0]

            def high(n):
                loads = sum(PARTS.get(PROJ[m], 1) for m in range(n % RAW, n + 1, RAW))
                act.wait_ge(raw_in[n % RAW], 16 * loads)
                if n >= SPLIT:
                    wait_fill(act, PROJ[n - SPLIT])
                nc.scalar.activation(w_hi[:, n % SPLIT, :, :], raw_w[:, n % RAW, :].rearrange("p (k c) -> p k c", k=DC),
                                     ACT.Copy).then_inc(sm["hi_ready"], 1)

            def next_high(job):
                if PROJ.index(job) + SPLIT < len(PROJ):
                    high(PROJ.index(job) + SPLIT)

            def link(ins):
                n_act[0] += 1
                ins.then_inc(act_step, 1)
                act.wait_ge(act_step, n_act[0])

            A = nc.scalar.activation
            act.wait_ge(sm["pad_zero"], 1)

            def layer_norm(k, t):
                act.wait_ge(sm["var_ready"], ST * k + t + 1)
                A(rstd[:, t:t + 1], mv[:, t, 1:2], ACT.Sqrt, bias=eps5).then_inc(sm["sd_ready"], 1)
                act.wait_ge(sm["shift_ready"], ST * k + t + 1)
                A(h[:, t, :], h[:, t, :], ACT.Identity, bias=shift[:, t:t + 1], scale=rstd[:, t:t + 1]).then_inc(sm["normed"], 1)

            for t in range(ST):
                layer_norm(0, t)
            high(0)
            for t in range(ST):
                for hh in range(2):
                    j = f"hT{t}{hh}"
                    b_ = bank(j).rearrange("p (k c) -> p k c", k=4)
                    A(hT_hi[:, 4 * hh:4 * hh + 4, t * P:(t + 1) * P], b_, ACT.Copy).then_inc(sm["hT_ready"], 1)
                    if t == ST - 1 and hh == 0:
                        high(1)
            for t in range(ST):
                for hh in range(2):
                    j = f"hT{t}{hh}"
                    act.wait_ge(sm["hT_split"], 2 * t + hh + 1)
                    link(A(hT0[:, 4 * hh:4 * hh + 4, t * P:(t + 1) * P], bank(j).rearrange("p (k c) -> p k c", k=4), ACT.Copy))
                    act.sem_inc(drained[BANK[j]], 1)
            act.sem_inc(sm["hT0_ready"], 1)
            def proj(job, dst, func=ACT.Copy):
                next_high(job)
                drain(job, A(dst, bank(job).rearrange("p (n c) -> p n c", n=2), func))

            proj("projBV0", bv[:, 0:2, KB - 1:])
            proj("projBV1", bv[:, 2:4, KB - 1:])
            proj("projBG0", bacc[:, 0:2, :], ACT.Sigmoid)
            j = "projBG1"
            next_high(j)
            link(A(bacc[:, 2:4, :], bank(j).rearrange("p (n c) -> p n c", n=2), ACT.Sigmoid))
            act.sem_inc(drained[BANK[j]], 1)
            act.sem_inc(sm["bgate"], 1)
            j = "relvec"
            link(A(relv, bank(j)[0:8, 0:384], ACT.Copy))
            act.sem_inc(drained[BANK[j]], 1)
            act.sem_inc(sm["relvec_sb"], 1)
            j = "ab"
            abv = bank(j)[:, 0:16].rearrange("p (t k h) -> p t k h", t=2, k=2)
            link(A(beta, abv[:, :, 0, :], ACT.Sigmoid))
            link(A(uu.rearrange("p (t h) -> p t h", t=2), abv[:, :, 1, :], ACT.Copy))
            act.sem_inc(drained[BANK[j]], 1)
            act.sem_inc(sm["beta_ready"], 1)
            A(ealog, rowp[:, R_ALOG:R_ALOG + 4], ACT.Exp)
            act.wait_ge(sm["aa_ready"], 1)
            A(yy, au, ACT.Exp, scale=-1.0).then_inc(sm["expu"], 1)
            drain("CK", A(ck, bank("CK")[:, 0:256], ACT.Copy))
            j = "CV"
            link(A(cv, bank(j)[:, 0:256].rearrange("p (b c) -> p b c", b=2), ACT.Copy))
            act.sem_inc(drained[BANK[j]], 1)
            act.sem_inc(sm["cv_ready"], 1)
            act.wait_ge(sm["gcs_ready"], 1)
            A(egc, gcs, ACT.Exp).then_inc(sm["egc_ready"], 1)
            act.wait_ge(sm["dmin"], 2)
            for t in range(ST):
                j = f"grow{t}"
                drain(j, A(eg[:, 4 * t:4 * t + 4, :], bank(j).rearrange("p (n c) -> p n c", n=4), ACT.Exp))
            for t in range(ST):
                j = f"brow{t}"
                drain(j, A(brow[:, 4 * t:4 * t + 4, :], bank(j).rearrange("p (n c) -> p n c", n=4), ACT.Copy))
            link(A(dt_, dt_, ACT.Exp))
            act.sem_inc(sm["dexp"], 1)
            base = {"Q": 0, "K": 4, "V": 8}
            dstT = {"K": kT, "Q": qT, "V": vT}

            def conv_in(x_, split=(0, 1)):
                for hh in range(2):
                    j = f"proj{x_}{hh}"
                    if hh in split:
                        next_high(j)
                    link(A(convin[:, base[x_] + 2 * hh:base[x_] + 2 * hh + 2, KA - 1:], bank(j).rearrange("p (n c) -> p n c", n=2), ACT.Copy))
                    act.sem_inc(drained[BANK[j]], 1)
                act.sem_inc(sm["conv_in"], 1)

            def silu(x_, n):
                act.wait_ge(sm["conv_out"], n)
                link(A(dstT[x_], dstT[x_], ACT.Silu))
                act.sem_inc(sm["silu_done"], 1)

            def l2(x_, n):
                if n > 1:
                    wait_fill(act, "ssK1")
                link(A(sq, dstT[x_], ACT.Square))
                act.sem_inc(sm["sq_ready"], 1)

            def l2_root(x_):
                for hh in range(2):
                    j = f"ss{x_}{hh}"
                    link(A(sq[:, 2 * hh:2 * hh + 2, :], bank(j).rearrange("p (n c) -> p n c", n=2), ACT.Sqrt, bias=eps6))
                    act.sem_inc(drained[BANK[j]], 1)
                act.sem_inc(sm["l2_sd"], 1)

            conv_in("K")
            next_high("projQ0")
            silu("K", 1)
            l2("K", 1)
            conv_in("Q", split=(1,))
            l2_root("K")
            conv_in("V")
            act.wait_ge(sm["l2_ready"], 1)
            silu("Q", 2)
            l2("Q", 2)
            l2_root("Q")

            def gate_z(hh):
                next_high(f"projZ{hh}")
                drain(f"projZ{hh}", A(az[:, 2 * hh:2 * hh + 2, :], bank(f"projZ{hh}").rearrange("p (n c) -> p n c", n=2), ACT.Silu))

            gate_z(0)
            silu("V", 3)
            gate_z(1)
            for hh in range(2):
                j = f"projC{hh}"
                next_high(j)
                link(A(cq[:, 2 * hh:2 * hh + 2, :], bank(j).rearrange("p (n c) -> p n c", n=2), ACT.Copy))
                act.sem_inc(drained[BANK[j]], 1)
            act.sem_inc(sm["cq_ready"], 1)

            def gate(job):
                k = 4 * int(job[5]) + 2 * int(job[6])
                drain(job, A(gates[:, k:k + 2, :], bank(job).rearrange("p (n c) -> p n c", n=2), ACT.Sigmoid))

            def level_p(job):
                t = int(job[3])
                link(A(p1[:, 4 * t:4 * t + 4, :], bank(job).rearrange("p (n c) -> p n c", n=4), ACT.Copy))
                act.sem_inc(drained[BANK[job]], 1)
                act.sem_inc(sm["p1_ready"], 1)

            def w_t(job):
                t = int(job[2])
                link(A(wT[:, 4 * t:4 * t + 4, :], bank(job).rearrange("p (n c) -> p n c", n=4), ACT.Copy, scale=-1.0))
                act.sem_inc(drained[BANK[job]], 1)
                act.sem_inc(sm["wT_ready"], 1)

            def v_new(job):
                r = 64 * (int(job[2]) % 2)
                link(A(vn[r:r + 64, :, :], bank(job)[r:r + 64, :].rearrange("p (n c) -> p n c", n=4), ACT.Copy))
                act.sem_inc(drained[BANK[job]], 1)
                act.sem_inc(sm["vn_ready"], 1)

            def o_t(job):
                n = int(job[2])
                link(A(oaT.rearrange("p a b -> p (a b)").rearrange("p (n c) -> p n c", n=4)[:, :, n * CH:(n + 1) * CH],
                       bank(job)[:, 0:256].rearrange("p (n c) -> p n c", n=4), ACT.Copy))
                act.sem_inc(drained[BANK[job]], 1)
                act.sem_inc(sm["oT_ready"], 1)

            def softmax(n):
                heads, keys = (4, 128) if n < 2 else (2, 256)
                act.wait_ge(sm["ssc_ready"], n + 1)
                for k in range(heads):
                    hd = 4 * n + k if n < 2 else 2 * (n - 2) + k
                    A(ssc[:, n % 2, k * keys:(k + 1) * keys], ssc[:, n % 2, k * keys:(k + 1) * keys], ACT.Exp,
                      bias=mxx[:, n, k:k + 1], accum_out=smx[:, n, k:k + 1])
                    ins = A(esk[:, n, k:k + 1], rowp[:, R_SINK + hd:R_SINK + hd + 1], ACT.Exp, bias=mxx[:, n, k:k + 1])
                ins.then_inc(sm["pexp"], 1)

            def p_t(job):
                n = int(job[2])
                link(A(pts[:, n % 2, :], bank(job), ACT.Copy))
                act.sem_inc(drained[BANK[job]], 1)
                act.sem_inc(sm["pt_ready"], 1)

            def p_v(job):
                n = int(job[2])
                g, j0, nh, q0 = (n, 0, 4, 0) if n < 2 else ((n - 2) // 2, 2 * (n % 2), 2, P)
                r = 64 * g
                link(A(ocT[r:r + 64, j0:j0 + nh, q0:q0 + P], bank(job)[r:r + 64, 0:nh * P].rearrange("p (n c) -> p n c", n=nh), ACT.Copy))
                act.sem_inc(drained[BANK[job]], 1)
                act.sem_inc(sm["oc_ready"], 1)

            def b_var(job):
                drain(job, A(tmpb, bank(job)[:, 0:256], ACT.Sqrt, bias=eps5))
                act.wait_ge(drained[BANK[job]], FILL[job])
                act.sem_inc(sm["bsd"], 1)

            def b_silu():
                act.wait_ge(sm["bnorm"], 1)
                for c in range(NB):
                    ins = A(bacc[:, c, :], bacc[:, c, :], ACT.Silu, bias=chp[:, H_BN + c:H_BN + c + 1], scale=chp[:, H_BG + c:H_BG + c + 1])
                ins.then_inc(sm["bsilu"], 1)

            def b_square(job):
                act.wait_ge(sm["bcent"], 1)
                A(bv[:, :, 0:S], bacc, ACT.Square).then_inc(sm["bsq"], 1)

            steps = {"projG": gate, "lp": level_p, "wT": w_t, "vn": v_new, "oT": o_t, "pt": p_t, "pv": p_v, "bvar": b_var, "bmean": b_square}
            first = JOBS.index("lp10")
            for n, job in enumerate(JOBS[first:JOBS.index("rms0")]):
                for key, step in steps.items():
                    if job.startswith(key):
                        step(job)
                if job.startswith("sc"):
                    softmax(int(job[2]))
                if job == "pt4":
                    b_silu()
                before = JOBS[first + n - 2]
                if before in PROJ[14:20]:
                    next_high(before)
                if job in PROJ[20:]:
                    next_high(job)
            act.wait_ge(sm["oT_ready"], 4)
            link(A(sq, oaT.rearrange("p a b -> p (a b)").rearrange("p (n c) -> p n c", n=4), ACT.Square))
            act.sem_inc(sm["osq"], 1)
            for hh in range(2):
                j = f"rms{hh}"
                link(A(sq[:, 2 * hh:2 * hh + 2, :], bank(j).rearrange("p (n c) -> p n c", n=2), ACT.Sqrt, bias=eps6))
                act.sem_inc(drained[BANK[j]], 1)
            act.sem_inc(sm["rms_sd"], 1)
            act.sem_inc(sm["mixer_done"], 1)
            act.wait_ge(wr_in, 64)
            act.wait_ge(sm["b1_pad"], 1)
            A(b1p, b1w, ACT.Copy).then_inc(sm["b1_high"], 1)
            for t in range(ST):
                layer_norm(1, t)
                for hh in range(2):
                    j = f"h1T{t}{hh}"
                    link(A(hT[:, 4 * hh:4 * hh + 4, t * P:(t + 1) * P], bank(j).rearrange("p (k c) -> p k c", k=4), ACT.Copy))
                    act.sem_inc(drained[BANK[j]], 1)
                    act.sem_inc(sm["h1T_ready"], 1)
            for t in range(ST):
                act.wait_ge(sm["top_ready"], t + 1)
                A(tw[:, t, :], top[:, t, 0:4], ACT.Exp, bias=ntop[:, t:t + 1], accum_out=tsum[:, t:t + 1]).then_inc(sm["texp"], 1)
            act.wait_ge(sm["table_ready"], 1)

            def window(g, width):
                for k, wk in enumerate((kc, kd)):
                    act.wait_ge(sm["gathered"], g * 2 + (k + 1))
                    A(xT[:, 4 * k:4 * k + 4, 0:width], wk[:, 0:4 * width].rearrange("p (n c) -> p n c", n=4), ACT.Copy).then_inc(sm["xt_ready"], 1)
                n = 256 if width == NARROW else 512
                for k in range(2):
                    act.wait_ge(sm["g_clamped"], g * 2 + (k + 1))
                    A(sg[:, k, 0:n], gm[:, k, 0:n], ACT.Sigmoid, scale=1.702).then_inc(sm["sig_ready"], 1)
                for k in range(2):
                    act.wait_ge(sm["turned"], g * 2 + (k + 1))
                    if width == NARROW:
                        dst = actT.rearrange("p (u j) c -> p j u c", u=2)[:, 2 * k:2 * k + 2, :, 0:NARROW]
                        src = (kb_, ka)[k][:, 0:256].rearrange("p (j u c) -> p j u c", j=2, u=2)
                    else:
                        dst = actT[:, 4 * k:4 * k + 4, :]
                        src = (ka, kc)[k].rearrange("p (j c) -> p j c", j=4)
                    A(dst, src, ACT.Copy).then_inc(sm["actT_ready"], 1)
                act.wait_ge(sm["y_filled"], g + 1)
                for k in range(2):
                    src = kd[64 * k:64 * k + 64, :] if width == NARROW else (kb_, kd)[k][:, :]
                    A(ys[0:width, 512 * k:512 * k + 512], src, ACT.Copy).then_inc(sm["ys_ready"], 1)

            with act.Fori(0, NE // 2) as i:
                for par in range(2):
                    g0 = act.value_load(tab_i[0:1, bass.ds(i * 2 + par, 1)], min_val=0, max_val=2 * NE)
                    cnt = act.value_load(tab_i[0:1, bass.ds(i * 2 + (par + NE), 1)], min_val=0, max_val=S)
                    with act.If(cnt > WIDE):
                        window(g0, WIDE)
                        window(g0 + 1, WIDE)
                    with act.Else():
                        with act.If(cnt > NARROW):
                            window(g0, WIDE)
                        with act.Else():
                            window(g0, NARROW)
            for t in range(ST):
                layer_norm(2, t)

        @block.vector
        def _(dve):
            V = nc.vector
            n_dve = [0]

            def link(ins):
                n_dve[0] += 1
                ins.then_inc(dve_step, 1)
                dve.wait_ge(dve_step, n_dve[0])

            def signal(ins, *sems):
                link(ins)
                for s in sems:
                    dve.sem_inc(s, 1)

            def bank(job):
                wait_fill(dve, job)
                return bk[BANK[job]]

            def moments(k, t):
                for q in range(2):
                    V.bn_stats(stats[:, t, q, :], h[:, t, 512 * q:512 * q + 512]).then_inc(dve_step, 1)
                    n_dve[0] += 1
                dve.wait_ge(dve_step, n_dve[0])
                V.bn_aggr(mv[:, t, :], stats[:, t, :, :].rearrange("p a b -> p (a b)")).then_inc(sm["var_ready"], 1)
                dve.wait_ge(sm["sd_ready"], ST * k + t + 1)
                link(V.reciprocal(rstd[:, t:t + 1], rstd[:, t:t + 1]))
                V.scalar_tensor_tensor(shift[:, t:t + 1], mv[:, t, 0:1], -1.0, rstd[:, t:t + 1], ALU.mult, ALU.mult).then_inc(sm["shift_ready"], 1)

            def gain(k, t):
                dve.wait_ge(ln_in[k], 16)
                dve.wait_ge(sm["normed"], ST * k + t + 1)
                link(V.tensor_tensor(h[:, t, :], h[:, t, :], lngb[:, 0, :], ALU.mult))
                signal(V.tensor_tensor(h[:, t, :], h[:, t, :], lngb[:, 1, :], ALU.add), sm["h_ready"])
                if t == ST - 1:
                    dve.sem_inc(sm["ln_used"], 1)

            link(V.memset(small[:, :], 0.0))
            V.memset(eps5, 1e-5)
            V.memset(eps6, 1e-6)
            V.memset(relw[32:33, :], -1e30)
            signal(V.memset(convin[:, :, 0:KA - 1], 0.0), sm["pad_zero"])
            for t in range(ST):
                dve.wait_ge(x_in[t], 16)
                moments(0, t)
            for t in range(ST):
                gain(0, t)
            for t in range(ST):
                for hh in range(2):
                    dve.wait_ge(sm["hT_ready"], 2 * t + hh + 1)
                    V.tensor_tensor(hT_lo[:, 4 * hh:4 * hh + 4, t * P:(t + 1) * P], bank(f"hT{t}{hh}").rearrange("p (k c) -> p k c", k=4),
                                    hT_hi[:, 4 * hh:4 * hh + 4, t * P:(t + 1) * P], ALU.subtract).then_inc(sm["hT_split"], 1)
            signal(V.memset(bv[:, :, 0:KB - 1], 0.0))
            dve.wait_ge(params_in, 64)
            for n in range(2, 6):
                low(dve, n)
            dve.wait_ge(sm["bgate"], 1)
            link(V.tensor_tensor(bv[:, :, KB - 1:], bv[:, :, KB - 1:], bacc, ALU.mult))
            dve.wait_ge(sm["beta_ready"], 1)
            v42 = "p (t h) -> p t h"
            dtb = rowp[:, R_DT:R_DT + 4].rearrange("p (o h) -> p o h", o=1).broadcast_to([P, 2, 4])
            link(V.tensor_tensor(uu.rearrange(v42, t=2), uu.rearrange(v42, t=2), dtb, ALU.add))
            link(V.tensor_scalar(au, uu, -1.0, None, ALU.mult))
            signal(V.tensor_tensor(au, au, uu, ALU.max), sm["aa_ready"])
            dve.wait_ge(sm["expu"], 1)
            link(V.tensor_scalar(ss, yy, 2.0, None, ALU.add))
            link(V.reciprocal(ss, ss))
            link(V.tensor_tensor(ss, ss, yy, ALU.mult))
            link(V.tensor_tensor(s2, ss, ss, ALU.mult))
            link(V.tensor_scalar(po, s2, 1.0 / 17, 1.0 / 15, ALU.mult, ALU.add))
            for k in (13, 11, 9, 7, 5, 3, 1):
                link(V.tensor_tensor(po, po, s2, ALU.mult))
                link(V.tensor_scalar(po, po, 1.0 / k, None, ALU.add))
            link(V.scalar_tensor_tensor(po, po, 2.0, ss, ALU.mult, ALU.mult))
            link(V.scalar_tensor_tensor(po, uu, 0.0, po, ALU.max, ALU.add))
            eal = ealog.rearrange("p (o h) -> p o h", o=1).broadcast_to([P, 2, 4])
            signal(V.scalar_tensor_tensor(gg, po.rearrange(v42, t=2), -1.0, eal, ALU.mult, ALU.mult), sm["g_ready"])
            j = "gcol"
            signal(V.tensor_copy(gcs, bank(j)[:, 0:16].rearrange("p (k t h) -> p k t h", k=2, t=2)),
                   sm["gcs_ready"], drained[BANK[j]])
            strict = consts[:, C_STR:C_STR + P]
            for t in range(ST):
                b_ = bank(f"grow{t}")
                for hh in range(AH):
                    link(V.scalar_tensor_tensor(dt_[:, 4 * t + hh, :], b_[:, hh * P:(hh + 1) * P], gcs[:, 0, t, hh:hh + 1],
                                                strict, ALU.subtract, ALU.mult))
                signal(V.tensor_scalar(dt_[:, 4 * t:4 * t + 4, :], dt_[:, 4 * t:4 * t + 4, :], 0.0, None, ALU.min), sm["dmin"])
            dve.wait_ge(sm["egc_ready"], 1)
            link(V.tensor_tensor(bek, beta, egc[:, 0], ALU.mult))

            n_conv = [0]

            def conv_a(x_, k0, dstT):
                dve.wait_ge(sm["conv_in"], n_conv[0] + 1)
                for c in range(4):
                    w = chp[:, H_ACW + (k0 + c) * KA:H_ACW + (k0 + c + 1) * KA]
                    V.tensor_scalar(dstT[:, c, :], convin[:, k0 + c, 0:S], w[:, 0:1], None, ALU.mult).then_inc(dve_step, 1)
                n_dve[0] += 4
                for k in range(1, KA):
                    for c in range(4):
                        w = chp[:, H_ACW + (k0 + c) * KA:H_ACW + (k0 + c + 1) * KA]
                        dve.wait_ge(dve_step, n_dve[0] - 3)
                        V.scalar_tensor_tensor(dstT[:, c, :], convin[:, k0 + c, k:k + S], w[:, k:k + 1], dstT[:, c, :],
                                               ALU.mult, ALU.add).then_inc(dve_step, 1)
                        n_dve[0] += 1
                dve.wait_ge(dve_step, n_dve[0])
                n_conv[0] += 1
                dve.sem_inc(sm["conv_out"], 1)

            def l2(dstT, n, scale):
                dve.wait_ge(sm["l2_sd"], n)
                link(V.reciprocal(sq, sq))
                signal(V.scalar_tensor_tensor(dstT, dstT, scale, sq, ALU.mult, ALU.mult), sm["l2_ready"])

            taps = [(k, c) for k in range(KB) for c in range(NB)]
            sem_conv = sm["bconv"]
            done = [0]

            def conv_b(count):
                for k, c in taps[done[0]:done[0] + count]:
                    w = chp[:, H_BW + c * KB + k:H_BW + c * KB + k + 1]
                    if k == 0:
                        V.tensor_scalar(bacc[:, c, :], bv[:, c, 0:S], w, chp[:, H_BB + c:H_BB + c + 1], ALU.mult, ALU.add).then_inc(sem_conv, 1)
                    else:
                        dve.wait_ge(sem_conv, done[0] - 3)
                        V.scalar_tensor_tensor(bacc[:, c, :], bv[:, c, k:k + S], w, bacc[:, c, :], ALU.mult, ALU.add).then_inc(sem_conv, 1)
                    done[0] += 1
                    if done[0] == len(taps):
                        dve.wait_ge(sem_conv, len(taps))
                        dve.sem_inc(sm["conv_out"], 1)

            conv_b(8)
            low(dve, 6)
            conv_b(8)
            conv_a("K", 4, kT)
            conv_b(15)
            conv_a("Q", 0, qT)
            l2(kT, 1, 1.0)
            dve.wait_ge(sm["dexp"], 1)
            incl = consts[:, C_TRI:C_TRI + P].rearrange("p (o c) -> p o c", o=1).broadcast_to([P, 8, P])
            link(V.tensor_tensor(dt_, dt_, incl, ALU.mult))
            conv_a("V", 8, vT)
            l2(qT, 2, 128 ** -0.5)
            for t in range(ST):
                j = f"kk{t}"
                link(V.tensor_tensor(at[:, 4 * t:4 * t + 4, :], bank(j).rearrange("p (n c) -> p n c", n=4), brow[:, 4 * t:4 * t + 4, :], ALU.mult))
                dve.sem_inc(drained[BANK[j]], 1)
                signal(V.tensor_tensor(at[:, 4 * t:4 * t + 4, :], at[:, 4 * t:4 * t + 4, :], dt_[:, 4 * t:4 * t + 4, :], ALU.mult), sm["at_ready"])
            m0 = consts[:, C_LVL:C_LVL + P].rearrange("p (o c) -> p o c", o=1).broadcast_to([P, 8, P])
            idb = ident.rearrange("p (o c) -> p o c", o=1).broadcast_to([P, 8, P])
            link(V.tensor_tensor(um, at, m0, ALU.mult))
            signal(V.tensor_tensor(um, idb, um, ALU.subtract), sm["u_ready"])
            for t in range(ST):
                j = f"ktok{t}"
                b_ = bank(j).rearrange("p (n c) -> p n c", n=4)
                V.tensor_tensor(kbt[:, 4 * t:4 * t + 4, :], b_, bek[:, t, :].rearrange("p (h o) -> p h o", o=1).broadcast_to([P, 4, P]), ALU.mult)
                signal(V.tensor_tensor(kdt[:, 4 * t:4 * t + 4, :], b_, egc[:, 1, t, :].rearrange("p (h o) -> p h o", o=1).broadcast_to([P, 4, P]), ALU.mult),
                       drained[BANK[j]], sm["kb_ready"])
            for t in range(ST):
                j = f"qk{t}"
                signal(V.tensor_tensor(dt_[:, 4 * t:4 * t + 4, :], bank(j).rearrange("p (n c) -> p n c", n=4), dt_[:, 4 * t:4 * t + 4, :], ALU.mult),
                       drained[BANK[j]], sm["qk_ready"])
            for t in range(ST):
                signal(V.tensor_tensor(qT[:, :, t * P:(t + 1) * P], qT[:, :, t * P:(t + 1) * P], eg[:, 4 * t:4 * t + 4, :], ALU.mult), sm["qd_ready"])
            for t in range(ST):
                j = f"vtok{t}"
                signal(V.tensor_tensor(vbt[:, 4 * t:4 * t + 4, :], bank(j).rearrange("p (n c) -> p n c", n=4),
                                       beta[:, t, :].rearrange("p (h o) -> p h o", o=1).broadcast_to([P, 4, P]), ALU.mult),
                       drained[BANK[j]], sm["vb_ready"])
            for t in range(ST):
                j = f"trT{t}"
                signal(V.tensor_copy(tm[:, 4 * t:4 * t + 4, :], bank(j).rearrange("p (n c) -> p n c", n=4)), drained[BANK[j]], sm["t_ready"])

            def level(job, buf, ready):
                t = int(job[3])
                v = buf[:, 4 * t:4 * t + 4, :]
                signal(V.tensor_tensor(v, v, bank(job).rearrange("p (n c) -> p n c", n=4), ALU.subtract), drained[BANK[job]], sm[ready])

            def scores(n):
                heads, keys = (4, 128) if n < 2 else (2, 256)
                job = f"sc{n}"
                if n >= 2:
                    wait_fill(dve, f"pt{n - 2}")
                b_ = bank(job)[:, 0:heads * keys].rearrange("p (n c) -> p n c", n=heads)
                s_ = ssc[:, n % 2, :].rearrange("p (n c) -> p n c", n=heads)
                h0 = 4 * n if n < 2 else 2 * (n - 2)
                if n == 0:
                    dve.wait_ge(rel_in, 16)
                signal(V.scalar_tensor_tensor(s_, b_, HD ** -0.5, bias[:, h0:h0 + heads, 256 - keys:256], ALU.mult, ALU.add), drained[BANK[job]])
                link(V.tensor_reduce(mxx[:, n, 0:heads], s_, AX.X, ALU.max))
                link(V.tensor_tensor(mxx[:, n, 0:heads], mxx[:, n, 0:heads], rowp[:, R_SINK + h0:R_SINK + h0 + heads], ALU.max))
                signal(V.tensor_scalar(mxx[:, n, 0:heads], mxx[:, n, 0:heads], -1.0, None, ALU.mult), sm["ssc_ready"])
                conv_b(4)

            def normalise(n):
                heads, keys = (4, 128) if n < 2 else (2, 256)
                s_ = ssc[:, n % 2, :].rearrange("p (n c) -> p n c", n=heads)
                dve.wait_ge(sm["pexp"], n + 1)
                link(V.tensor_tensor(smx[:, n, 0:heads], smx[:, n, 0:heads], esk[:, n, 0:heads], ALU.add))
                link(V.reciprocal(smx[:, n, 0:heads], smx[:, n, 0:heads]))
                signal(V.tensor_tensor(s_, s_, smx[:, n, 0:heads].rearrange("p (h o) -> p h o", o=1).broadcast_to([P, heads, keys]), ALU.mult), sm["pnorm"])

            def state(n):
                job = f"dS{n}"
                t, r = n // 2, n % 2
                if n == 0:
                    signal(V.tensor_copy(st, bank(job).rearrange("p (n c) -> p n c", n=4)), drained[BANK[job]], sm["st_ready"])
                    return
                for hh in range(AH):
                    ins = V.scalar_tensor_tensor(st[:, hh, :], st[:, hh, :], eg[:, 4 * t + hh, 64 * r + 63:64 * r + 64],
                                                 bank(job)[:, hh * P:(hh + 1) * P], ALU.mult, ALU.add)
                signal(ins, drained[BANK[job]], sm["st_ready"])

            def merge(br, b, q):
                job = f"y{br}{q}"
                g_ = gates[:, 8 * b + 2 * q:8 * b + 2 * q + 2, :]
                b_ = bank(job).rearrange("p (n c) -> p n c", n=2)
                dst = mxT[:, 2 * q:2 * q + 2, :]
                if br == "B":
                    signal(V.tensor_tensor(dst, b_, g_, ALU.mult), drained[BANK[job]])
                else:
                    signal(V.tensor_tensor(g_, b_, g_, ALU.mult), drained[BANK[job]])
                    signal(V.tensor_tensor(dst, dst, g_, ALU.add), *([sm["mx_ready"]] if br == "A" else []))

            waiting = []
            for job in JOBS[JOBS.index("lp10"):JOBS.index("rms0")]:
                if job[0] == "y":
                    merge("B", 1, int(job[2]))
                elif job[:2] == "lt":
                    level(job, tm, "t_ready")
                elif job[:2] == "lu":
                    level(job, um, "u_ready")
                elif job[:5] == "projG":
                    conv_b(9)
                elif job[:2] == "sc":
                    n = int(job[2])
                    scores(n)
                    for m in waiting + ([n] if n == 5 else []):
                        normalise(m)
                    waiting = [n] if n < 5 else []
                elif job[:2] == "dS":
                    state(int(job[2]))
                    for m in waiting:
                        normalise(m)
                    waiting = []
                elif job == "bmean":
                    b_ = bank(job)[:, 0:256].rearrange("p (o c) -> p o c", o=1).broadcast_to([P, 4, 256])
                    signal(V.tensor_tensor(bacc, bacc, b_, ALU.subtract), drained[BANK[job]], sm["bcent"])
                elif job == "bvar":
                    dve.wait_ge(sm["bsd"], 1)
                    link(V.reciprocal(tmpb, tmpb))
                    signal(V.tensor_tensor(bacc, bacc, tmpb.rearrange("p (o c) -> p o c", o=1).broadcast_to([P, 4, 256]), ALU.mult), sm["bnorm"])

            dve.wait_ge(sm["rms_sd"], 1)
            oa4 = oaT.rearrange("p a b -> p (a b)").rearrange("p (n c) -> p n c", n=4)
            link(V.reciprocal(sq, sq))
            link(V.tensor_tensor(oa4, oa4, sq, ALU.mult))
            signal(V.scalar_tensor_tensor(oa4, oa4, chp[:, H_AN:H_AN + 1], az, ALU.mult, ALU.mult), sm["oa_ready"], sm["mixer_done"])
            for q in range(4):
                merge("C", 2, q)
            for q in range(4):
                merge("A", 0, q)
            dve.wait_ge(sm["b1_high"], 1)
            V.tensor_tensor(b1p[NE:2 * NE, :], b1w[NE:2 * NE, :], b1p[NE:2 * NE, :], ALU.subtract).then_inc(sm["b1_split"], 1)
            V.memset(ys, 0.0)
            signal(V.memset(ptw, 0.0))
            dve.sem_inc(sm["ys_ready"], 2)
            dve.sem_inc(sm["ptw_ready"], 1)
            for t in range(ST):
                for hf in range(2):
                    job = f"mix{t}{hf}"
                    v = h[:, t, 512 * hf:512 * hf + 512]
                    signal(V.scalar_tensor_tensor(v, v, ALPHA, bank(job), ALU.mult, ALU.add), drained[BANK[job]])
                moments(1, t)
                gain(1, t)
            dve.wait_ge(wr_in, 64)
            io = consts[:, C_IOTA0:C_IOTA0 + NE]
            for t in range(ST):
                j = f"router{t}"
                signal(V.tensor_tensor(lg[:, t, :], bank(j)[:, 0:NE], rowp[:, R_BR:R_BR + NE], ALU.add), drained[BANK[j]])
                link(V.max(top[:, t, :], lg[:, t, :]))
                link(V.max_index(idx[:, t, :], top[:, t, :], lg[:, t, :]))
                link(V.tensor_copy(idf[:, t, :], idx[:, t, :]))
                signal(V.tensor_scalar(ntop[:, t:t + 1], top[:, t, 0:1], -1.0, None, ALU.mult), sm["top_ready"])
                link(V.tensor_scalar(mask[:, t, :], io, idf[:, t, 0:1], None, ALU.is_equal))
                for k in range(1, 4):
                    link(V.scalar_tensor_tensor(mask[:, t, :], io, idf[:, t, k:k + 1], mask[:, t, :], ALU.is_equal, ALU.add))
                dve.sem_inc(sm["mask_ready"], 1)
                dve.wait_ge(sm["texp"], t + 1)
                link(V.reciprocal(tsum[:, t:t + 1], tsum[:, t:t + 1]))
                link(V.tensor_scalar(tw[:, t, :], tw[:, t, :], tsum[:, t:t + 1], None, ALU.mult))
                link(V.tensor_scalar(comb[:, t, :], io, idf[:, t, 0:1], tw[:, t, 0:1], ALU.is_equal, ALU.mult))
                for k in range(1, 4):
                    link(V.tensor_scalar(oneh[:, t, :], io, idf[:, t, k:k + 1], tw[:, t, k:k + 1], ALU.is_equal, ALU.mult))
                    link(V.tensor_tensor(comb[:, t, :], comb[:, t, :], oneh[:, t, :], ALU.add))
            dve.sem_inc(sm["comb_ready"], 1)
            j = "combT"
            signal(V.tensor_copy(combTs, bank(j)[0:NE, 0:256].rearrange("p (t c) -> p t c", t=2)), drained[BANK[j]], sm["combT_ready"])
            j = "rank"
            link(V.scalar_tensor_tensor(rk[:, 0], bank(j)[:, 0:2 * NE].rearrange("p (t e) -> p t e", t=2), 1.0, mask, ALU.add, ALU.mult))
            dve.sem_inc(drained[BANK[j]], 1)
            link(V.tensor_scalar(rk[:, 1], rk[:, 0], float(WIDE), None, ALU.subtract))
            j = "count"
            link(V.tensor_copy(tabf[:, 1, :], bank(j)[0:1, 0:NE]))
            dve.sem_inc(drained[BANK[j]], 1)
            link(V.tensor_copy(tab_i[0:1, NE:2 * NE], tabf[:, 1, :]))
            link(V.tensor_scalar(tabf[:, 2, :], tabf[:, 1, :], float(WIDE), 1.0, ALU.is_gt, ALU.add))
            link(V.memset(tabf[:, 3, :], 1.0))
            link(V.tensor_tensor_scan(tabf[:, 0, :], tabf[:, 3, :], tabf[:, 2, :], 0.0, ALU.mult, ALU.add))
            link(V.tensor_copy(tab_i[0:1, 3 * NE:3 * NE + 1], tabf[:, 0, NE - 1:NE]))
            link(V.tensor_tensor(tabf[:, 0, :], tabf[:, 0, :], tabf[:, 2, :], ALU.subtract))
            link(V.tensor_copy(tab_i[0:1, 0:NE], tabf[:, 0, :]))
            link(V.tensor_scalar(tabf[:, 0, :], tabf[:, 0, :], -1.0, 0.0, ALU.add, ALU.max))
            link(V.tensor_copy(tab_i[0:1, 2 * NE:3 * NE], tabf[:, 0, :]))
            dve.sem_inc(sm["table_ready"], 1)
            io1 = consts[:, C_IOTA1:C_IOTA1 + P]

            def window(e, g, width, part):
                for t in range(ST):
                    V.tensor_scalar(pg[:, t, :], io1, rk[:, part, t, bass.ds(e, 1)], None, ALU.is_equal)
                    V.tensor_scalar(pw[:, t, :], io1, rk[:, part, t, bass.ds(e, 1)], comb[:, t, bass.ds(e, 1)], ALU.is_equal, ALU.mult)
                V.tensor_copy(pick, consts[:, bass.ds(e + C_PICK, 1)].broadcast_to([P, P])).then_inc(sm["p_ready"], 1)
                dve.wait_ge(sm["w1_used"], g * 4 + 4)
                n = 256 if width == NARROW else 512
                parts = [(ka[:, 0:256], kc[:, 0:256]), (ka[:, 256:512], kc[:, 256:512])] if width == NARROW else [(ka, kc), (kb_, kd)]
                for k in range(2):
                    V.tensor_scalar(gm[:, k, 0:n], parts[k][0], 7.0, None, ALU.min).then_inc(sm["g_clamped"], 1)
                for k in range(2):
                    V.tensor_scalar(ln_[:, k, 0:n], parts[k][1], 7.0, -7.0, ALU.min, ALU.max)
                    dve.wait_ge(sm["sig_ready"], g * 2 + (k + 1))
                    V.tensor_tensor(gm[:, k, 0:n], gm[:, k, 0:n], sg[:, k, 0:n], ALU.mult).then_inc(sm["swish_ready"], 1)
                    dve.wait_ge(sm["swish_ready"], g * 2 + (k + 1))
                    V.scalar_tensor_tensor(act_tok[:, n * k:n * k + n], ln_[:, k, 0:n], 1.0, gm[:, k, 0:n], ALU.add, ALU.mult).then_inc(sm["act_ready"], 1)
                dve.wait_ge(sm["pt_filled"], g + 1)
                V.tensor_copy(ptw, (kd if width == NARROW else ka)[:, 0:256].rearrange("p (t c) -> p t c", t=2)).then_inc(sm["ptw_ready"], 1)

            with dve.Fori(0, NE // 2) as i:
                for par in range(2):
                    g0 = dve.value_load(tab_i[0:1, bass.ds(i * 2 + par, 1)], min_val=0, max_val=2 * NE)
                    cnt = dve.value_load(tab_i[0:1, bass.ds(i * 2 + (par + NE), 1)], min_val=0, max_val=S)
                    e = i * 2 + par
                    with dve.If(cnt > WIDE):
                        window(e, g0, WIDE, 0)
                        window(e, g0 + 1, WIDE, 1)
                    with dve.Else():
                        with dve.If(cnt > NARROW):
                            window(e, g0, WIDE, 0)
                        with dve.Else():
                            window(e, g0, NARROW, 0)
            for t in range(ST):
                dve.wait_ge(sm["all_scattered"], t + 1)
                for k in range(2):
                    v = h[:, t, 512 * k:512 * k + 512]
                    link(V.scalar_tensor_tensor(v, v, ALPHA, acc[t][k][:, :], ALU.mult, ALU.add))
                moments(2, t)
            for t in range(ST):
                gain(2, t)

        @block.tensor
        def _(pe):
            mm = nc.tensor.matmul

            def tr(o, i):
                return nc.tensor.transpose(o, i, ident)

            def open_bank(job):
                if FILL[job] > 1:
                    pe.wait_ge(drained[BANK[job]], FILL[job] - 1)
                return bk[BANK[job]]

            def close(job, ins):
                ins.then_inc(filled[BANK[job]], 1)

            def keep_warm(b, count):
                for _ in range(count):
                    mm(b, lhsT=ident, rhs=consts[:, 0:512], start=True, stop=True)

            def tile(name):
                s = TILE[name] % W1C
                pe.wait_ge(tile_in[s], 16 * sum(2 if m == "WC" else 1 for m in TILES[s:TILE[name] + 1:W1C]))
                return w1s[:, s, :]

            tile_total = [sum(2 if m == "WC" else 1 for m in TILES[s::W1C]) for s in range(W1C)]

            def proj(job):
                n = PROJ.index(job)
                wait_low(pe, n)
                if n == 0:
                    pe.wait_ge(sm["hT_split"], 4)
                b = open_bank(job)
                hi, lo = w_hi[:, n % SPLIT, :, :], w_lo[:, n % SPLIT, :, :]
                hi, lo = (v.rearrange("p k (j c) -> p k j c", j=2) for v in (hi, lo))
                for j in range(2):
                    for k in range(DC):
                        o = b[:, j * S:(j + 1) * S]
                        mm(o, lhsT=hi[:, k, j], rhs=hT_hi[:, k, :], start=k == 0, stop=False)
                        mm(o, lhsT=hi[:, k, j], rhs=hT_lo[:, k, :], start=False, stop=False)
                        ins = mm(o, lhsT=lo[:, k, j], rhs=hT_hi[:, k, :], start=False, stop=k == DC - 1)
                close(job, ins)

            for job in JOBS:
                if job[:2] == "hT" or job[:3] == "h1T":
                    t, hh = int(job[-2]), int(job[-1])
                    if job == "h1T10":
                        keep_warm(open_bank(job), 3)
                    pe.wait_ge(ident_in, 16)
                    pe.wait_ge(sm["h_ready"], t + 1 + (ST if job[1] == "1" else 0))
                    b = open_bank(job)
                    for k in range(4):
                        ins = tr(b[:, k * P:(k + 1) * P], h[:, t, (4 * hh + k) * P:(4 * hh + k + 1) * P])
                    close(job, ins)
                elif job == "relvec":
                    pe.wait_ge(sm["pad_zero"], 1)
                    pe.wait_ge(params_in, 64)
                    close(job, mm(open_bank(job)[0:8, 0:384], lhsT=relw[:, :], rhs=consts[0:33, C_OH:C_OH + 384], start=True, stop=True))
                elif job[:4] == "proj":
                    proj(job)
                elif job == "ab":
                    pe.wait_ge(m_in, 32)
                    pe.wait_ge(sm["hT0_ready"], 1)
                    b = open_bank(job)
                    for t in range(ST):
                        for k in range(DC):
                            ins = mm(b[:, 8 * t:8 * t + 8], lhsT=hT0[:, k, t * P:(t + 1) * P], rhs=wM[:, k, 0:8], start=k == 0, stop=k == DC - 1)
                    close(job, ins)
                elif job == "CK":
                    b = open_bank(job)
                    for k in range(DC):
                        ins = mm(b[:, 0:S], lhsT=wM[:, k, P:2 * P], rhs=hT0[:, k, :], start=k == 0, stop=k == DC - 1)
                    close(job, ins)
                elif job == "CV":
                    b = open_bank(job)
                    for t in range(ST):
                        for k in range(DC):
                            ins = mm(b[:, P * t:P * t + P], lhsT=hT0[:, k, t * P:(t + 1) * P], rhs=wM[:, k, 2 * P:3 * P], start=k == 0, stop=k == DC - 1)
                    close(job, ins)
                elif job == "gcol":
                    pe.wait_ge(sm["g_ready"], 1)
                    b = open_bank(job)
                    for k, m in enumerate((C_TRI, C_SUF)):
                        for t in range(ST):
                            ins = mm(b[:, 8 * k + 4 * t:8 * k + 4 * t + 4], lhsT=consts[:, m:m + P], rhs=gg[:, t, :], start=True, stop=True)
                    close(job, ins)
                elif job[:4] in ("grow", "brow"):
                    t = int(job[4])
                    b = open_bank(job)
                    src, m = (gg, C_TRI) if job[0] == "g" else (beta, C_ID)
                    for hh in range(AH):
                        ins = mm(b[:, hh * P:(hh + 1) * P], lhsT=src[:, t, hh:hh + 1].broadcast_to([P, P]), rhs=consts[:, m:m + P], start=True, stop=True)
                    close(job, ins)
                elif job[:2] == "ss":
                    hh = int(job[3])
                    pe.wait_ge(sm["sq_ready"], 1 if job[2] == "K" else 2)
                    b = open_bank(job)
                    close(job, mm(b[:, :], lhsT=ones, rhs=sq[:, 2 * hh:2 * hh + 2, :], start=True, stop=True))
                elif job[:2] in ("kk", "qk"):
                    t = int(job[2])
                    pe.wait_ge(sm["l2_ready"], 1 if job[0] == "k" else 2)
                    b = open_bank(job)
                    for hh in range(AH):
                        tt = slice(t * P, (t + 1) * P)
                        ins = mm(b[:, hh * P:(hh + 1) * P], lhsT=kT[:, hh, tt], rhs=(kT if job[0] == "k" else qT)[:, hh, tt], start=True, stop=True)
                    close(job, ins)
                elif job[1:4] == "tok":
                    t = int(job[4])
                    if job[0] == "v":
                        pe.wait_ge(sm["silu_done"], 3)
                    b = open_bank(job)
                    for hh in range(AH):
                        ins = tr(b[:, hh * P:(hh + 1) * P], (kT if job[0] == "k" else vT)[:, hh, t * P:(t + 1) * P])
                    close(job, ins)
                elif job[:3] == "trT":
                    t = int(job[3])
                    pe.wait_ge(sm["u_ready"], 1)
                    b = open_bank(job)
                    for hh in range(AH):
                        ins = tr(b[:, hh * P:(hh + 1) * P], um[:, 4 * t + hh, :])
                    close(job, ins)
                elif job[:2] in ("lp", "lt", "lu"):
                    l, t = int(job[2]), int(job[3])
                    if job[1] == "p":
                        pe.wait_ge(sm["mst_ready"], l)
                        pe.wait_ge(sm["t_ready"], 2 * (l - 1) + t + 1)
                        lhs, rhs = mst, tm
                    else:
                        pe.wait_ge(sm["p1_ready"], 2 * (l - 1) + t + 1)
                        pe.wait_ge(sm["u_ready"], 1 + 2 * (l - 1))
                        lhs, rhs = (um, p1) if job[1] == "t" else (p1, um)
                    b = open_bank(job)
                    for hh in range(AH):
                        ins = mm(b[:, hh * P:(hh + 1) * P], lhsT=lhs[:, 4 * t + hh, :], rhs=rhs[:, 4 * t + hh, :], start=True, stop=True)
                    close(job, ins)
                elif job == "bmean":
                    pe.wait_ge(sm["conv_out"], 4)
                    b = open_bank(job)
                    for c in range(NB):
                        ins = mm(b[:, 0:S], lhsT=inv512[:, :], rhs=bacc[:, c, :], start=c == 0, stop=c == NB - 1)
                    close(job, ins)
                elif job == "bvar":
                    pe.wait_ge(sm["bsq"], 1)
                    b = open_bank(job)
                    for c in range(NB):
                        ins = mm(b[:, 0:S], lhsT=inv512[:, :], rhs=bv[:, c, 0:S], start=c == 0, stop=c == NB - 1)
                    close(job, ins)
                elif job[:2] == "wT":
                    t = int(job[2])
                    pe.wait_ge(sm["u_ready"], 1 + 2 * (LEVELS - 1))
                    pe.wait_ge(sm["kb_ready"], 2)
                    b = open_bank(job)
                    for hh in range(AH):
                        ins = mm(b[:, hh * P:(hh + 1) * P], lhsT=kbt[:, 4 * t + hh, :], rhs=um[:, 4 * t + hh, :], start=True, stop=True)
                    close(job, ins)
                elif job[:2] == "vn":
                    n = int(job[2])
                    t, r = n // 2, 64 * (n % 2)
                    pe.wait_ge(sm["wT_ready"], t + 1)
                    pe.wait_ge(sm["vb_ready"], 2)
                    if n:
                        pe.wait_ge(sm["st_ready"], n)
                    b = open_bank(job)
                    for hh in range(AH):
                        o = b[r:r + 64, hh * P:(hh + 1) * P]
                        ins = mm(o, lhsT=um[r:r + 64, 4 * t + hh, r:r + 64], rhs=vbt[r:r + 64, 4 * t + hh, :], start=True, stop=n == 0)
                        if n:
                            ins = mm(o, lhsT=wT[:, 4 * t + hh, r:r + 64], rhs=st[:, hh, :], start=False, stop=True)
                    close(job, ins)
                elif job[:2] == "oT":
                    n = int(job[2])
                    t, r = n // 2, 64 * (n % 2)
                    pe.wait_ge(sm["vn_ready"], n + 1)
                    pe.wait_ge(sm["qk_ready"], 2)
                    pe.wait_ge(sm["qd_ready"], 2)
                    b = open_bank(job)
                    for hh in range(AH):
                        o = b[:, hh * CH:(hh + 1) * CH]
                        ins = mm(o, lhsT=vn[r:r + 64, hh, :], rhs=dt_[r:r + 64, 4 * t + hh, r:r + 64], start=True, stop=n == 0)
                        if n:
                            ins = mm(o, lhsT=st[:, hh, :], rhs=qT[:, hh, n * CH:(n + 1) * CH], start=False, stop=True)
                    close(job, ins)
                elif job[:2] == "dS":
                    n = int(job[2])
                    t, r = n // 2, 64 * (n % 2)
                    b = open_bank(job)
                    for hh in range(AH):
                        ins = mm(b[:, hh * P:(hh + 1) * P], lhsT=kdt[r:r + 64, 4 * t + hh, :], rhs=vn[r:r + 64, hh, :], start=True, stop=True)
                    close(job, ins)
                elif job[:2] == "sc":
                    n = int(job[2])
                    pe.wait_ge(sm["cq_ready"], 1)
                    pe.wait_ge(sm["cv_ready"], 1)
                    g, j0, nh, q0 = (n, 0, 4, 0) if n < 2 else ((n - 2) // 2, 2 * (n % 2), 2, P)
                    keys = P if n < 2 else 2 * P
                    b = open_bank(job)
                    for k in range(nh):
                        ins = mm(b[:, k * keys:(k + 1) * keys], lhsT=cq[64 * g:64 * g + 64, j0 + k, q0:q0 + P],
                                 rhs=ck[64 * g:64 * g + 64, 0:keys], start=True, stop=True)
                    close(job, ins)
                elif job[:2] == "pt":
                    n = int(job[2])
                    pe.wait_ge(sm["pnorm"], n + 1)
                    b = open_bank(job)
                    for k in range(4):
                        ins = tr(b[:, k * P:(k + 1) * P], ssc[:, n % 2, k * P:(k + 1) * P])
                    close(job, ins)
                elif job[:2] == "pv":
                    n = int(job[2])
                    g, j0, nh, q0 = (n, 0, 4, 0) if n < 2 else ((n - 2) // 2, 2 * (n % 2), 2, P)
                    pe.wait_ge(sm["pt_ready"], n + 1)
                    b = open_bank(job)
                    nk = 1 if n < 2 else 2
                    for k in range(nh):
                        for kb in range(nk):
                            ins = mm(b[64 * g:64 * g + 64, k * P:(k + 1) * P], lhsT=cv[:, kb, 64 * g:64 * g + 64],
                                     rhs=pts[:, n % 2, (k * nk + kb) * P:(k * nk + kb + 1) * P], start=kb == 0, stop=kb == nk - 1)
                    close(job, ins)
                elif job[:3] == "rms":
                    hh = int(job[3])
                    pe.wait_ge(sm["osq"], 1)
                    b = open_bank(job)
                    close(job, mm(b[:, :], lhsT=inv128[:, :], rhs=sq[:, 2 * hh:2 * hh + 2, :], start=True, stop=True))
                elif job[0] == "y":
                    q = int(job[2])
                    src, ready, cnt_ = {"B": (bacc, "bsilu", 1), "C": (ocT, "oc_ready", 6), "A": (oaT.rearrange("p a b -> p (a b)").rearrange("p (n c) -> p n c", n=4), "oa_ready", 1)}[job[1]]
                    pe.wait_ge(sm[ready], cnt_)
                    w = tile("W" + job[1]).rearrange("p (k c) -> p k c", k=4)
                    b = open_bank(job)
                    for n in range(2):
                        c = (2 * q + n) * P
                        for k in range(4):
                            ins = mm(b[:, n * S:(n + 1) * S], lhsT=w[:, k, c:c + P], rhs=src[:, k, :], start=k == 0, stop=k == 3)
                    close(job, ins)
                elif job[:3] == "mix":
                    t, hf = int(job[3]), int(job[4])
                    pe.wait_ge(sm["mx_ready"], 4)
                    w = tile(f"WO{hf}").rearrange("p (k c) -> p k c", k=DC)
                    b = open_bank(job)
                    for k in range(DC):
                        ins = mm(b[:, :], lhsT=mxT[:, k, t * P:(t + 1) * P], rhs=w[:, k, :], start=k == 0, stop=k == DC - 1)
                    close(job, ins)
                elif job[:6] == "router":
                    t = int(job[6])
                    keep_warm(open_bank(job), 2)
                    pe.wait_ge(sm["h1T_ready"], 2 * t + 2)
                    pe.wait_ge(wr_in, 64)
                    b = open_bank(job)
                    for k in range(DC):
                        ins = mm(b[:, 0:NE], lhsT=hT[:, k, t * P:(t + 1) * P], rhs=wr[:, k, :], start=k == 0, stop=k == DC - 1)
                    close(job, ins)
                elif job == "rank":
                    keep_warm(open_bank(job), 5)
                    pe.wait_ge(sm["mask_ready"], 2)
                    b = open_bank(job)
                    tri = consts[:, C_TRI128:C_TRI128 + P]
                    mm(b[:, 0:NE], lhsT=tri, rhs=mask[:, 0, :], start=True, stop=True)
                    mm(b[:, NE:2 * NE], lhsT=ones, rhs=mask[:, 0, :], start=True, stop=False)
                    close(job, mm(b[:, NE:2 * NE], lhsT=tri, rhs=mask[:, 1, :], start=False, stop=True))
                elif job == "count":
                    b = open_bank(job)
                    mm(b[:, 0:NE], lhsT=ones, rhs=mask[:, 0, :], start=True, stop=False)
                    close(job, mm(b[:, 0:NE], lhsT=ones, rhs=mask[:, 1, :], start=False, stop=True))
                elif job == "combT":
                    keep_warm(open_bank(job), 1)
                    pe.wait_ge(sm["comb_ready"], 1)
                    b = open_bank(job)
                    for t in range(ST):
                        ins = tr(b[0:NE, t * P:(t + 1) * P], comb[:, t, :])
                    close(job, ins)
                else:
                    raise ValueError(job)
            pe.wait_ge(drained[6], FILL["router0"])
            keep_warm(kc, 3)
            pe.wait_ge(sm["combT_ready"], 1)
            for b in range(8):
                last = [n for n in JOBS if BANK[n] == b][-1]
                pe.wait_ge(drained[b], FILL[last])
            for t in range(ST):
                for k in range(2):
                    ins = mm(acc[t][k][:, :], lhsT=combTs[:, t, :], rhs=b2s[:, 512 * k:512 * k + 512], start=True, stop=False, skip_group_check=True)
            keep_warm(kc, 3)
            pe.wait_ge(sm["table_ready"], 1)

            pe.wait_ge(sm["b1_split"], 1)

            def scatter(last=False):
                for t in range(ST):
                    for k in range(2):
                        ins = mm(acc[t][k][:, :], lhsT=ptw[:, t, :], rhs=ys[:, 512 * k:512 * k + 512], start=False, stop=last, skip_group_check=True)
                    if last:
                        ins.then_inc(sm["all_scattered"], 1)

            def turn_weights(g, bank_):
                for t in range(ST):
                    ins = tr(bank_[:, t * P:(t + 1) * P], pw[:, t, :])
                ins.then_inc(sm["pt_filled"], 1)

            def window(i, par, g, width):
                narrow = width == NARROW
                pe.wait_ge(sm["p_ready"], g + 1)
                for b, wk in enumerate((kc, kd)):
                    if b == 1:
                        pe.wait_ge(sm["ys_ready"], g * 2 + 2)
                    for k in range(4):
                        for t in range(ST):
                            ins = mm(wk[:, k * width:(k + 1) * width], lhsT=h[:, t, (4 * b + k) * P:(4 * b + k + 1) * P], rhs=pg[:, t, 0:width],
                                     start=t == 0, stop=t == ST - 1)
                    ins.then_inc(sm["gathered"], 1)
                if narrow:
                    hidden = [(ka[0:64, :], 0), (ka[64:128, :], 512), (kc[0:64, :], F), (kc[64:128, :], F + 512)]
                else:
                    hidden = [(ka, 0), (kb_, 512), (kc, F), (kd, F + 512)]
                pe.wait_ge(sm["ptw_ready"], g + 1)
                for n, (o, c) in enumerate(hidden):
                    if n == 2:
                        pe.wait_ge(sm["xt_ready"], g * 2 + 2)
                    row, biases = pick[:, 0:width], b1p[:, c:c + 512]
                    if narrow:
                        row, biases = row.bitcast(f32), biases.bitcast(f32)
                    mm(o, lhsT=row, rhs=biases, start=True, stop=False, skip_group_check=True)
                for j in range(W1C):
                    s = (NT + j) % W1C
                    pe.wait_ge(tile_in[s], i * 32 + (16 * tile_total[s] + 16 * (par + 1)))
                    for k in range(2):
                        for o, c in hidden:
                            ins = mm(o, lhsT=xT[:, 2 * j + k, 0:width], rhs=w1s[:, s, 2048 * k + c:2048 * k + c + 512], start=False,
                                     stop=j == W1C - 1 and k == 1, skip_group_check=True)
                    ins.then_inc(sm["w1_used"], 1)
                scatter()
                if narrow:
                    turn_weights(g, kd)
                for k in range(2):
                    pe.wait_ge(sm["act_ready"], g * 2 + (k + 1))
                    bank_ = (kb_, ka)[k] if narrow else (ka, kc)[k]
                    nj = 2 if narrow else 4
                    for j in range(nj):
                        ins = tr(bank_[:, j * P:(j + 1) * P], act_tok[:, (nj * k + j) * P:(nj * k + j + 1) * P])
                    ins.then_inc(sm["turned"], 1)
                if narrow:
                    pe.wait_ge(sm["ptw_ready"], g + 2)
                    outs = [(kd[0:64, :], 0), (kd[64:128, :], 512)]
                    order = (0, 1, 4, 5, 2, 3, 6, 7)
                else:
                    outs = [(kb_, 0), (kd, 512)]
                    order = range(8)
                for n, f in enumerate(order):
                    if n == 0:
                        pe.wait_ge(w2_in[par][0], i * 16 + 16)
                    if n == (2 if narrow else 4):
                        pe.wait_ge(w2_in[par][1], i * 16 + 16)
                    if n % 4 == 0:
                        pe.wait_ge(sm["actT_ready"], g * 2 + (n // 4 + 1))
                    if n == 4 and not narrow:
                        turn_weights(g, ka)
                    w = (w2s, w2x)[par][:, f // 4, :]
                    for o, c in outs:
                        ins = mm(o, lhsT=actT[:, f, 0:width], rhs=w[:, 1024 * (f % 4) + c:1024 * (f % 4) + c + 512], start=n == 0, stop=n == 7,
                                 skip_group_check=True)
                ins.then_inc(sm["y_filled"], 1)

            with pe.Fori(0, NE // 2) as i:
                for par in range(2):
                    g0 = pe.value_load(tab_i[0:1, bass.ds(i * 2 + par, 1)], min_val=0, max_val=2 * NE)
                    cnt = pe.value_load(tab_i[0:1, bass.ds(i * 2 + (par + NE), 1)], min_val=0, max_val=S)
                    with pe.If(cnt > WIDE):
                        window(i, par, g0, WIDE)
                        window(i, par, g0 + 1, WIDE)
                    with pe.Else():
                        with pe.If(cnt > NARROW):
                            window(i, par, g0, WIDE)
                        with pe.Else():
                            window(i, par, g0, NARROW)
            windows = pe.value_load(tab_i[0:1, 3 * NE:3 * NE + 1], min_val=NE, max_val=2 * NE)
            pe.wait_ge(sm["ys_ready"], windows * 2 + 2)
            pe.wait_ge(sm["ptw_ready"], windows + 1)
            scatter(last=True)



def kernel(**inputs):
    import numpy as _np
    import concourse.bacc as _bacc
    from concourse import mybir as _mybir
    from concourse.bass_utils import run_bass_kernel_spmd as _run

    a = {k: _np.asarray(v) for k, v in inputs.items()}
    chan = _np.concatenate([
        a["a_conv_w"][0].reshape(KA, 12, P).transpose(2, 1, 0).reshape(P, 12 * KA),
        a["b_dw_w"][0].reshape(KB, NB, P).transpose(2, 1, 0).reshape(P, NB * KB),
        a["b_dw_b"][0].reshape(NB, P).T, a["b_ln_g"][0].reshape(NB, P).T, a["b_ln_b"][0].reshape(NB, P).T,
        a["a_norm_g"][0].reshape(P, 1)], axis=1)
    arrays = {
        "x": a["x"][0],
        "lnp": _np.stack([a["ln_in_g"], a["ln_in_b"], a["ln1_g"][0], a["ln1_b"][0], a["ln2_g"][0], a["ln2_b"][0]]),
        "rel": a["rel_bias"], "w_in": a["w_in"][0], "wa": a["w_a_out"][0], "wb": a["w_b_out"][0], "wc": a["w_c_out"][0],
        "wo": a["w_out"][0], "chan": chan,
        "rows": _np.concatenate([a["a_log"][0], a["a_dt_bias"][0], a["c_sinks"][0], a["b_router"][0]])[None],
        "w_router": a["w_router"][0], "w1": a["w1"][0], "b1": a["b1"][0], "w2": a["w2"][0], "b2": a["b2"][0], "cst": constants(),
    }
    arrays = {k + "_dram": _np.ascontiguousarray(v) for k, v in arrays.items()}
    nc = _bacc.Bacc("TRN2", target_bir_lowering=False, num_devices=1)
    args = [nc.dram_tensor(k, v.shape, _mybir.dt.from_np(v.dtype), kind="ExternalInput").ap() for k, v in arrays.items()]
    args.append(nc.dram_tensor("out_dram", (S, D), _mybir.dt.float32, kind="ExternalOutput").ap())
    build(nc, *args)
    r = _run(nc, [arrays], core_ids=[0])
    return r.results[0]["out_dram"].reshape(1, S, D)
```
